# Optimizing a Trainium2 kernel written in Bass

```python
import math
import jax
import jax.numpy as jnp
from jax import lax
import numpy as np

D_MODEL = 1024
BATCH = 1
SEQ = 1024
DEPTH = 2

GRID_W = 64
CTX_LEN = 256
HEAD_DIM = 64
GROUP_HEADS = 4
GROUP_WIDTH = GROUP_HEADS * HEAD_DIM
N_MIXERS = 4
MIX_WIDTH = N_MIXERS * GROUP_WIDTH
KV_HEADS = 2
KV_GROUPS = GROUP_HEADS // KV_HEADS
KV_WIDTH = KV_HEADS * HEAD_DIM
GDN_CONV = 3
GDN_CHUNK = 64
HGRN_CHUNK = 16
Q_BLOCK = 128
WINDOW = 128
ROPE_THETA = 10000.0
D_FF = 2816
FFN_CONV = 3
N_MOD = 6
EPS = 1e-6
NEG = -1e30
F32 = jnp.float32

IN_SIZES = (
    3 * GROUP_WIDTH,
    GROUP_WIDTH,
    2 * GROUP_HEADS,
    2 * GROUP_HEADS,
    GROUP_WIDTH,
    2 * KV_WIDTH,
    GROUP_WIDTH,
    2 * KV_WIDTH,
    GROUP_WIDTH,
    2 * GROUP_WIDTH,
    GROUP_WIDTH,
    GROUP_WIDTH,
)
IN_WIDTH = sum(IN_SIZES)

kernel_name = 'hybrid_parallel_heads_dit_block'

def rms_norm(x, gain):
    xf = x.astype(F32)
    y = xf * lax.rsqrt(jnp.mean(xf * xf, axis=-1, keepdims=True) + EPS)
    return (y * gain.astype(F32)).astype(x.dtype)

def l2_normalize(x):
    xf = x.astype(F32)
    return xf * lax.rsqrt(jnp.sum(xf * xf, axis=-1, keepdims=True) + EPS)

def split_heads(x, n_heads):
    b, length, _ = x.shape
    return x.reshape(b, length, n_heads, -1).transpose(0, 2, 1, 3)

def merge_heads(x):
    b, n, length, d = x.shape
    return x.transpose(0, 2, 1, 3).reshape(b, length, n * d)

def modulate(x, shift, scale):
    return x * (1.0 + scale) + shift

def split_columns(p):
    offsets = np.cumsum(IN_SIZES)[:-1].tolist()
    return jnp.split(p, offsets, axis=-1)

def dwconv_centered(x, w, b=None):
    k_width = w.shape[0]
    pad = k_width // 2
    length = x.shape[1]
    xp = jnp.pad(x, ((0, 0), (pad, pad), (0, 0)))
    y = xp[:, 0:length] * w[0]
    for j in range(1, k_width):
        y = y + xp[:, j:j + length] * w[j]
    return y if b is None else y + b

def axial_rope_tables(rows):
    row = jnp.repeat(jnp.arange(rows), GRID_W).astype(F32)
    col = jnp.tile(jnp.arange(GRID_W), rows).astype(F32)
    n_freq = HEAD_DIM // 4
    inv_freq = 1.0 / (ROPE_THETA ** (jnp.arange(n_freq, dtype=F32) / n_freq))
    ang = jnp.concatenate([row[:, None] * inv_freq, col[:, None] * inv_freq], axis=-1)
    return jnp.cos(ang), jnp.sin(ang)

def apply_rope(x, cos, sin):
    xf = x.astype(F32).reshape(x.shape[:-1] + (HEAD_DIM // 2, 2))
    x0, x1 = xf[..., 0], xf[..., 1]
    out = jnp.stack([x0 * cos - x1 * sin, x0 * sin + x1 * cos], axis=-1)
    return out.reshape(x.shape).astype(x.dtype)

def bidirectional_scan(scan_fn, ctx_fwd, ctx_bwd, lat_fwd, lat_bwd, s0):
    rev = lambda args: tuple(jnp.flip(a, axis=2) for a in args)
    o_cf, s_cf = scan_fn(*ctx_fwd, s0)
    o_lf, _ = scan_fn(*lat_fwd, s_cf)
    o_cb, s_cb = scan_fn(*rev(ctx_bwd), s0)
    o_lb, _ = scan_fn(*rev(lat_bwd), s_cb)
    return o_cf + jnp.flip(o_cb, axis=2), o_lf + jnp.flip(o_lb, axis=2)

def gdn_chunked(q, k, v, g, beta, s0):
    b, h, length, dk = q.shape
    dv = v.shape[-1]
    cs = GDN_CHUNK
    n = length // cs
    q = q.reshape(b, h, n, cs, dk)
    k = k.reshape(b, h, n, cs, dk)
    v = v.reshape(b, h, n, cs, dv)
    beta = beta.reshape(b, h, n, cs)
    gc = jnp.cumsum(g.reshape(b, h, n, cs), axis=-1)
    incl = jnp.tril(jnp.ones((cs, cs), bool))
    strict = jnp.tril(jnp.ones((cs, cs), bool), -1)
    decay = jnp.exp(jnp.where(incl, gc[..., :, None] - gc[..., None, :], NEG))
    kb = k * beta[..., None]
    m = jnp.where(strict, jnp.einsum('bhnid,bhnjd->bhnij', kb, k) * decay, 0.0)
    a = m + jnp.eye(cs, dtype=F32)
    rhs = jnp.concatenate([v * beta[..., None], kb * jnp.exp(gc)[..., None]], axis=-1)
    sol = lax.linalg.triangular_solve(a, rhs, left_side=True, lower=True, unit_diagonal=True)
    u, w = sol[..., :dv], sol[..., dv:]
    attn = jnp.einsum('bhnid,bhnjd->bhnij', q, k) * decay
    q_dec = q * jnp.exp(gc)[..., None]
    k_dec = k * jnp.exp(gc[..., -1:] - gc)[..., None]
    g_last = jnp.exp(gc[..., -1])

    def step(state, xs):
        u_i, w_i, qd_i, kd_i, at_i, gl_i = xs
        v_new = u_i - jnp.einsum('bhcd,bhde->bhce', w_i, state)
        o_i = jnp.einsum('bhcd,bhde->bhce', qd_i, state) + jnp.einsum('bhij,bhje->bhie', at_i, v_new)
        state = state * gl_i[..., None, None] + jnp.einsum('bhcd,bhce->bhde', kd_i, v_new)
        return state, o_i

    xs = tuple(jnp.moveaxis(t, 2, 0) for t in (u, w, q_dec, k_dec, attn, g_last))
    s_fin, o = lax.scan(step, s0, xs)
    return jnp.moveaxis(o, 0, 2).reshape(b, h, length, dv), s_fin

def hgrn_chunked(q, k, v, log_f, s0):
    b, h, length, dk = q.shape
    dv = v.shape[-1]
    cs = HGRN_CHUNK
    n = length // cs
    q = q.reshape(b, h, n, cs, dk)
    k = k.reshape(b, h, n, cs, dk)
    v = v.reshape(b, h, n, cs, dv)
    bc = jnp.cumsum(log_f.reshape(b, h, n, cs, dk), axis=3)
    incl = jnp.tril(jnp.ones((cs, cs), bool))[:, :, None]
    rel = bc[:, :, :, :, None, :] - bc[:, :, :, None, :, :]
    decay = jnp.exp(jnp.where(incl, rel, NEG))
    attn = jnp.einsum('bhnid,bhnjd,bhnijd->bhnij', q, k, decay)
    q_dec = q * jnp.exp(bc)
    k_dec = k * jnp.exp(bc[:, :, :, -1:] - bc)
    f_last = jnp.exp(bc[:, :, :, -1])

    def step(state, xs):
        qd_i, kd_i, v_i, at_i, fl_i = xs
        o_i = jnp.einsum('bhcd,bhde->bhce', qd_i, state) + jnp.einsum('bhij,bhje->bhie', at_i, v_i)
        state = state * fl_i[..., None] + jnp.einsum('bhcd,bhce->bhde', kd_i, v_i)
        return state, o_i

    xs = tuple(jnp.moveaxis(t, 2, 0) for t in (q_dec, k_dec, v, attn, f_last))
    s_fin, o = lax.scan(step, s0, xs)
    return jnp.moveaxis(o, 0, 2).reshape(b, h, length, dv), s_fin

def gdn_mixer(qkv_c, z_c, beta_c, a_c, qkv_l, z_l, beta_l, a_l, conv_w, a_log, dt_bias, o_gain):
    def prep(qkv, beta_raw, a_raw):
        b, length, _ = qkv.shape
        qkv = jax.nn.silu(dwconv_centered(qkv, conv_w))
        q, k, v = jnp.split(qkv, 3, axis=-1)
        q = l2_normalize(split_heads(q, GROUP_HEADS)) * HEAD_DIM ** -0.5
        k = l2_normalize(split_heads(k, GROUP_HEADS))
        v = split_heads(v, GROUP_HEADS).astype(F32)
        beta = jax.nn.sigmoid(beta_raw.astype(F32)).reshape(b, length, 2, GROUP_HEADS).transpose(2, 0, 3, 1)
        a = a_raw.astype(F32).reshape(b, length, 2, GROUP_HEADS) + dt_bias.astype(F32)
        g = (-jnp.exp(a_log.astype(F32)) * jax.nn.softplus(a)).transpose(2, 0, 3, 1)
        return q, k, v, g, beta

    qc, kc, vc, gc, bc = prep(qkv_c, beta_c, a_c)
    ql, kl, vl, gl, bl = prep(qkv_l, beta_l, a_l)
    s0 = jnp.zeros((qkv_l.shape[0], GROUP_HEADS, HEAD_DIM, HEAD_DIM), F32)
    o_c, o_l = bidirectional_scan(gdn_chunked,
                                  (qc, kc, vc, gc[0], bc[0]), (qc, kc, vc, gc[1], bc[1]),
                                  (ql, kl, vl, gl[0], bl[0]), (ql, kl, vl, gl[1], bl[1]), s0)

    def out(o, z):
        gate = jax.nn.silu(split_heads(z, GROUP_HEADS).astype(F32))
        return merge_heads(rms_norm(o, o_gain) * gate).astype(z.dtype)

    return out(o_c, z_c), out(o_l, z_l)

def softmax_attend(q, k, v):
    s = jnp.einsum('bkgqd,bksd->bkgqs', q, k).astype(F32) * HEAD_DIM ** -0.5
    p = jax.nn.softmax(s, axis=-1).astype(v.dtype)
    return jnp.einsum('bkgqs,bksd->bkgqd', p, v)

def global_gqa(q_c, kv_c, q_l, kv_l, q_gain, k_gain, cos, sin, with_ctx):
    b, length, _ = q_l.shape
    k_c, v_c = jnp.split(kv_c, 2, axis=-1)
    k_l, v_l = jnp.split(kv_l, 2, axis=-1)
    k_c = rms_norm(split_heads(k_c, KV_HEADS), k_gain)
    v_c = split_heads(v_c, KV_HEADS)
    k_l = apply_rope(rms_norm(split_heads(k_l, KV_HEADS), k_gain), cos, sin)
    v_l = split_heads(v_l, KV_HEADS)
    q_l = apply_rope(rms_norm(split_heads(q_l, GROUP_HEADS), q_gain), cos, sin)
    keys = jnp.concatenate([k_c, k_l], axis=2)
    vals = jnp.concatenate([v_c, v_l], axis=2)
    nb = length // Q_BLOCK
    qb = jnp.moveaxis(q_l.reshape(b, KV_HEADS, KV_GROUPS, nb, Q_BLOCK, HEAD_DIM), 3, 0)
    o_l = lax.map(lambda q_blk: softmax_attend(q_blk, keys, vals), qb)
    o_l = merge_heads(jnp.moveaxis(o_l, 0, 3).reshape(b, GROUP_HEADS, length, HEAD_DIM))
    if not with_ctx:
        return None, o_l
    qc = rms_norm(split_heads(q_c, GROUP_HEADS), q_gain).reshape(b, KV_HEADS, KV_GROUPS, -1, HEAD_DIM)
    o_c = softmax_attend(qc, k_c, v_c).reshape(b, GROUP_HEADS, -1, HEAD_DIM)
    return merge_heads(o_c), o_l

def window_gqa(q_c, kv_c, q_l, kv_l, sink, cos, sin, with_ctx):
    b, length, _ = q_l.shape
    nb = length // Q_BLOCK
    scale = HEAD_DIM ** -0.5
    k_c, v_c = jnp.split(kv_c, 2, axis=-1)
    k_l, v_l = jnp.split(kv_l, 2, axis=-1)
    k_c = split_heads(k_c, KV_HEADS)
    v_c = split_heads(v_c, KV_HEADS)
    k_l = apply_rope(split_heads(k_l, KV_HEADS), cos, sin)
    v_l = split_heads(v_l, KV_HEADS)
    q_l = apply_rope(split_heads(q_l, GROUP_HEADS), cos, sin)

    def band(t):
        tp = jnp.pad(t, ((0, 0), (0, 0), (Q_BLOCK, Q_BLOCK), (0, 0))).reshape(b, KV_HEADS, nb + 2, Q_BLOCK, HEAD_DIM)
        return jnp.concatenate([tp[:, :, :-2], tp[:, :, 1:-1], tp[:, :, 2:]], axis=3)

    k_band, v_band = band(k_l), band(v_l)
    qb = q_l.reshape(b, KV_HEADS, KV_GROUPS, nb, Q_BLOCK, HEAD_DIM)
    s_band = jnp.einsum('bkgnqd,bknsd->bkgnqs', qb, k_band).astype(F32) * scale
    blk = jnp.arange(nb)[:, None, None]
    q_pos = blk * Q_BLOCK + jnp.arange(Q_BLOCK)[None, :, None]
    k_pos = (blk - 1) * Q_BLOCK + jnp.arange(3 * Q_BLOCK)[None, None, :]
    valid = (jnp.abs(q_pos - k_pos) <= WINDOW) & (k_pos >= 0) & (k_pos < length)
    s_band = jnp.where(valid, s_band, NEG)
    s_ctx = jnp.einsum('bkgnqd,bksd->bkgnqs', qb, k_c).astype(F32) * scale
    sink_col = jnp.broadcast_to(sink.astype(F32).reshape(1, KV_HEADS, KV_GROUPS, 1, 1, 1), s_band.shape[:-1] + (1,))
    p = jax.nn.softmax(jnp.concatenate([s_band, s_ctx, sink_col], axis=-1), axis=-1).astype(v_l.dtype)
    n_band = 3 * Q_BLOCK
    n_ctx = k_c.shape[2]
    o_l = (jnp.einsum('bkgnqs,bknsd->bkgnqd', p[..., :n_band], v_band)
           + jnp.einsum('bkgnqs,bksd->bkgnqd', p[..., n_band:n_band + n_ctx], v_c))
    o_l = merge_heads(o_l.reshape(b, GROUP_HEADS, length, HEAD_DIM))
    if not with_ctx:
        return None, o_l
    qc = split_heads(q_c, GROUP_HEADS).reshape(b, KV_HEADS, KV_GROUPS, -1, HEAD_DIM)
    s_c = jnp.einsum('bkgqd,bksd->bkgqs', qc, k_c).astype(F32) * scale
    sink_c = jnp.broadcast_to(sink.astype(F32).reshape(1, KV_HEADS, KV_GROUPS, 1, 1), s_c.shape[:-1] + (1,))
    p_c = jax.nn.softmax(jnp.concatenate([s_c, sink_c], axis=-1), axis=-1)[..., :-1].astype(v_c.dtype)
    o_c = jnp.einsum('bkgqs,bksd->bkgqd', p_c, v_c).reshape(b, GROUP_HEADS, -1, HEAD_DIM)
    return merge_heads(o_c), o_l

def hgrn_mixer(q_c, f_c, i_c, g_c, q_l, f_l, i_l, g_l, lower_bound, o_gain):
    def prep(q, f, i):
        b, length, _ = q.shape
        q = split_heads(jax.nn.silu(q), GROUP_HEADS).astype(F32)
        v = split_heads(i, GROUP_HEADS).astype(F32)
        z = f.astype(F32).reshape(b, length, 2, GROUP_WIDTH)
        f_gate = lower_bound + (1.0 - lower_bound) * jax.nn.sigmoid(z)
        log_f = jnp.log(f_gate)
        log_f = log_f.reshape(b, length, 2, GROUP_HEADS, HEAD_DIM).transpose(2, 0, 3, 1, 4)
        k = -jnp.expm1(log_f)
        return q, v, k, log_f

    qc, vc, kc, lfc = prep(q_c, f_c, i_c)
    ql, vl, kl, lfl = prep(q_l, f_l, i_l)
    s0 = jnp.zeros((q_l.shape[0], GROUP_HEADS, HEAD_DIM, HEAD_DIM), F32)
    o_c, o_l = bidirectional_scan(hgrn_chunked,
                                  (qc, kc[0], vc, lfc[0]), (qc, kc[1], vc, lfc[1]),
                                  (ql, kl[0], vl, lfl[0]), (ql, kl[1], vl, lfl[1]), s0)

    def out(o, g):
        gate = jax.nn.silu(split_heads(g, GROUP_HEADS).astype(F32))
        return merge_heads(rms_norm(o, o_gain) * gate).astype(g.dtype)

    return out(o_c, g_c), out(o_l, g_l)

def token_mixing(h_c, h_l, w_in, w_out, gdn_conv_w, gdn_a_log, gdn_dt_bias, gdn_norm,
                 attn_q_norm, attn_k_norm, swa_sink, hgrn_lb, hgrn_norm, cos, sin, with_ctx):
    pc = split_columns(h_c @ w_in)
    pl = split_columns(h_l @ w_in)
    a_c, a_l = gdn_mixer(*pc[0:4], *pl[0:4], gdn_conv_w, gdn_a_log, gdn_dt_bias, gdn_norm)
    b_c, b_l = global_gqa(pc[4], pc[5], pl[4], pl[5], attn_q_norm, attn_k_norm, cos, sin, with_ctx)
    c_c, c_l = window_gqa(pc[6], pc[7], pl[6], pl[7], swa_sink, cos, sin, with_ctx)
    d_c, d_l = hgrn_mixer(*pc[8:12], *pl[8:12], hgrn_lb, hgrn_norm)
    o_l = jnp.concatenate([a_l, b_l, c_l, d_l], axis=-1) @ w_out
    if not with_ctx:
        return None, o_l
    o_c = jnp.concatenate([a_c, b_c, c_c, d_c], axis=-1) @ w_out
    return o_c, o_l

def conv_ffn(h, w_up, conv_w, conv_b, w_down):
    u = dwconv_centered(h @ w_up, conv_w, conv_b)
    gate, val = jnp.split(u, 2, axis=-1)
    return (jax.nn.silu(gate) * val) @ w_down

def setup_inputs(seed: int = 0) -> dict:
    key = jax.random.key(seed)
    ks = jax.random.split(key, 25)

    def normal(k, shape, scale):
        return jax.random.normal(k, shape, F32) * scale

    def gain(k, shape):
        return 1.0 + 0.05 * jax.random.normal(k, shape, F32)

    dt = jnp.exp(jax.random.uniform(ks[14], (DEPTH, 2, GROUP_HEADS), F32, math.log(1e-3), math.log(1e-1)))
    return {
        'x': normal(ks[0], (BATCH, SEQ, D_MODEL), 1.0),
        'c': normal(ks[1], (BATCH, D_MODEL), 1.0),
        'ctx': normal(ks[2], (BATCH, CTX_LEN, D_MODEL), 1.0),
        'c_ctx': normal(ks[3], (D_MODEL,), 1.0),
        'ada_w': normal(ks[4], (DEPTH, D_MODEL, N_MOD * D_MODEL), D_MODEL ** -0.5),
        'ada_b': normal(ks[5], (DEPTH, N_MOD * D_MODEL), 0.02),
        'norm_pre_mix': gain(ks[6], (DEPTH, D_MODEL)),
        'norm_post_mix': gain(ks[7], (DEPTH, D_MODEL)),
        'norm_pre_ffn': gain(ks[8], (DEPTH, D_MODEL)),
        'norm_post_ffn': gain(ks[9], (DEPTH, D_MODEL)),
        'w_in': normal(ks[10], (DEPTH, D_MODEL, IN_WIDTH), D_MODEL ** -0.5),
        'w_out': normal(ks[11], (DEPTH, MIX_WIDTH, D_MODEL), MIX_WIDTH ** -0.5),
        'gdn_conv_w': normal(ks[12], (DEPTH, GDN_CONV, 3 * GROUP_WIDTH), GDN_CONV ** -0.5),
        'gdn_a_log': jnp.log(jax.random.uniform(ks[13], (DEPTH, 2, GROUP_HEADS), F32, 1.0, 16.0)),
        'gdn_dt_bias': dt + jnp.log(-jnp.expm1(-dt)),
        'gdn_norm': gain(ks[15], (DEPTH, HEAD_DIM)),
        'attn_q_norm': gain(ks[16], (DEPTH, HEAD_DIM)),
        'attn_k_norm': gain(ks[17], (DEPTH, HEAD_DIM)),
        'swa_sink': normal(ks[18], (DEPTH, GROUP_HEADS), 0.5),
        'hgrn_lb_raw': normal(ks[19], (DEPTH, 2, GROUP_WIDTH), 0.5),
        'hgrn_norm': gain(ks[20], (DEPTH, HEAD_DIM)),
        'ffn_w_up': normal(ks[21], (DEPTH, D_MODEL, 2 * D_FF), D_MODEL ** -0.5),
        'ffn_conv_w': normal(ks[22], (DEPTH, FFN_CONV, 2 * D_FF), FFN_CONV ** -0.5),
        'ffn_conv_b': normal(ks[23], (DEPTH, 2 * D_FF), 0.02),
        'ffn_w_down': normal(ks[24], (DEPTH, D_FF, D_MODEL), D_FF ** -0.5),
    }

def reference(x, c, ctx, c_ctx, ada_w, ada_b, norm_pre_mix, norm_post_mix, norm_pre_ffn, norm_post_ffn,
              w_in, w_out, gdn_conv_w, gdn_a_log, gdn_dt_bias, gdn_norm, attn_q_norm, attn_k_norm,
              swa_sink, hgrn_lb_raw, hgrn_norm, ffn_w_up, ffn_conv_w, ffn_conv_b, ffn_w_down):
    rows = x.shape[1] // GRID_W
    cos, sin = axial_rope_tables(rows)
    lb_p = jax.nn.softmax(hgrn_lb_raw.astype(F32), axis=0)
    hgrn_lb = jnp.cumsum(lb_p, axis=0) - lb_p[0]
    c_act = jax.nn.silu(c)
    c_ctx_act = jax.nn.silu(c_ctx)
    x_l, x_c = x, ctx
    for layer in range(DEPTH):
        with_ctx = layer < DEPTH - 1
        mod_l = jnp.split((c_act @ ada_w[layer] + ada_b[layer])[:, None, :], N_MOD, axis=-1)
        mod_c = jnp.split(c_ctx_act @ ada_w[layer] + ada_b[layer], N_MOD, axis=-1)
        h_l = modulate(rms_norm(x_l, norm_pre_mix[layer]), mod_l[0], mod_l[1])
        h_c = modulate(rms_norm(x_c, norm_pre_mix[layer]), mod_c[0], mod_c[1])
        o_c, o_l = token_mixing(h_c, h_l, w_in[layer], w_out[layer], gdn_conv_w[layer], gdn_a_log[layer],
                                gdn_dt_bias[layer], gdn_norm[layer], attn_q_norm[layer], attn_k_norm[layer],
                                swa_sink[layer], hgrn_lb[layer], hgrn_norm[layer], cos, sin, with_ctx)
        x_l = x_l + mod_l[2] * rms_norm(o_l, norm_post_mix[layer])
        f_l = conv_ffn(modulate(rms_norm(x_l, norm_pre_ffn[layer]), mod_l[3], mod_l[4]),
                       ffn_w_up[layer], ffn_conv_w[layer], ffn_conv_b[layer], ffn_w_down[layer])
        x_l = x_l + mod_l[5] * rms_norm(f_l, norm_post_ffn[layer])
        if with_ctx:
            x_c = x_c + mod_c[2] * rms_norm(o_c, norm_post_mix[layer])
            f_c = conv_ffn(modulate(rms_norm(x_c, norm_pre_ffn[layer]), mod_c[3], mod_c[4]),
                           ffn_w_up[layer], ffn_conv_w[layer], ffn_conv_b[layer], ffn_w_down[layer])
            x_c = x_c + mod_c[5] * rms_norm(f_c, norm_post_ffn[layer])
    return x_l


_drawn_inputs = setup_inputs


def setup_inputs(seed=0):
    import zlib

    import numpy as np

    out = dict(_drawn_inputs(seed))
    spreads = {}
    factors = {'gdn_norm': 2.953,
     'attn_q_norm': 8.0,
     'attn_k_norm': 8.0,
     'swa_sink': 59.076,
     'hgrn_lb_raw': 7.213,
     'hgrn_norm': 2.904,
     'ffn_conv_b': 4.096}
    for name, (base, spread) in spreads.items():
        noise = np.random.default_rng([zlib.crc32(name.encode()), seed]).standard_normal(out[name].shape)
        drawn = base * np.exp(spread * noise) if base else spread * noise
        out[name] = jnp.asarray(drawn.astype(out[name].dtype))
    for name, factor in factors.items():
        out[name] = (out[name] * factor).astype(out[name].dtype)
    return out
```

```python
from contextlib import ExitStack

import numpy as np

import concourse.bass as bass
from concourse import mybir

ALU = mybir.AluOpType
ACT = mybir.ActivationFunctionType
F32 = mybir.dt.float32
U32 = mybir.dt.uint32
AX_X = mybir.AxisListType.X

P = 128
D_MODEL = 1024
SEQ = 1024
CTX = 256
T = SEQ + CTX
DEPTH = 2
HD = 64
H = 4
KD = D_MODEL // P
NT = T // P
D_FF = 2816
KF = D_FF // P
KH = KF // 2
N_MOD = 6
EPS = 1e-6
NEG = -1e30
LEVELS = 7

T_GDN, T_Z, T_BQ, T_BK, T_BV, T_CQ, T_CK, T_CV, T_HQ, T_HF, T_HI, T_HG, T_BETA = (
    0, 6, 8, 10, 11, 12, 14, 15, 16, 18, 22, 24, 26)
N_IN = 27
BETA_ROW, G_ROW = 0, 32

V_ADAB = 0
V_PRE_MIX = V_ADAB + N_MOD * KD
V_POST_MIX = V_PRE_MIX + KD
V_PRE_FFN = V_POST_MIX + KD
V_POST_FFN = V_PRE_FFN + KD
V_GCONV = V_POST_FFN + KD
V_FCONV = V_GCONV + 18
V_FBIAS = V_FCONV + 3 * 2 * KF
V_GNORM = V_FBIAS + 2 * KF
V_QNORM = V_GNORM + 1
V_KNORM = V_QNORM + 1
V_HNORM = V_KNORM + 1
V_ALOG = V_HNORM + 1
V_DTB = V_ALOG + 1
V_LB = V_DTB + 1
V_SINK = V_LB + DEPTH * 4
NV = V_SINK + H

C_IDENT = 0
C_ONES = C_IDENT + P
C_BLK = C_ONES + P
C_ROT = C_BLK + P
C_CUM = C_ROT + P
C_STR = C_CUM + 2 * P
C_LVL = C_STR + 2 * P
C_BAND = C_LVL + 2 * LEVELS * P
C_COS = C_BAND + 3 * P
C_SIN = C_COS + SEQ
NC = C_SIN + SEQ
N_MIX = C_BAND
SEGS = ((0, 512), (512, 512), (1024, 256))


def constants():
    i = np.arange(P)
    c = np.zeros((P, NC), np.float32)
    c[:, C_IDENT:C_IDENT + P] = np.eye(P)
    c[:, C_ONES:C_ONES + P] = 1
    c[:, C_BLK:C_BLK + P] = (i[:, None] // HD) == (i[None, :] // HD)
    for m in range(0, P, 2):
        c[m + 1, C_ROT + m] = -1
        c[m, C_ROT + m + 1] = 1
    a, b = i[:, None], i[None, :]
    c[:, C_CUM:C_CUM + P] = a <= b
    c[:, C_CUM + P:C_CUM + 2 * P] = a >= b
    c[:, C_STR:C_STR + P] = a > b
    c[:, C_STR + P:C_STR + 2 * P] = a < b
    for l in range(LEVELS):
        x, y = a >> l, b >> l
        even_odd = (x % 2 == 0) & (y == x + 1)
        c[:, C_LVL + l * P:C_LVL + (l + 1) * P] = even_odd
        c[:, C_LVL + (LEVELS + l) * P:C_LVL + (LEVELS + l + 1) * P] = even_odd.T
    c[:, C_BAND:C_BAND + P] = np.where(b >= a, 0, NEG)
    c[:, C_BAND + 2 * P:C_BAND + 3 * P] = np.where(b <= a, 0, NEG)
    n_freq = HD // 4
    inv = (1.0 / (np.float32(10000.0) ** (np.arange(n_freq, dtype=np.float32) / np.float32(n_freq)))).astype(np.float32)
    pos = np.arange(SEQ)
    ang = np.concatenate([(pos // 64).astype(np.float32)[:, None] * inv,
                          (pos % 64).astype(np.float32)[:, None] * inv], axis=-1)
    pair = (i % HD) // 2
    c[:, C_COS:C_COS + SEQ] = np.cos(ang.astype(np.float64))[:, pair].T
    c[:, C_SIN:C_SIN + SEQ] = np.sin(ang.astype(np.float64))[:, pair].T
    return c



class Chip:

    def __init__(self, nc):
        self.nc = nc
        self.count = 0

    def phase(self):
        self.count += 1
        return ExitStack()

    def sb(self, stack, name, shape, dt=F32):
        return stack.enter_context(self.nc.sbuf_tensor(f"{name}_{self.count}", shape, dt))

    def banks(self, stack, name, n):
        return stack.enter_context(self.nc.psum_tensor(f"{name}_{self.count}", [P, n * 512], F32))

    def sem(self, stack, name):
        return stack.enter_context(self.nc.semaphore(f"{name}_{self.count}"))

    def sems(self, stack, name, n):
        return [self.sem(stack, f"{name}{i}") for i in range(n)]

    def const(self, col, n=P):
        return self.consts[:, col:col + n]

    def vec(self, col, n=1):
        return self.vecs[:, col:col + n]


def spread(ap, n):
    return ap.unsqueeze(1).to_broadcast([ap.shape[0], n, ap.shape[1]])


def widen(ap, n):
    return ap.unsqueeze(2).to_broadcast([ap.shape[0], ap.shape[1], n])


def load_phase(k, a):
    with k.phase() as st:
        loaded, own = k.sem(st, "loaded"), k.sem(st, "own")
        with k.nc.Block() as block:
            @block.sync
            def _(sp):
                sp.dma_start(k.consts[:, :], a["consts"][:, 0:N_MIX]).then_inc(loaded, 16)
                sp.dma_start(k.cact[:, :, :], a["cond"]).then_inc(loaded, 16)
                sp.dma_start(k.xT[:, :, :], a["xT"]).then_inc(loaded, 16)

            @block.scalar
            def _(act):
                act.wait_ge(loaded, 48)
                act.sem_inc(loaded, -48)
                act.activation(k.cact[:, :, :], k.cact[:, :, :], ACT.Silu).then_inc(own, 1)
                act.wait_ge(own, 1)
                act.sem_inc(own, -1)


def modulation_phase(k, a, layer):
    n_it = N_MOD * D_MODEL // 512
    with k.phase() as st:
        w = k.sb(st, "ada_w", [P, 2, KD, 512])
        ps = [k.banks(st, f"mod_ps{s}", 1) for s in range(2)]
        vec_in = k.sem(st, "vec_in")
        w_full, w_free = k.sems(st, "w_full", 2), k.sems(st, "w_free", 2)
        ps_full, ps_free = k.sems(st, "ps_full", 2), k.sems(st, "ps_free", 2)
        own = k.sem(st, "own")
        with k.nc.Block() as block:
            @block.sync
            def _(sp):
                sp.dma_start(k.vecs[:, :], a["vecs"][layer]).then_inc(vec_in, 16)
                with sp.Fori(0, n_it // 2) as i:
                    for s in range(2):
                        sp.wait_ge(w_free[s], 1)
                        sp.sem_inc(w_free[s], -1)
                        sp.dma_start(w[:, s], a["ada_w"][layer, i * 2 + s]).then_inc(w_full[s], 16)

            @block.tensor
            def _(pe):
                with pe.Fori(0, n_it // 2) as i:
                    for s in range(2):
                        pe.wait_ge(w_full[s], 16)
                        pe.sem_inc(w_full[s], -16)
                        pe.wait_ge(ps_free[s], 1)
                        pe.sem_inc(ps_free[s], -1)
                        for q in range(4):
                            for t in range(KD):
                                mm = pe.matmul(ps[s][:, 2 * q:2 * q + 2], w[:, s, t, q * P:(q + 1) * P],
                                               k.cact[:, t, :], start=(t == 0), stop=(t == KD - 1))
                        mm.then_inc(ps_full[s], 1)

            @block.vector
            def _(dve):
                for s in range(2):
                    dve.sem_inc(w_free[s], 1)
                    dve.sem_inc(ps_free[s], 1)
                dve.wait_ge(vec_in, 16)
                dve.sem_inc(vec_in, -16)
                with dve.Fori(0, n_it // 2) as i:
                    for s in range(2):
                        dve.wait_ge(ps_full[s], 1)
                        dve.sem_inc(ps_full[s], -1)
                        dve.sem_inc(w_free[s], 1)
                        cols = bass.ds((i * 2 + s) * 4, 4)
                        dve.tensor_tensor(
                            k.mods[:, cols, :], ps[s][:, 0:8].rearrange("p (n s) -> p n s", s=2),
                            widen(k.vecs[:, bass.ds(V_ADAB + (i * 2 + s) * 4, 4)], 2), ALU.add).then_inc(own, 1)
                        dve.wait_ge(own, 1)
                        dve.sem_inc(own, -1)
                        dve.sem_inc(ps_free[s], 1)
                for s in range(2):
                    dve.wait_ge(ps_free[s], 1)
                    dve.sem_inc(ps_free[s], -1)
                for m, col in ((1, V_PRE_MIX), (4, V_PRE_FFN)):
                    part = k.mods[:, m * KD:(m + 1) * KD, :]
                    dve.tensor_scalar(part, part, 1.0, None, ALU.add).then_inc(own, 1)
                    dve.wait_ge(own, 1)
                    dve.sem_inc(own, -1)
                    dve.tensor_tensor(part, part, widen(k.vec(col, KD), 2), ALU.mult).then_inc(own, 1)
                    dve.wait_ge(own, 1)
                    dve.sem_inc(own, -1)
                for m, col in ((2, V_POST_MIX), (5, V_POST_FFN)):
                    part = k.mods[:, m * KD:(m + 1) * KD, :]
                    dve.tensor_tensor(part, part, widen(k.vec(col, KD), 2), ALU.mult).then_inc(own, 1)
                    dve.wait_ge(own, 1)
                    dve.sem_inc(own, -1)
                lb0, lb1 = k.vec(V_LB, 4), k.vec(V_LB + 4, 4)
                if layer == 0:
                    dve.memset(k.lb[:, 0:4], 0.0).then_inc(own, 1)
                    dve.wait_ge(own, 1)
                    dve.sem_inc(own, -1)
                    dve.memset(k.lb[:, 4:8], 1.0).then_inc(own, 1)
                    dve.wait_ge(own, 1)
                    dve.sem_inc(own, -1)
                else:
                    dve.tensor_tensor(k.lb[:, 0:4], lb1, lb0, ALU.subtract).then_inc(own, 1)
                    dve.wait_ge(own, 1)
                    dve.sem_inc(own, -1)
                for s in range(2):
                    dve.wait_ge(w_free[s], 1)
                    dve.sem_inc(w_free[s], -1)

        own_a, go, back = k.sem(st, "own_a"), k.sem(st, "go"), k.sem(st, "back")
        with k.nc.Block() as block:
            @block.scalar
            def _(act):
                if layer:
                    act.activation(k.lb[:, 4:8], k.lb[:, 0:4], ACT.Sigmoid, scale=-1.0)
                    act.activation(k.lb[:, 0:4], k.lb[:, 0:4], ACT.Sigmoid).then_inc(own_a, 1)
                    act.wait_ge(own_a, 1)
                    act.sem_inc(own_a, -1)
                act.activation(k.expa[:, :], k.vec(V_ALOG), ACT.Exp).then_inc(own_a, 1)
                act.wait_ge(own_a, 1)
                act.sem_inc(own_a, -1)
                act.activation(k.expa[:, :], k.expa[:, :], ACT.Copy, scale=-1.0).then_inc(own_a, 1)
                act.wait_ge(own_a, 1)
                act.sem_inc(own_a, -1)


def token_parts(n):
    return [(0, SEQ, 0)] + ([(SEQ, n, 1)] if n > SEQ else [])


def row_factor(k, st, dve, act_sems, ps, r, n, own, width, eps=EPS):
    dve.tensor_scalar(r[:, 0:n], ps[:, 0:n], 1.0 / width, eps, ALU.mult, ALU.add).then_inc(own, 1)
    dve.wait_ge(own, 1)
    dve.sem_inc(own, -1)
    dve.reciprocal(r[:, 0:n], r[:, 0:n]).then_inc(own, 1)
    dve.wait_ge(own, 1)
    dve.sem_inc(own, -1)
    dve.sem_inc(act_sems, 1)


def norm_phase(k, n, m_shift, m_scale, spill=None):
    with k.phase() as st:
        sq = k.sb(st, "sq", [P, 2, T])
        acc = k.sb(st, "acc", [P, T])
        r = k.sb(st, "r", [P, T])
        ps = k.banks(st, "ps", 3)
        sq_full, sq_free = k.sems(st, "sq_full", 2), k.sems(st, "sq_free", 2)
        acc_pe, sum_dve, inv_act, root_dve = (k.sem(st, s) for s in ("acc_pe", "sum_dve", "inv_act", "root_dve"))
        scaled = k.sem(st, "scaled")
        own_a, own_v, spilled = k.sem(st, "own_a"), k.sem(st, "own_v"), k.sem(st, "spilled")
        with k.nc.Block() as block:
            @block.scalar
            def _(act):
                for t in range(KD):
                    if t >= 2:
                        act.wait_ge(sq_free[t % 2], 1)
                        act.sem_inc(sq_free[t % 2], -1)
                    act.activation(sq[:, t % 2, 0:n], k.xT[:, t, 0:n], ACT.Square).then_inc(sq_full[t % 2], 1)
                act.wait_ge(inv_act, 1)
                act.sem_inc(inv_act, -1)
                act.activation(r[:, 0:n], r[:, 0:n], ACT.Sqrt).then_inc(own_a, 1)
                act.wait_ge(own_a, 1)
                act.sem_inc(own_a, -1)
                act.sem_inc(root_dve, 1)
                for t in range(KD):
                    act.wait_ge(scaled, 1)
                    act.sem_inc(scaled, -1)
                    for lo, hi, s in token_parts(n):
                        last = act.activation(k.hT[:, t, lo:hi], k.hT[:, t, lo:hi], ACT.Identity,
                                              bias=k.mods[:, m_shift * KD + t, s:s + 1])
                last.then_inc(own_a, 1)
                act.wait_ge(own_a, 1)
                act.sem_inc(own_a, -1)

            @block.vector
            def _(dve):
                for t in range(KD):
                    dve.wait_ge(sq_full[t % 2], 1)
                    dve.sem_inc(sq_full[t % 2], -1)
                    if t == 0:
                        ins = dve.tensor_copy(acc[:, 0:n], sq[:, 0, 0:n])
                    else:
                        ins = dve.tensor_tensor(acc[:, 0:n], acc[:, 0:n], sq[:, t % 2, 0:n], ALU.add)
                    if t < KD - 2:
                        ins.then_inc(own_v, 1)
                        dve.wait_ge(own_v, 1)
                        dve.sem_inc(own_v, -1)
                        dve.sem_inc(sq_free[t % 2], 1)
                    elif t < KD - 1:
                        ins.then_inc(own_v, 1)
                        dve.wait_ge(own_v, 1)
                        dve.sem_inc(own_v, -1)
                    else:
                        ins.then_inc(own_v, 1)
                        dve.wait_ge(own_v, 1)
                        dve.sem_inc(own_v, -1)
                        dve.sem_inc(acc_pe, 1)
                dve.wait_ge(sum_dve, 1)
                dve.sem_inc(sum_dve, -1)
                row_factor(k, st, dve, inv_act, ps, r, n, own_v, D_MODEL)
                dve.wait_ge(root_dve, 1)
                dve.sem_inc(root_dve, -1)
                for t in range(KD):
                    for lo, hi, s in token_parts(n):
                        ins = dve.scalar_tensor_tensor(k.hT[:, t, lo:hi], k.xT[:, t, lo:hi],
                                                       k.mods[:, m_scale * KD + t, s:s + 1], r[:, lo:hi],
                                                       ALU.mult, ALU.mult)
                        if hi < n:
                            ins.then_inc(own_v, 1)
                            dve.wait_ge(own_v, 1)
                            dve.sem_inc(own_v, -1)
                    ins.then_inc(scaled, 1)

            @block.tensor
            def _(pe):
                pe.wait_ge(acc_pe, 1)
                pe.sem_inc(acc_pe, -1)
                for lo, w in SEGS:
                    if lo < n:
                        mm = pe.matmul(ps[:, lo:lo + w], k.const(C_ONES), acc[:, lo:lo + w], start=True, stop=True)
                mm.then_inc(sum_dve, 1)

            if spill is not None:
                @block.sync
                def _(sp):
                    sp.dma_start(spill, k.xT[:, :, :]).then_inc(spilled, 16)
                    sp.wait_ge(spilled, 16)
                    sp.sem_inc(spilled, -16)


def products(pe, ps, w, rhs, n_k, n):
    for t in range(n_k):
        for lo, width in SEGS:
            if lo < n:
                mm = pe.matmul(ps[:, lo:lo + width], w[:, t, :], rhs[:, t, lo:lo + width],
                               start=(t == 0), stop=(t == n_k - 1))
    return mm


def input_projection_phase(k, a, layer):
    with k.phase() as st:
        w = k.sb(st, "w_in", [P, 2, KD, P])
        out = k.sb(st, "rows", [P, 2, T])
        ps = [k.banks(st, f"ps{s}", 3) for s in range(2)]
        w_full, w_free = k.sems(st, "w_full", 2), k.sems(st, "w_free", 2)
        ps_full, ps_free = k.sems(st, "ps_full", 2), k.sems(st, "ps_free", 2)
        out_free = k.sems(st, "out_free", 2)
        own = k.sem(st, "own")
        pairs = N_IN // 2

        def load(sp, s, tile):
            sp.wait_ge(w_free[s], 1)
            sp.sem_inc(w_free[s], -1)
            sp.dma_start(w[:, s], a["w_in"][layer, tile]).then_inc(w_full[s], 16)

        def multiply(pe, s):
            pe.wait_ge(w_full[s], 16)
            pe.sem_inc(w_full[s], -16)
            pe.wait_ge(ps_free[s], 1)
            pe.sem_inc(ps_free[s], -1)
            products(pe, ps[s], w[:, s], k.hT, KD, T).then_inc(ps_full[s], 1)

        def collect(act, s, tile):
            act.wait_ge(ps_full[s], 1)
            act.sem_inc(ps_full[s], -1)
            act.sem_inc(w_free[s], 1)
            act.wait_ge(out_free[s], 16)
            act.sem_inc(out_free[s], -16)
            act.activation(out[:, s, :], ps[s][:, 0:T], ACT.Copy).then_inc(own, 1)
            act.wait_ge(own, 1)
            act.sem_inc(own, -1)
            act.sem_inc(ps_free[s], 1)
            act.dma_start(k.rows[tile], out[:, s, :]).then_inc(out_free[s], 16)

        with k.nc.Block() as block:
            @block.sync
            def _(sp):
                with sp.Fori(0, pairs) as i:
                    for s in range(2):
                        load(sp, s, i * 2 + s)
                load(sp, 0, N_IN - 1)

            @block.tensor
            def _(pe):
                with pe.Fori(0, pairs) as i:
                    for s in range(2):
                        multiply(pe, s)
                multiply(pe, 0)

            @block.scalar
            def _(act):
                for s in range(2):
                    act.sem_inc(w_free[s], 1)
                    act.sem_inc(ps_free[s], 1)
                    act.sem_inc(out_free[s], 16)
                with act.Fori(0, pairs) as i:
                    for s in range(2):
                        collect(act, s, i * 2 + s)
                collect(act, 0, N_IN - 1)
                for s in range(2):
                    act.wait_ge(w_free[s], 1)
                    act.sem_inc(w_free[s], -1)
                    act.wait_ge(ps_free[s], 1)
                    act.sem_inc(ps_free[s], -1)
                    act.wait_ge(out_free[s], 16)
                    act.sem_inc(out_free[s], -16)


def matmul_into_phase(k, w_dram, n_k, rhs, dest, n, add):
    with k.phase() as st:
        w = k.sb(st, "w", [P, 2, n_k, P])
        ps = [k.banks(st, f"ps{s}", 3) for s in range(2)]
        w_full, w_free = k.sems(st, "w_full", 2), k.sems(st, "w_free", 2)
        ps_full, ps_free = k.sems(st, "ps_full", 2), k.sems(st, "ps_free", 2)
        own = k.sem(st, "own")
        with k.nc.Block() as block:
            @block.sync
            def _(sp):
                with sp.Fori(0, KD // 2) as i:
                    for s in range(2):
                        sp.wait_ge(w_free[s], 1)
                        sp.sem_inc(w_free[s], -1)
                        sp.dma_start(w[:, s], w_dram[i * 2 + s]).then_inc(w_full[s], 16)

            @block.tensor
            def _(pe):
                with pe.Fori(0, KD // 2) as i:
                    for s in range(2):
                        pe.wait_ge(w_full[s], 16)
                        pe.sem_inc(w_full[s], -16)
                        pe.wait_ge(ps_free[s], 1)
                        pe.sem_inc(ps_free[s], -1)
                        products(pe, ps[s], w[:, s], rhs, n_k, n).then_inc(ps_full[s], 1)

            @block.vector
            def _(dve):
                for s in range(2):
                    dve.sem_inc(w_free[s], 1)
                    dve.sem_inc(ps_free[s], 1)
                with dve.Fori(0, KD // 2) as i:
                    for s in range(2):
                        dve.wait_ge(ps_full[s], 1)
                        dve.sem_inc(ps_full[s], -1)
                        dve.sem_inc(w_free[s], 1)
                        target = dest[:, i * 2 + s, 0:n]
                        if add:
                            ins = dve.tensor_tensor(target, ps[s][:, 0:n], target, ALU.add)
                        else:
                            ins = dve.tensor_copy(target, ps[s][:, 0:n])
                        ins.then_inc(own, 1)
                        dve.wait_ge(own, 1)
                        dve.sem_inc(own, -1)
                        dve.sem_inc(ps_free[s], 1)
                for s in range(2):
                    dve.wait_ge(w_free[s], 1)
                    dve.sem_inc(w_free[s], -1)
                    dve.wait_ge(ps_free[s], 1)
                    dve.sem_inc(ps_free[s], -1)


def residual_phase(k, y, n, m_gate, reload=None):
    with k.phase() as st:
        sq = k.sb(st, "sq", [P, 2, T])
        acc = k.sb(st, "acc", [P, T])
        r = k.sb(st, "r", [P, T])
        ps = k.banks(st, "ps", 3)
        sq_full, sq_free = k.sems(st, "sq_full", 2), k.sems(st, "sq_free", 2)
        acc_pe, sum_dve, inv_act, root_dve = (k.sem(st, s) for s in ("acc_pe", "sum_dve", "inv_act", "root_dve"))
        own_a, own_v, x_in, scaled = (k.sem(st, s) for s in ("own_a", "own_v", "x_in", "scaled"))
        own_p = k.sem(st, "own_p")
        with k.nc.Block() as block:
            @block.scalar
            def _(act):
                for t in range(KD):
                    if t >= 2:
                        act.wait_ge(sq_free[t % 2], 1)
                        act.sem_inc(sq_free[t % 2], -1)
                    act.activation(sq[:, t % 2, 0:n], y[:, t, 0:n], ACT.Square).then_inc(sq_full[t % 2], 1)
                act.wait_ge(inv_act, 1)
                act.sem_inc(inv_act, -1)
                act.activation(r[:, 0:n], r[:, 0:n], ACT.Sqrt).then_inc(own_a, 1)
                act.wait_ge(own_a, 1)
                act.sem_inc(own_a, -1)
                act.sem_inc(root_dve, 1)

            @block.vector
            def _(dve):
                for t in range(KD):
                    dve.wait_ge(sq_full[t % 2], 1)
                    dve.sem_inc(sq_full[t % 2], -1)
                    if t == 0:
                        ins = dve.tensor_copy(acc[:, 0:n], sq[:, 0, 0:n])
                    else:
                        ins = dve.tensor_tensor(acc[:, 0:n], acc[:, 0:n], sq[:, t % 2, 0:n], ALU.add)
                    if t < KD - 2:
                        ins.then_inc(own_v, 1)
                        dve.wait_ge(own_v, 1)
                        dve.sem_inc(own_v, -1)
                        dve.sem_inc(sq_free[t % 2], 1)
                    elif t < KD - 1:
                        ins.then_inc(own_v, 1)
                        dve.wait_ge(own_v, 1)
                        dve.sem_inc(own_v, -1)
                    else:
                        ins.then_inc(own_v, 1)
                        dve.wait_ge(own_v, 1)
                        dve.sem_inc(own_v, -1)
                        dve.sem_inc(acc_pe, 1)
                dve.wait_ge(sum_dve, 1)
                dve.sem_inc(sum_dve, -1)
                row_factor(k, st, dve, inv_act, ps, r, n, own_v, D_MODEL)
                dve.wait_ge(root_dve, 1)
                dve.sem_inc(root_dve, -1)
                for t in range(KD):
                    for lo, hi, s in token_parts(n):
                        ins = dve.scalar_tensor_tensor(y[:, t, lo:hi], y[:, t, lo:hi],
                                                       k.mods[:, m_gate * KD + t, s:s + 1], r[:, lo:hi],
                                                       ALU.mult, ALU.mult)
                        if hi < n:
                            ins.then_inc(own_v, 1)
                            dve.wait_ge(own_v, 1)
                            dve.sem_inc(own_v, -1)
                    ins.then_inc(scaled, 1)

            @block.gpsimd
            def _(pool):
                if reload is not None:
                    pool.wait_ge(x_in, 16)
                    pool.sem_inc(x_in, -16)
                for t in range(KD):
                    pool.wait_ge(scaled, 1)
                    pool.sem_inc(scaled, -1)
                    last = pool.tensor_tensor(k.xT[:, t, 0:n], k.xT[:, t, 0:n], y[:, t, 0:n], ALU.add)
                last.then_inc(own_p, 1)
                pool.wait_ge(own_p, 1)
                pool.sem_inc(own_p, -1)

            @block.tensor
            def _(pe):
                pe.wait_ge(acc_pe, 1)
                pe.sem_inc(acc_pe, -1)
                for lo, w in SEGS:
                    if lo < n:
                        mm = pe.matmul(ps[:, lo:lo + w], k.const(C_ONES), acc[:, lo:lo + w], start=True, stop=True)
                mm.then_inc(sum_dve, 1)

            if reload is not None:
                @block.sync
                def _(sp):
                    sp.dma_start(k.xT[:, :, :], reload).then_inc(x_in, 16)


def conv_parts(n):
    return [(0, SEQ)] + ([(SEQ, n)] if n > SEQ else [])


class Job:

    def __init__(self, tile, dest, taps=None, silu=False, width=None, factor=None, rope=False, to_tokens=None):
        self.tile, self.dest, self.taps, self.silu = tile, dest, taps, silu
        self.width, self.factor, self.rope, self.to_tokens = width, factor, rope, to_tokens


def rows_phase(k, jobs, trig=None):
    with k.phase() as st:
        raw = k.sb(st, "raw", [P, 2, T])
        sq = k.sb(st, "sq", [P, 2, T])
        r = k.sb(st, "r", [P, 2, T])
        rot = k.sb(st, "rot", [P, SEQ]) if trig is not None else None
        ps = [k.banks(st, f"ps{s}", 3) for s in range(2)]
        ps_rot = k.banks(st, "ps_rot", 2)
        raw_in, raw_free = k.sems(st, "raw_in", 2), k.sems(st, "raw_free", 2)
        centre_dve, taps_act, y_dve, sq_pe, sum_dve, inv_act, root_dve = (
            k.sem(st, s) for s in ("centre_dve", "taps_act", "y_dve", "sq_pe", "sum_dve", "inv_act", "root_dve"))
        y_pe, rot_dve, pass_pe, tok_dve, tok_free = (
            k.sem(st, s) for s in ("y_pe", "rot_dve", "pass_pe", "tok_dve", "tok_free"))
        own_a, own_v = k.sem(st, "own_a"), k.sem(st, "own_v")
        with k.nc.Block() as block:
            @block.sync
            def _(sp):
                for j, job in enumerate(jobs):
                    if j >= 2:
                        sp.wait_ge(raw_free[j % 2], 1)
                        sp.sem_inc(raw_free[j % 2], -1)
                    sp.dma_start(raw[:, j % 2, :], k.rows[job.tile]).then_inc(raw_in[j % 2], 16)

            @block.scalar
            def _(act):
                for j, job in enumerate(jobs):
                    s = j % 2
                    act.wait_ge(raw_in[s], 16)
                    act.sem_inc(raw_in[s], -16)
                    if job.taps is not None:
                        act.activation(job.dest, raw[:, s, :], ACT.Copy,
                                       scale=k.vec(V_GCONV + 6 + job.taps)).then_inc(own_a, 1)
                        act.wait_ge(own_a, 1)
                        act.sem_inc(own_a, -1)
                        act.sem_inc(centre_dve, 1)
                        act.wait_ge(taps_act, 1)
                        act.sem_inc(taps_act, -1)
                        act.activation(job.dest, job.dest, ACT.Silu).then_inc(own_a, 1)
                        act.wait_ge(own_a, 1)
                        act.sem_inc(own_a, -1)
                    else:
                        act.activation(job.dest, raw[:, s, :], ACT.Silu if job.silu else ACT.Copy).then_inc(own_a, 1)
                        act.wait_ge(own_a, 1)
                        act.sem_inc(own_a, -1)
                    act.sem_inc(raw_free[s], 1)
                    if job.width is not None:
                        act.activation(sq[:, s, :], job.dest, ACT.Square).then_inc(own_a, 1)
                        act.wait_ge(own_a, 1)
                        act.sem_inc(own_a, -1)
                        act.sem_inc(sq_pe, 1)
                        act.wait_ge(inv_act, 1)
                        act.sem_inc(inv_act, -1)
                        act.activation(r[:, s, :], r[:, s, :], ACT.Sqrt).then_inc(own_a, 1)
                        act.wait_ge(own_a, 1)
                        act.sem_inc(own_a, -1)
                        act.sem_inc(root_dve, 1)
                    elif job.rope or job.to_tokens is not None:
                        act.sem_inc(y_dve, 1)
                for s in range(min(2, len(jobs))):
                    act.wait_ge(raw_free[s], 1)
                    act.sem_inc(raw_free[s], -1)

            @block.vector
            def _(dve):
                for j, job in enumerate(jobs):
                    s = j % 2
                    if job.taps is not None:
                        dve.wait_ge(centre_dve, 1)
                        dve.sem_inc(centre_dve, -1)
                        for lo, hi in conv_parts(T):
                            dve.scalar_tensor_tensor(
                                job.dest[:, lo + 1:hi], raw[:, s, lo:hi - 1], k.vec(V_GCONV + job.taps),
                                job.dest[:, lo + 1:hi], ALU.mult, ALU.add).then_inc(own_v, 1)
                            dve.wait_ge(own_v, 1)
                            dve.sem_inc(own_v, -1)
                            dve.scalar_tensor_tensor(
                                job.dest[:, lo:hi - 1], raw[:, s, lo + 1:hi], k.vec(V_GCONV + 12 + job.taps),
                                job.dest[:, lo:hi - 1], ALU.mult, ALU.add).then_inc(own_v, 1)
                            dve.wait_ge(own_v, 1)
                            dve.sem_inc(own_v, -1)
                        dve.sem_inc(taps_act, 1)
                    if job.width is not None:
                        dve.wait_ge(sum_dve, 1)
                        dve.sem_inc(sum_dve, -1)
                        row_factor(k, st, dve, inv_act, ps[s], r[:, s, :], T, own_v, job.width)
                        dve.wait_ge(root_dve, 1)
                        dve.sem_inc(root_dve, -1)
                        dve.scalar_tensor_tensor(job.dest, job.dest, job.factor, r[:, s, :],
                                                 ALU.mult, ALU.mult).then_inc(own_v, 1)
                        dve.wait_ge(own_v, 1)
                        dve.sem_inc(own_v, -1)
                    elif job.rope or job.to_tokens is not None:
                        dve.wait_ge(y_dve, 1)
                        dve.sem_inc(y_dve, -1)
                    if job.rope:
                        dve.sem_inc(y_pe, 1)
                        dve.wait_ge(rot_dve, 1)
                        dve.sem_inc(rot_dve, -1)
                        dve.tensor_tensor(rot[:, :], ps_rot[:, 0:SEQ], trig[:, SEQ:], ALU.mult).then_inc(own_v, 1)
                        dve.wait_ge(own_v, 1)
                        dve.sem_inc(own_v, -1)
                        lat = job.dest[:, 0:SEQ]
                        dve.tensor_tensor(lat, lat, trig[:, 0:SEQ], ALU.mult).then_inc(own_v, 1)
                        dve.wait_ge(own_v, 1)
                        dve.sem_inc(own_v, -1)
                        dve.tensor_tensor(lat, lat, rot[:, :], ALU.add).then_inc(own_v, 1)
                        dve.wait_ge(own_v, 1)
                        dve.sem_inc(own_v, -1)
                    if job.to_tokens is not None:
                        dve.sem_inc(pass_pe, 1)
                        for c0 in range(0, NT, 4):
                            n = min(4, NT - c0)
                            dve.wait_ge(tok_dve, 1)
                            dve.sem_inc(tok_dve, -1)
                            dve.tensor_copy(job.to_tokens[:, c0:c0 + n, :],
                                            ps_rot[:, 0:n * P].rearrange("p (c f) -> p c f", f=P)).then_inc(own_v, 1)
                            dve.wait_ge(own_v, 1)
                            dve.sem_inc(own_v, -1)
                            dve.sem_inc(tok_free, 1)

            @block.tensor
            def _(pe):
                for j, job in enumerate(jobs):
                    s = j % 2
                    if job.width is not None:
                        pe.wait_ge(sq_pe, 1)
                        pe.sem_inc(sq_pe, -1)
                        for lo, w in SEGS:
                            mm = pe.matmul(ps[s][:, lo:lo + w], k.const(C_BLK), sq[:, s, lo:lo + w],
                                           start=True, stop=True)
                        mm.then_inc(sum_dve, 1)
                    if job.rope:
                        pe.wait_ge(y_pe, 1)
                        pe.sem_inc(y_pe, -1)
                        for lo, w in SEGS[:2]:
                            mm = pe.matmul(ps_rot[:, lo:lo + w], k.const(C_ROT), job.dest[:, lo:lo + w],
                                           start=True, stop=True)
                        mm.then_inc(rot_dve, 1)
                    if job.to_tokens is not None:
                        pe.wait_ge(pass_pe, 1)
                        pe.sem_inc(pass_pe, -1)
                        for c0 in range(0, NT, 4):
                            if c0:
                                pe.wait_ge(tok_free, 1)
                                pe.sem_inc(tok_free, -1)
                            for c in range(c0, min(c0 + 4, NT)):
                                mm = pe.transpose(ps_rot[:, (c - c0) * P:(c - c0 + 1) * P],
                                                  job.dest[:, c * P:(c + 1) * P], k.const(C_IDENT))
                            mm.then_inc(tok_dve, 1)
                        pe.wait_ge(tok_free, 1)
                        pe.sem_inc(tok_free, -1)


def gate_phase(k, pairs, oT_tile, z_tile, gain_col):
    with k.phase() as st:
        z = k.sb(st, "z", [P, 2, T])
        sq = k.sb(st, "sq", [P, 2, T])
        r = k.sb(st, "r", [P, 2, T])
        ps = [k.banks(st, f"ps{s}", 3) for s in range(2)]
        z_in = k.sems(st, "z_in", 2)
        o_act, sq_pe, sum_dve, inv_act, root_dve = (
            k.sem(st, s) for s in ("o_act", "sq_pe", "sum_dve", "inv_act", "root_dve"))
        own_a, own_v = k.sem(st, "own_a"), k.sem(st, "own_v")
        with k.nc.Block() as block:
            @block.sync
            def _(sp):
                for s in range(2):
                    sp.dma_start(z[:, s, :], k.rows[z_tile + s]).then_inc(z_in[s], 16)

            @block.scalar
            def _(act):
                for s in range(2):
                    act.wait_ge(z_in[s], 16)
                    act.sem_inc(z_in[s], -16)
                    act.activation(z[:, s, :], z[:, s, :], ACT.Silu).then_inc(own_a, 1)
                    act.wait_ge(own_a, 1)
                    act.sem_inc(own_a, -1)
                for s in range(2):
                    act.wait_ge(o_act, 1)
                    act.sem_inc(o_act, -1)
                    act.activation(sq[:, s, :], pairs[:, 0, s, :], ACT.Square).then_inc(own_a, 1)
                    act.wait_ge(own_a, 1)
                    act.sem_inc(own_a, -1)
                    act.sem_inc(sq_pe, 1)
                for s in range(2):
                    act.wait_ge(inv_act, 1)
                    act.sem_inc(inv_act, -1)
                    act.activation(r[:, s, :], r[:, s, :], ACT.Sqrt).then_inc(own_a, 1)
                    act.wait_ge(own_a, 1)
                    act.sem_inc(own_a, -1)
                    act.sem_inc(root_dve, 1)

            @block.tensor
            def _(pe):
                for s in range(2):
                    pe.wait_ge(sq_pe, 1)
                    pe.sem_inc(sq_pe, -1)
                    for lo, w in SEGS:
                        mm = pe.matmul(ps[s][:, lo:lo + w], k.const(C_BLK), sq[:, s, lo:lo + w], start=True, stop=True)
                    mm.then_inc(sum_dve, 1)

            @block.vector
            def _(dve):
                for s in range(2):
                    dve.tensor_tensor(pairs[:, 0, s, :], pairs[:, 0, s, :], pairs[:, 1, s, :], ALU.add)\
                        .then_inc(own_v, 1)
                    dve.wait_ge(own_v, 1)
                    dve.sem_inc(own_v, -1)
                    dve.sem_inc(o_act, 1)
                for s in range(2):
                    dve.wait_ge(sum_dve, 1)
                    dve.sem_inc(sum_dve, -1)
                    row_factor(k, st, dve, inv_act, ps[s], r[:, s, :], T, own_v, HD)
                for s in range(2):
                    dve.wait_ge(root_dve, 1)
                    dve.sem_inc(root_dve, -1)
                    dve.scalar_tensor_tensor(pairs[:, 0, s, :], pairs[:, 0, s, :], k.vec(gain_col),
                                             r[:, s, :], ALU.mult, ALU.mult).then_inc(own_v, 1)
                    dve.wait_ge(own_v, 1)
                    dve.sem_inc(own_v, -1)
                    dve.tensor_tensor(k.hT[:, oT_tile + s, :], pairs[:, 0, s, :], z[:, s, :], ALU.mult)\
                        .then_inc(own_v, 1)
                    dve.wait_ge(own_v, 1)
                    dve.sem_inc(own_v, -1)


def decay_rows_phase(k, bg):
    with k.phase() as st:
        lin = k.sb(st, "lin", [HD, T])
        soft = k.sb(st, "soft", [HD, T])
        came, a_dve, v_act, own_a, own_v = (k.sem(st, s) for s in ("came", "a_dve", "v_act", "own_a", "own_v"))
        g = slice(G_ROW, G_ROW + 2 * H)
        with k.nc.Block() as block:
            @block.sync
            def _(sp):
                sp.dma_start(bg[:, :], k.rows[T_BETA][0:HD]).then_inc(came, 16)

            @block.scalar
            def _(act):
                act.wait_ge(came, 16)
                act.sem_inc(came, -16)
                act.activation(lin[g, :], bg[g, :], ACT.Identity, bias=k.vecs[g, V_DTB:V_DTB + 1]).then_inc(own_a, 1)
                act.wait_ge(own_a, 1)
                act.sem_inc(own_a, -1)
                act.sem_inc(a_dve, 1)
                act.activation(bg[0:2 * H, :], bg[0:2 * H, :], ACT.Sigmoid).then_inc(own_a, 1)
                act.wait_ge(own_a, 1)
                act.sem_inc(own_a, -1)
                act.wait_ge(v_act, 1)
                act.sem_inc(v_act, -1)
                act.activation(soft[g, :], soft[g, :], ACT.Exp).then_inc(own_a, 1)
                act.wait_ge(own_a, 1)
                act.sem_inc(own_a, -1)
                act.activation(soft[g, :], soft[g, :], ACT.Ln, bias=1.0).then_inc(own_a, 1)
                act.wait_ge(own_a, 1)
                act.sem_inc(own_a, -1)
                act.sem_inc(a_dve, 1)

            @block.vector
            def _(dve):
                dve.wait_ge(a_dve, 1)
                dve.sem_inc(a_dve, -1)
                dve.tensor_scalar(soft[g, :], lin[g, :], 0.0, 2.0, ALU.min, ALU.mult).then_inc(own_v, 1)
                dve.wait_ge(own_v, 1)
                dve.sem_inc(own_v, -1)
                dve.tensor_tensor(soft[g, :], soft[g, :], lin[g, :], ALU.subtract).then_inc(own_v, 1)
                dve.wait_ge(own_v, 1)
                dve.sem_inc(own_v, -1)
                dve.sem_inc(v_act, 1)
                dve.tensor_scalar(lin[g, :], lin[g, :], 0.0, None, ALU.max).then_inc(own_v, 1)
                dve.wait_ge(own_v, 1)
                dve.sem_inc(own_v, -1)
                dve.wait_ge(a_dve, 1)
                dve.sem_inc(a_dve, -1)
                dve.tensor_tensor(lin[g, :], lin[g, :], soft[g, :], ALU.add).then_inc(own_v, 1)
                dve.wait_ge(own_v, 1)
                dve.sem_inc(own_v, -1)
                dve.tensor_scalar(bg[g, :], lin[g, :], k.expa[g, 0:1], None, ALU.mult).then_inc(own_v, 1)
                dve.wait_ge(own_v, 1)
                dve.sem_inc(own_v, -1)


def chunk_of(d, i):
    return (i + NT - CTX // P) % NT if d == 0 else NT - 1 - i


def gdn_phase(k, qkv, bg, both):
    with k.phase() as st:
        stg = k.sb(st, "stg", [P, 2, 6, P])
        bgs = k.sb(st, "bgs", [HD, 2, P])
        tok = k.sb(st, "tok", [P, 2, 4, P])
        bgt = k.sb(st, "bgt", [P, 2, HD])
        nb = k.sb(st, "nb", [P, 2, H])
        gm = k.sb(st, "gm", [P, 2, H, P])
        gb = k.sb(st, "gb", [P, 2, H, HD])
        dec = k.sb(st, "dec", [P, 2, H, P])
        ecum = k.sb(st, "ecum", [P, 2, 2 * P + 2 * H])
        dm = dec
        attn = k.sb(st, "attn", [P, 2, H, P])
        nm = k.sb(st, "nm", [P, 2, H, P])
        S = k.sb(st, "S", [P, 2, H, P])
        Ti = k.sb(st, "Ti", [P, 2, H, P])
        vm, nbd = gm, S
        qd = k.sb(st, "qd", [P, 2, 2, P])
        ke = k.sb(st, "ke", [P, 2, H, HD])
        kd = k.sb(st, "kd", [P, 2, H, HD])
        wtn = k.sb(st, "wtn", [P, 2, 2, P])
        vn = k.sb(st, "vn", [P, 2, H, HD])
        state = k.sb(st, "state", [P, 2, 2, P])
        tmp = k.sb(st, "tmp", [P, 2, 2, P])
        B = [[k.banks(st, f"b{d}{b}", 1) for b in range(4)] for d in range(2)]
        names = ("staged_pe tr_act bgt_dve tok_pe gm_pe nb_pool rc_act de_pool dm_dve ke_pe kk_dve s2_pe t2_act "
                 "inv_pe v_dve vm_pe u_dve wt_act wtn_pe vn_dve vn_pe o_act su_dve state_pe").split()
        sem = {n: k.sems(st, n, 2) for n in names}
        own = {e: k.sem(st, f"own_{e}") for e in ("act", "dve", "pool")}
        beta = [bgt[:, d, BETA_ROW + H * d:BETA_ROW + H * (d + 1)] for d in range(2)]
        gcol = [bgt[:, d, G_ROW + H * d:G_ROW + H * (d + 1)] for d in range(2)]
        ident = k.const(C_IDENT)
        cum = [k.const(C_CUM + d * P) for d in range(2)]
        strict = [k.const(C_STR + d * P) for d in range(2)]
        after = [k.const(C_STR + (1 - d) * P) for d in range(2)]

        def heads(b):
            return b[:, :].rearrange("p (h f) -> p h f", f=P)

        def level_ji(d, l):
            return k.const(C_LVL + (d * LEVELS + l) * P)

        def level_ij(d, l):
            return k.const(C_LVL + ((1 - d) * LEVELS + l) * P)

        with k.nc.Block() as block:
            @block.scalar
            def _(act):
                with act.Fori(0, NT) as i:
                    for d in range(2):
                        col = bass.ds(chunk_of(d, i) * P, P)
                        act.activation(stg[:, d], qkv[:, :, col], ACT.Copy)
                        act.activation(bgs[:, d, :], bg[:, col], ACT.Copy).then_inc(own["act"], 1)
                        act.wait_ge(own["act"], 1)
                        act.sem_inc(own["act"], -1)
                        act.sem_inc(sem["staged_pe"][d], 1)
                    for d in range(2):
                        act.wait_ge(sem["tr_act"][d], 1)
                        act.sem_inc(sem["tr_act"][d], -1)
                        act.activation(tok[:, d], heads(B[d][0]), ACT.Copy).then_inc(own["act"], 1)
                        act.wait_ge(own["act"], 1)
                        act.sem_inc(own["act"], -1)
                        act.activation(bgt[:, d, :], B[d][1][:, 0:HD], ACT.Copy).then_inc(own["act"], 1)
                        act.wait_ge(own["act"], 1)
                        act.sem_inc(own["act"], -1)
                        act.sem_inc(sem["bgt_dve"][d], 1)
                        act.sem_inc(sem["tok_pe"][d], 1)
                    for d in range(2):
                        act.wait_ge(sem["rc_act"][d], 1)
                        act.sem_inc(sem["rc_act"][d], -1)
                        act.activation(dec[:, d], heads(B[d][2]), ACT.Exp).then_inc(own["act"], 1)
                        act.wait_ge(own["act"], 1)
                        act.sem_inc(own["act"], -1)
                        act.activation(ecum[:, d, :], B[d][3][:, 0:2 * P + 2 * H], ACT.Exp).then_inc(own["act"], 1)
                        act.wait_ge(own["act"], 1)
                        act.sem_inc(own["act"], -1)
                        act.sem_inc(sem["de_pool"][d], 1)
                    for d in range(2):
                        act.wait_ge(sem["t2_act"][d], 1)
                        act.sem_inc(sem["t2_act"][d], -1)
                        act.activation(Ti[:, d], heads(B[d][2]), ACT.Copy).then_inc(own["act"], 1)
                        act.wait_ge(own["act"], 1)
                        act.sem_inc(own["act"], -1)
                        act.sem_inc(sem["inv_pe"][d], 1)
                    for d in range(2):
                        act.wait_ge(sem["wt_act"][d], 1)
                        act.sem_inc(sem["wt_act"][d], -1)
                        act.activation(wtn[:, d], B[d][0][:, 0:2 * P].rearrange("p (a f) -> p a f", f=P),
                                       ACT.Copy, scale=-1.0).then_inc(own["act"], 1)
                        act.wait_ge(own["act"], 1)
                        act.sem_inc(own["act"], -1)
                        act.sem_inc(sem["wtn_pe"][d], 1)
                    for d in range(2):
                        act.wait_ge(sem["o_act"][d], 1)
                        act.sem_inc(sem["o_act"][d], -1)
                        act.activation(both[:, d, :, bass.ds(chunk_of(d, i) * P, P)],
                                       B[d][2][:, 0:2 * P].rearrange("p (a f) -> p a f", f=P), ACT.Copy)\
                            .then_inc(own["act"], 1)
                        act.wait_ge(own["act"], 1)
                        act.sem_inc(own["act"], -1)

            @block.vector
            def _(dve):
                dve.memset(state[:, :, :, :], 0.0).then_inc(own["dve"], 1)
                dve.wait_ge(own["dve"], 1)
                dve.sem_inc(own["dve"], -1)
                for d in range(2):
                    dve.sem_inc(sem["state_pe"][d], 1)
                with dve.Fori(0, NT):
                    for d in range(2):
                        dve.wait_ge(sem["bgt_dve"][d], 1)
                        dve.sem_inc(sem["bgt_dve"][d], -1)
                        dve.tensor_scalar(nb[:, d, :], beta[d], -1.0, None, ALU.mult).then_inc(own["dve"], 1)
                        dve.wait_ge(own["dve"], 1)
                        dve.sem_inc(own["dve"], -1)
                        dve.sem_inc(sem["nb_pool"][d], 1)
                        dve.tensor_copy(gb[:, d], widen(gcol[d], HD)).then_inc(own["dve"], 1)
                        dve.wait_ge(own["dve"], 1)
                        dve.sem_inc(own["dve"], -1)
                        dve.tensor_tensor(gm[:, d], spread(strict[d], H), widen(gcol[d], P), ALU.mult)\
                            .then_inc(own["dve"], 1)
                        dve.wait_ge(own["dve"], 1)
                        dve.sem_inc(own["dve"], -1)
                        dve.sem_inc(sem["gm_pe"][d], 1)
                    for d in range(2):
                        dve.wait_ge(sem["dm_dve"][d], 1)
                        dve.sem_inc(sem["dm_dve"][d], -1)
                        dve.wait_ge(sem["kk_dve"][d], 1)
                        dve.sem_inc(sem["kk_dve"][d], -1)
                        for p in range(2):
                            pair = B[d][p][:, :].rearrange("p (a x f) -> p a x f", a=2, x=2)
                            dve.tensor_tensor(nm[:, d, p::2, :], pair[:, :, 1, :], nbd[:, d, p::2, :],
                                              ALU.mult).then_inc(own["dve"], 1)
                            dve.wait_ge(own["dve"], 1)
                            dve.sem_inc(own["dve"], -1)
                            dve.tensor_tensor(attn[:, d, p::2, :], pair[:, :, 0, :], dm[:, d, p::2, :],
                                              ALU.mult).then_inc(own["dve"], 1)
                            dve.wait_ge(own["dve"], 1)
                            dve.sem_inc(own["dve"], -1)
                        dve.tensor_tensor(S[:, d], nm[:, d], spread(level_ji(d, 0), H), ALU.mult)\
                            .then_inc(own["dve"], 1)
                        dve.wait_ge(own["dve"], 1)
                        dve.sem_inc(own["dve"], -1)
                        dve.tensor_tensor(S[:, d], S[:, d], spread(ident, H), ALU.add).then_inc(own["dve"], 1)
                        dve.wait_ge(own["dve"], 1)
                        dve.sem_inc(own["dve"], -1)
                        dve.sem_inc(sem["s2_pe"][d], 1)
                    for l in range(1, LEVELS):
                        for d in range(2):
                            dve.wait_ge(sem["v_dve"][d], 1)
                            dve.sem_inc(sem["v_dve"][d], -1)
                            dve.tensor_tensor(vm[:, d], heads(B[d][0]), spread(level_ij(d, l), H),
                                              ALU.mult).then_inc(own["dve"], 1)
                            dve.wait_ge(own["dve"], 1)
                            dve.sem_inc(own["dve"], -1)
                            dve.sem_inc(sem["vm_pe"][d], 1)
                        for d in range(2):
                            dve.wait_ge(sem["u_dve"][d], 1)
                            dve.sem_inc(sem["u_dve"][d], -1)
                            dve.tensor_tensor(S[:, d], heads(B[d][1]), S[:, d], ALU.add).then_inc(own["dve"], 1)
                            dve.wait_ge(own["dve"], 1)
                            dve.sem_inc(own["dve"], -1)
                            if l < LEVELS - 1:
                                dve.tensor_tensor(Ti[:, d], heads(B[d][2]), Ti[:, d], ALU.add)\
                                    .then_inc(own["dve"], 1)
                                dve.wait_ge(own["dve"], 1)
                                dve.sem_inc(own["dve"], -1)
                            dve.sem_inc(sem["inv_pe"][d], 1)
                    for d in range(2):
                        dve.wait_ge(sem["vn_dve"][d], 1)
                        dve.sem_inc(sem["vn_dve"][d], -1)
                        dve.tensor_tensor(vn[:, d], B[d][1][:, 0:2 * P].rearrange("p (h f) -> p h f", f=HD),
                                          widen(beta[d], HD), ALU.mult).then_inc(own["dve"], 1)
                        dve.wait_ge(own["dve"], 1)
                        dve.sem_inc(own["dve"], -1)
                        dve.sem_inc(sem["vn_pe"][d], 1)
                    for d in range(2):
                        dve.wait_ge(sem["su_dve"][d], 1)
                        dve.sem_inc(sem["su_dve"][d], -1)
                        dve.tensor_tensor(tmp[:, d], B[d][3][:, 0:2 * P].rearrange("p (a f) -> p a f", f=P),
                                          spread(k.const(C_BLK), 2), ALU.mult).then_inc(own["dve"], 1)
                        dve.wait_ge(own["dve"], 1)
                        dve.sem_inc(own["dve"], -1)
                        for a in range(2):
                            whole = a * P + (P - 1 if d == 0 else 0)
                            dve.scalar_tensor_tensor(state[:, d, a, :], state[:, d, a, :],
                                                     ecum[:, d, whole:whole + 1], tmp[:, d, a, :],
                                                     ALU.mult, ALU.add).then_inc(own["dve"], 1)
                            dve.wait_ge(own["dve"], 1)
                            dve.sem_inc(own["dve"], -1)
                        dve.sem_inc(sem["state_pe"][d], 1)
                for d in range(2):
                    dve.wait_ge(sem["state_pe"][d], 1)
                    dve.sem_inc(sem["state_pe"][d], -1)

            @block.gpsimd
            def _(pool):
                with pool.Fori(0, NT):
                    for d in range(2):
                        pool.wait_ge(sem["de_pool"][d], 1)
                        pool.sem_inc(sem["de_pool"][d], -1)
                        pool.wait_ge(sem["nb_pool"][d], 1)
                        pool.sem_inc(sem["nb_pool"][d], -1)
                        pool.tensor_tensor(nbd[:, d], dec[:, d], spread(after[d], H), ALU.mult)\
                            .then_inc(own["pool"], 1)
                        pool.wait_ge(own["pool"], 1)
                        pool.sem_inc(own["pool"], -1)
                        pool.tensor_tensor(nbd[:, d], nbd[:, d], widen(nb[:, d, :], P), ALU.mult)\
                            .then_inc(own["pool"], 1)
                        pool.wait_ge(own["pool"], 1)
                        pool.sem_inc(own["pool"], -1)
                        pool.tensor_tensor(dm[:, d], dec[:, d], spread(cum[d], H), ALU.mult).then_inc(own["pool"], 1)
                        pool.wait_ge(own["pool"], 1)
                        pool.sem_inc(own["pool"], -1)
                        pool.sem_inc(sem["dm_dve"][d], 1)
                    for d in range(2):
                        pool.tensor_tensor(qd[:, d], stg[:, d, 0:2, :],
                                           ecum[:, d, 0:2 * P].rearrange("p (a f) -> p a f", f=P), ALU.mult)
                        ktok = tok[:, d, 0:2, :].rearrange("p a (h f) -> p (a h) f", f=HD)
                        pool.tensor_tensor(kd[:, d], ktok, widen(ecum[:, d, 2 * P:2 * P + H], HD), ALU.mult)
                        pool.tensor_tensor(ke[:, d], ktok, widen(ecum[:, d, 2 * P + H:2 * P + 2 * H], HD),
                                           ALU.mult).then_inc(own["pool"], 1)
                        pool.wait_ge(own["pool"], 1)
                        pool.sem_inc(own["pool"], -1)
                        pool.sem_inc(sem["ke_pe"][d], 1)

            @block.tensor
            def _(pe):
                with pe.Fori(0, NT):
                    for d in range(2):
                        pe.wait_ge(sem["staged_pe"][d], 1)
                        pe.sem_inc(sem["staged_pe"][d], -1)
                        for x in range(4):
                            pe.transpose(B[d][0][:, x * P:(x + 1) * P], stg[:, d, 2 + x, :], ident)
                        pe.transpose(B[d][1][:, 0:HD], bgs[:, d, :], k.consts[0:HD, C_IDENT:C_IDENT + HD])\
                            .then_inc(sem["tr_act"][d], 1)
                    for d in range(2):
                        pe.wait_ge(sem["gm_pe"][d], 1)
                        pe.sem_inc(sem["gm_pe"][d], -1)
                        for h in range(H):
                            pe.matmul(B[d][2][:, h * P:(h + 1) * P], gm[:, d, h, :], cum[d], start=True, stop=True)
                        for a in range(2):
                            pe.matmul(B[d][3][:, a * P:(a + 1) * P],
                                      gb[:, d, 2 * a:2 * a + 2, :].rearrange("p h f -> p (h f)"), cum[d],
                                      start=True, stop=True)
                        pe.matmul(B[d][3][:, 2 * P:2 * P + H], strict[d], gcol[d], start=True, stop=True)
                        pe.matmul(B[d][3][:, 2 * P + H:2 * P + 2 * H], cum[d], gcol[d], start=True, stop=True)\
                            .then_inc(sem["rc_act"][d], 1)
                    for d in range(2):
                        pe.wait_ge(sem["tok_pe"][d], 1)
                        pe.sem_inc(sem["tok_pe"][d], -1)
                        for h in range(H):
                            rows, a = slice(HD * (h % 2), HD * (h % 2 + 1)), h // 2
                            mm = pe.matmul(B[d][h % 2][:, 2 * a * P:2 * (a + 1) * P], stg[rows, d, 2 + a, :],
                                           stg[rows, d, a:a + 3:2, :], start=True, stop=True)
                        mm.then_inc(sem["kk_dve"][d], 1)
                    for d in range(2):
                        pe.wait_ge(sem["s2_pe"][d], 1)
                        pe.sem_inc(sem["s2_pe"][d], -1)
                        for h in range(H):
                            mm = pe.transpose(B[d][2][:, h * P:(h + 1) * P], S[:, d, h, :], ident)
                        mm.then_inc(sem["t2_act"][d], 1)
                    for l in range(1, LEVELS):
                        for d in range(2):
                            pe.wait_ge(sem["inv_pe"][d], 1)
                            pe.sem_inc(sem["inv_pe"][d], -1)
                            for h in range(H):
                                mm = pe.matmul(B[d][0][:, h * P:(h + 1) * P], nm[:, d, h, :], Ti[:, d, h, :],
                                               start=True, stop=True)
                            mm.then_inc(sem["v_dve"][d], 1)
                        for d in range(2):
                            pe.wait_ge(sem["vm_pe"][d], 1)
                            pe.sem_inc(sem["vm_pe"][d], -1)
                            for h in range(H):
                                mm = pe.matmul(B[d][1][:, h * P:(h + 1) * P], vm[:, d, h, :], S[:, d, h, :],
                                               start=True, stop=True)
                            if l < LEVELS - 1:
                                for h in range(H):
                                    mm = pe.matmul(B[d][2][:, h * P:(h + 1) * P], S[:, d, h, :], vm[:, d, h, :],
                                                   start=True, stop=True)
                            mm.then_inc(sem["u_dve"][d], 1)
                    for d in range(2):
                        pe.wait_ge(sem["inv_pe"][d], 1)
                        pe.sem_inc(sem["inv_pe"][d], -1)
                        pe.wait_ge(sem["ke_pe"][d], 1)
                        pe.sem_inc(sem["ke_pe"][d], -1)
                        for h in range(H):
                            a, p = h // 2, h % 2
                            mm = pe.matmul(B[d][0][HD * p:HD * (p + 1), a * P:(a + 1) * P], ke[:, d, h, :],
                                           S[:, d, h, :], start=True, stop=True)
                        mm.then_inc(sem["wt_act"][d], 1)
                        for h in range(H):
                            pe.matmul(B[d][1][:, h * HD:(h + 1) * HD], S[:, d, h, :],
                                      tok[:, d, 2 + h // 2, HD * (h % 2):HD * (h % 2 + 1)],
                                      start=(h == 0), stop=False, skip_group_check=True)
                    for d in range(2):
                        pe.wait_ge(sem["wtn_pe"][d], 1)
                        pe.sem_inc(sem["wtn_pe"][d], -1)
                        pe.wait_ge(sem["state_pe"][d], 1)
                        pe.sem_inc(sem["state_pe"][d], -1)
                        for a in range(2):
                            mm = pe.matmul(B[d][1][:, a * P:(a + 1) * P], wtn[:, d, a, :], state[:, d, a, :],
                                           start=False, stop=True, skip_group_check=True)
                        mm.then_inc(sem["vn_dve"][d], 1)
                        for a in range(2):
                            pe.matmul(B[d][2][:, a * P:(a + 1) * P], state[:, d, a, :], qd[:, d, a, :],
                                      start=(a == 0), stop=False, skip_group_check=True)
                    for d in range(2):
                        pe.wait_ge(sem["vn_pe"][d], 1)
                        pe.sem_inc(sem["vn_pe"][d], -1)
                        for h in range(H):
                            a, p = h // 2, h % 2
                            mm = pe.matmul(B[d][2][HD * p:HD * (p + 1), a * P:(a + 1) * P], vn[:, d, h, :],
                                           attn[:, d, h, :], start=False, stop=True, skip_group_check=True)
                        mm.then_inc(sem["o_act"][d], 1)
                        for a in range(2):
                            mm = pe.matmul(B[d][3][:, a * P:(a + 1) * P],
                                           kd[:, d, 2 * a:2 * a + 2, :].rearrange("p h f -> p (h f)"),
                                           vn[:, d, 2 * a:2 * a + 2, :].rearrange("p h f -> p (h f)"),
                                           start=True, stop=True)
                        mm.then_inc(sem["su_dve"][d], 1)


def gdn_group(k):
    with k.phase() as st:
        both = k.sb(st, "both", [P, 2, 2, T])
        with ExitStack() as inner:
            qkv = k.sb(inner, "qkv", [P, 6, T])
            bg = k.sb(inner, "bg", [HD, T])
            decay_rows_phase(k, bg)
            jobs = []
            for m in range(6):
                job = Job(T_GDN + m, qkv[:, m, :], taps=m)
                if m < 4:
                    job.width, job.factor = 1.0, (HD ** -0.5 if m < 2 else 1.0)
                jobs.append(job)
            rows_phase(k, jobs)
            gdn_phase(k, qkv, bg, both)
        gate_phase(k, both, 0, T_Z, V_GNORM)


def hgrn_rows_phase(k, q, f, kk, v):
    with k.phase() as st:
        raw = k.sb(st, "raw", [P, 2, T])
        raw_in, raw_free = k.sems(st, "raw_in", 2), k.sems(st, "raw_free", 2)
        sig_dve, own_a, own_v = k.sem(st, "sig_dve"), k.sem(st, "own_a"), k.sem(st, "own_v")
        tiles = [T_HF, T_HF + 1, T_HF + 2, T_HF + 3, T_HQ, T_HQ + 1]
        direct = k.sem(st, "direct")
        with k.nc.Block() as block:
            @block.sync
            def _(sp):
                for j, t in enumerate(tiles):
                    if j >= 2:
                        sp.wait_ge(raw_free[j % 2], 1)
                        sp.sem_inc(raw_free[j % 2], -1)
                    sp.dma_start(raw[:, j % 2, :], k.rows[t]).then_inc(raw_in[j % 2], 16)
                for a in range(2):
                    sp.dma_start(v[:, a, :], k.rows[T_HI + a]).then_inc(direct, 16)
                sp.wait_ge(direct, 32)
                sp.sem_inc(direct, -32)

            @block.scalar
            def _(act):
                for j in range(6):
                    act.wait_ge(raw_in[j % 2], 16)
                    act.sem_inc(raw_in[j % 2], -16)
                    if j < 4:
                        act.activation(f[:, j, :], raw[:, j % 2, :], ACT.Sigmoid)
                        act.activation(kk[:, j, :], raw[:, j % 2, :], ACT.Sigmoid, scale=-1.0).then_inc(own_a, 1)
                        act.wait_ge(own_a, 1)
                        act.sem_inc(own_a, -1)
                        act.sem_inc(raw_free[j % 2], 1)
                        act.sem_inc(sig_dve, 1)
                    else:
                        act.activation(q[:, j - 4, :], raw[:, j % 2, :], ACT.Silu).then_inc(own_a, 1)
                        act.wait_ge(own_a, 1)
                        act.sem_inc(own_a, -1)
                        act.sem_inc(raw_free[j % 2], 1)
                for s in range(2):
                    act.wait_ge(raw_free[s], 1)
                    act.sem_inc(raw_free[s], -1)

            @block.vector
            def _(dve):
                for j in range(4):
                    dve.wait_ge(sig_dve, 1)
                    dve.sem_inc(sig_dve, -1)
                    one_less = k.lb[:, 4 + j:5 + j]
                    dve.tensor_scalar(kk[:, j, :], kk[:, j, :], one_less, None, ALU.mult)
                    last = dve.tensor_scalar(f[:, j, :], f[:, j, :], one_less, k.lb[:, j:j + 1], ALU.mult, ALU.add)
                last.then_inc(own_v, 1)
                dve.wait_ge(own_v, 1)
                dve.sem_inc(own_v, -1)


def hgrn_phase(k, q, f, kk, v, both):
    with k.phase() as st:
        qp = k.sb(st, "qp", [P, 2, 2, P])
        kr = k.sb(st, "kr", [P, 2, 2, P])
        vs = k.sb(st, "vs", [P, 2, 2, P])
        tot = [k.sb(st, f"tot{l}", [P, 2, 2 * (P >> l)]) for l in range(LEVELS + 1)]
        attn = k.sb(st, "attn", [P, 2, H, P])
        krt = k.sb(st, "krt", [P, 2, 2, P])
        vt = k.sb(st, "vt", [P, 2, 2, P])
        state = k.sb(st, "state", [P, 2, 2, P])
        tmp = k.sb(st, "tmp", [P, 2, 2, P])
        B = [[k.banks(st, f"b{d}{b}", 1) for b in range(4)] for d in range(2)]
        names = "staged_pe staged_pool lv_dve read_pool lvl_pe free0_pe free1_pe tr_act attn_pe tok_pe o_act su_dve state_pe".split()
        sem = {n: k.sems(st, n, 2) for n in names}
        own = {e: k.sem(st, f"own_{e}") for e in ("act", "dve", "pool")}
        ident = k.const(C_IDENT)

        def two(b):
            return b[:, 0:2 * P].rearrange("p (a f) -> p a f", f=P)

        with k.nc.Block() as block:
            @block.scalar
            def _(act):
                with act.Fori(0, NT) as i:
                    for d in range(2):
                        col = bass.ds(chunk_of(d, i) * P, P)
                        act.activation(qp[:, d], q[:, :, col], ACT.Copy)
                        act.activation(kr[:, d], kk[:, 2 * d:2 * d + 2, col], ACT.Copy)
                        act.activation(vs[:, d], v[:, :, col], ACT.Copy)
                        act.activation(tot[0][:, d, :].rearrange("p (a f) -> p a f", f=P),
                                       f[:, 2 * d:2 * d + 2, col], ACT.Copy).then_inc(own["act"], 1)
                        act.wait_ge(own["act"], 1)
                        act.sem_inc(own["act"], -1)
                        act.sem_inc(sem["staged_pe"][d], 1)
                    for d in range(2):
                        act.wait_ge(sem["tr_act"][d], 1)
                        act.sem_inc(sem["tr_act"][d], -1)
                        act.activation(krt[:, d], two(B[d][0]), ACT.Copy)
                        act.activation(vt[:, d], two(B[d][1]), ACT.Copy).then_inc(own["act"], 1)
                        act.wait_ge(own["act"], 1)
                        act.sem_inc(own["act"], -1)
                        act.sem_inc(sem["tok_pe"][d], 1)
                    for d in range(2):
                        act.wait_ge(sem["o_act"][d], 1)
                        act.sem_inc(sem["o_act"][d], -1)
                        act.activation(both[:, d, :, bass.ds(chunk_of(d, i) * P, P)], two(B[d][2]),
                                       ACT.Copy).then_inc(own["act"], 1)
                        act.wait_ge(own["act"], 1)
                        act.sem_inc(own["act"], -1)

            @block.vector
            def _(dve):
                dve.memset(attn[:, :, :, :], 0.0)
                dve.memset(state[:, :, :, :], 0.0).then_inc(own["dve"], 1)
                dve.wait_ge(own["dve"], 1)
                dve.sem_inc(own["dve"], -1)
                for d in range(2):
                    dve.sem_inc(sem["state_pe"][d], 1)
                with dve.Fori(0, NT):
                    for l in range(-1, LEVELS):
                        for d in range(2):
                            mask = ident if l < 0 else k.const(C_LVL + (d * LEVELS + l) * P)
                            dve.wait_ge(sem["lv_dve"][d], 1)
                            dve.sem_inc(sem["lv_dve"][d], -1)
                            dve.sem_inc(sem["read_pool"][d], 1)
                            for p in range(2):
                                ins = dve.copy_predicated(attn[:, d, p::2, :], spread(mask, 2).bitcast(U32),
                                                          two(B[d][2 * ((l + 1) % 2) + p]))
                                ins.then_inc(own["dve"], 1)
                                dve.wait_ge(own["dve"], 1)
                                dve.sem_inc(own["dve"], -1)
                            dve.sem_inc(sem["free1_pe" if l % 2 == 0 else "free0_pe"][d], 1)
                    for d in range(2):
                        dve.sem_inc(sem["attn_pe"][d], 1)
                    for d in range(2):
                        dve.wait_ge(sem["su_dve"][d], 1)
                        dve.sem_inc(sem["su_dve"][d], -1)
                        dve.tensor_tensor(tmp[:, d], two(B[d][3]), spread(k.const(C_BLK), 2), ALU.mult)\
                            .then_inc(own["dve"], 1)
                        dve.wait_ge(own["dve"], 1)
                        dve.sem_inc(own["dve"], -1)
                        for a in range(2):
                            dve.scalar_tensor_tensor(state[:, d, a, :], state[:, d, a, :],
                                                     tot[LEVELS][:, d, a:a + 1], tmp[:, d, a, :],
                                                     ALU.mult, ALU.add).then_inc(own["dve"], 1)
                            dve.wait_ge(own["dve"], 1)
                            dve.sem_inc(own["dve"], -1)
                        dve.sem_inc(sem["state_pe"][d], 1)
                for d in range(2):
                    dve.wait_ge(sem["state_pe"][d], 1)
                    dve.sem_inc(sem["state_pe"][d], -1)

            @block.gpsimd
            def _(pool):
                with pool.Fori(0, NT):
                    for d in range(2):
                        pool.wait_ge(sem["read_pool"][d], 1)
                        pool.sem_inc(sem["read_pool"][d], -1)
                        pool.tensor_tensor(qp[:, d].rearrange("p a f -> p (a f)"),
                                           qp[:, d].rearrange("p a f -> p (a f)"), tot[0][:, d, :],
                                           ALU.mult).then_inc(own["pool"], 1)
                        pool.wait_ge(own["pool"], 1)
                        pool.sem_inc(own["pool"], -1)
                        pool.sem_inc(sem["lvl_pe"][d], 1)
                    for l in range(LEVELS):
                        w = 1 << l
                        for d in range(2):
                            late, early = (1, 0) if d == 0 else (0, 1)
                            blocks = tot[l][:, d, :].rearrange("p (n x) -> p n x", x=2)
                            qv = qp[:, d].rearrange("p a f -> p (a f)").rearrange("p (n x w) -> p n x w", x=2, w=w)
                            kv = kr[:, d].rearrange("p a f -> p (a f)").rearrange("p (n x w) -> p n x w", x=2, w=w)
                            pool.wait_ge(sem["read_pool"][d], 1)
                            pool.sem_inc(sem["read_pool"][d], -1)
                            pool.tensor_tensor(qv[:, :, late, :], qv[:, :, late, :], widen(blocks[:, :, early], w),
                                               ALU.mult)
                            pool.tensor_tensor(kv[:, :, early, :], kv[:, :, early, :], widen(blocks[:, :, late], w),
                                               ALU.mult)
                            pool.tensor_tensor(tot[l + 1][:, d, :], blocks[:, :, 0], blocks[:, :, 1],
                                               ALU.mult).then_inc(own["pool"], 1)
                            pool.wait_ge(own["pool"], 1)
                            pool.sem_inc(own["pool"], -1)
                            pool.sem_inc(sem["lvl_pe"][d], 1)

            @block.tensor
            def _(pe):
                with pe.Fori(0, NT):
                    for l in range(-1, LEVELS):
                        for d in range(2):
                            if l < 0:
                                pe.wait_ge(sem["staged_pe"][d], 1)
                                pe.sem_inc(sem["staged_pe"][d], -1)
                            else:
                                pe.wait_ge(sem["lvl_pe"][d], 1)
                                pe.sem_inc(sem["lvl_pe"][d], -1)
                            if l >= 1:
                                pe.wait_ge(sem["free0_pe" if l % 2 else "free1_pe"][d], 1)
                                pe.sem_inc(sem["free0_pe" if l % 2 else "free1_pe"][d], -1)
                            for h in range(H):
                                rows, a = slice(HD * (h % 2), HD * (h % 2 + 1)), h // 2
                                mm = pe.matmul(B[d][2 * ((l + 1) % 2) + h % 2][:, a * P:(a + 1) * P], kr[rows, d, a, :],
                                               qp[rows, d, a, :], start=True, stop=True)
                            mm.then_inc(sem["lv_dve"][d], 1)
                    for d in range(2):
                        pe.wait_ge(sem["lvl_pe"][d], 1)
                        pe.sem_inc(sem["lvl_pe"][d], -1)
                        pe.wait_ge(sem["free0_pe"][d], 1)
                        pe.sem_inc(sem["free0_pe"][d], -1)
                        pe.wait_ge(sem["free1_pe"][d], 1)
                        pe.sem_inc(sem["free1_pe"][d], -1)
                        for a in range(2):
                            pe.transpose(B[d][0][:, a * P:(a + 1) * P], kr[:, d, a, :], ident)
                        for a in range(2):
                            mm = pe.transpose(B[d][1][:, a * P:(a + 1) * P], vs[:, d, a, :], ident)
                        mm.then_inc(sem["tr_act"][d], 1)
                    for d in range(2):
                        pe.wait_ge(sem["state_pe"][d], 1)
                        pe.sem_inc(sem["state_pe"][d], -1)
                        for a in range(2):
                            pe.matmul(B[d][2][:, a * P:(a + 1) * P], state[:, d, a, :], qp[:, d, a, :],
                                      start=(a == 0), stop=False, skip_group_check=True)
                        pe.wait_ge(sem["attn_pe"][d], 1)
                        pe.sem_inc(sem["attn_pe"][d], -1)
                        pe.wait_ge(sem["tok_pe"][d], 1)
                        pe.sem_inc(sem["tok_pe"][d], -1)
                        for h in range(H):
                            a, p = h // 2, h % 2
                            mm = pe.matmul(B[d][2][HD * p:HD * (p + 1), a * P:(a + 1) * P],
                                           vt[:, d, a, HD * p:HD * (p + 1)], attn[:, d, h, :],
                                           start=False, stop=True, skip_group_check=True)
                        mm.then_inc(sem["o_act"][d], 1)
                        for a in range(2):
                            mm = pe.matmul(B[d][3][:, a * P:(a + 1) * P], krt[:, d, a, :], vt[:, d, a, :],
                                           start=True, stop=True)
                        mm.then_inc(sem["su_dve"][d], 1)


def hgrn_group(k):
    with k.phase() as st:
        both = k.sb(st, "both", [P, 2, 2, T])
        with ExitStack() as inner:
            q, v = k.sb(inner, "q", [P, 2, T]), k.sb(inner, "v", [P, 2, T])
            f, kk = k.sb(inner, "f", [P, 4, T]), k.sb(inner, "kk", [P, 4, T])
            hgrn_rows_phase(k, q, f, kk, v)
            hgrn_phase(k, q, f, kk, v, both)
        gate_phase(k, both, 6, T_HG, V_HNORM)


def attention_phase(k, q, kT, vt, oT_tile, window, band, with_ctx):
    with k.phase() as st:
        qs = k.sb(st, "qs", [P, 2, P])
        near = k.sb(st, "near", [P, 3 * P])
        prob = k.sb(st, "prob", [P, 2, T])
        probT = k.sb(st, "probT", [P, 2, NT, P])
        otok = k.sb(st, "otok", [P, 2 * P])
        mx = k.sb(st, "mx", [P, 2, 2])
        tot = k.sb(st, "tot", [P, 2, 2])
        ps = [k.banks(st, f"score{s}", 3) for s in range(2)]
        pt = [k.banks(st, f"turn{s}", 1) for s in range(2)]
        q_pe, q_act = k.sem(st, "q_pe"), k.sem(st, "q_act")
        names = "score_dve mx_act prob_pe sum_dve turn_full turn_free turned_pe out_dve score_free".split()
        sem = {n: k.sems(st, n, 2) for n in names}
        otok_pe = k.sem(st, "otok_pe")
        own = {e: k.sem(st, f"own_{e}") for e in ("act", "dve")}
        scale = HD ** -0.5
        order = ((0, 0), (0, 1), (1, 0), (1, 1))

        def keys_of(chunk, kind):
            if kind == "ctx":
                return [(0, kT[:, SEQ:T])]
            if not window:
                return [(lo, kT[:, lo:lo + w]) for lo, w in SEGS]
            return [(256, kT[:, SEQ:T]), (512, near[:, 0:(3 if kind == "middle" else 2) * P])]

        def span(kind):
            lo = 256 if window and kind != "ctx" else 0
            n = {"ctx": CTX, "all": T, "first": CTX + 2 * P, "last": CTX + 2 * P, "middle": CTX + 3 * P}[kind]
            return lo, n

        def key_chunk(chunk, kind, j):
            if kind == "ctx":
                return SEQ // P + j
            if not window:
                return j
            if j < CTX // P:
                return SEQ // P + j
            return chunk + j - CTX // P - (0 if kind == "first" else 1)

        def batches(kind):
            n = span(kind)[1] // P
            return [(c, min(4, n - c), (c // 4) % 2) for c in range(0, n, 4)]

        def tensor_step(pe, chunk, kind):
            pe.wait_ge(q_pe, 1)
            pe.sem_inc(q_pe, -1)

            def scores(x, g):
                pe.wait_ge(sem["score_free"][g], 1)
                pe.sem_inc(sem["score_free"][g], -1)
                rows = slice(HD * g, HD * (g + 1))
                for col, keys in keys_of(chunk, kind):
                    mm = pe.matmul(ps[g][:, col:col + keys.shape[1]], qs[rows, x, :], keys[rows, :],
                                   start=True, stop=True)
                mm.then_inc(sem["score_dve"][g], 1)

            def values(x, g):
                pe.wait_ge(sem["prob_pe"][g], 1)
                pe.sem_inc(sem["prob_pe"][g], -1)
                for c, n, b in batches(kind):
                    pe.wait_ge(sem["turn_free"][b], 1)
                    pe.sem_inc(sem["turn_free"][b], -1)
                    for j in range(c, c + n):
                        mm = pe.transpose(pt[b][:, (j - c) * P:(j - c + 1) * P], prob[:, g, j * P:(j + 1) * P],
                                          k.const(C_IDENT))
                    mm.then_inc(sem["turn_full"][b], 1)
                for c, n, b in batches(kind):
                    pe.wait_ge(sem["turned_pe"][b], 1)
                    pe.sem_inc(sem["turned_pe"][b], -1)
                    for j in range(c, c + n):
                        mm = pe.matmul(ps[g][:, 0:HD], probT[:, g, j, :],
                                       vt[:, key_chunk(chunk, kind, j), HD * g:HD * (g + 1)],
                                       start=(j == 0), stop=(c + n == span(kind)[1] // P and j == c + n - 1))
                mm.then_inc(sem["out_dve"][g], 1)

            for x in range(2):
                scores(x, 0)
                scores(x, 1)
                values(x, 0)
                values(x, 1)
            pe.wait_ge(otok_pe, 1)
            pe.sem_inc(otok_pe, -1)
            pe.wait_ge(sem["turn_free"][0], 1)
            pe.sem_inc(sem["turn_free"][0], -1)
            for a in range(2):
                mm = pe.transpose(pt[0][:, a * P:(a + 1) * P], otok[:, a * P:(a + 1) * P], k.const(C_IDENT))
            mm.then_inc(sem["turn_full"][0], 1)

        def turn(eng, g, b, kind, copy, name):
            for c, n, bb in batches(kind):
                if bb == b:
                    eng.wait_ge(sem["turn_full"][b], 1)
                    eng.sem_inc(sem["turn_full"][b], -1)
                    copy(probT[:, g, c:c + n, :], pt[b][:, 0:n * P].rearrange("p (c f) -> p c f", f=P))\
                        .then_inc(own[name], 1)
                    eng.wait_ge(own[name], 1)
                    eng.sem_inc(own[name], -1)
                    eng.sem_inc(sem["turn_free"][b], 1)
                    eng.sem_inc(sem["turned_pe"][b], 1)

        def scalar_step(act, chunk, kind):
            act.wait_ge(q_act, 1)
            act.sem_inc(q_act, -1)
            if window and kind != "ctx":
                n_near = (3 if kind == "middle" else 2) * P
                start = (chunk if kind == "first" else chunk - 1) * P
                act.activation(near[:, 0:n_near], kT[:, bass.ds(start, n_near)], ACT.Copy)
            act.activation(qs[:, :, :], q[:, :, bass.ds(chunk * P, P)] if not isinstance(chunk, int)
                           else q[:, :, chunk * P:(chunk + 1) * P], ACT.Copy).then_inc(own["act"], 1)
            act.wait_ge(own["act"], 1)
            act.sem_inc(own["act"], -1)
            act.sem_inc(q_pe, 1)
            lo, n = span(kind)
            for x in range(2):
                for g in range(2):
                    act.wait_ge(sem["mx_act"][g], 1)
                    act.sem_inc(sem["mx_act"][g], -1)
                    if window:
                        act.activation(tot[:, g, 1:2], k.vec(V_SINK + 2 * g + x), ACT.Exp,
                                       bias=mx[:, g, 1:2]).then_inc(own["act"], 1)
                        act.wait_ge(own["act"], 1)
                        act.sem_inc(own["act"], -1)
                    act.activation(prob[:, g, 0:n], ps[g][:, lo:lo + n], ACT.Exp, bias=mx[:, g, 1:2],
                                   scale=scale, accum_out=tot[:, g, 0:1]).then_inc(own["act"], 1)
                    act.wait_ge(own["act"], 1)
                    act.sem_inc(own["act"], -1)
                    act.sem_inc(sem["prob_pe"][g], 1)
                    act.sem_inc(sem["sum_dve"][g], 1)
                for g in range(2):
                    turn(act, g, 0, kind, lambda o, s: act.activation(o, s, ACT.Copy), "act")
            act.wait_ge(sem["turn_full"][0], 1)
            act.sem_inc(sem["turn_full"][0], -1)
            cols = bass.ds(chunk * P, P) if not isinstance(chunk, int) else slice(chunk * P, (chunk + 1) * P)
            act.activation(k.hT[:, oT_tile:oT_tile + 2, cols],
                           pt[0][:, 0:2 * P].rearrange("p (a f) -> p a f", f=P), ACT.Copy).then_inc(own["act"], 1)
            act.wait_ge(own["act"], 1)
            act.sem_inc(own["act"], -1)
            act.sem_inc(sem["turn_free"][0], 1)

        def vector_step(dve, chunk, kind):
            lo, n = span(kind)
            for x in range(2):
                for g in range(2):
                    dve.wait_ge(sem["score_dve"][g], 1)
                    dve.sem_inc(sem["score_dve"][g], -1)
                    if window and kind != "ctx":
                        blocks = {"first": [(512 + P, 2)], "last": [(512, 0)], "middle": [(512, 0), (512 + 2 * P, 2)]}
                        for col, m in blocks[kind]:
                            part = ps[g][:, col:col + P]
                            dve.tensor_tensor(part, part, band[:, m * P:(m + 1) * P], ALU.add)\
                                .then_inc(own["dve"], 1)
                            dve.wait_ge(own["dve"], 1)
                            dve.sem_inc(own["dve"], -1)
                    dve.reduce_max(mx[:, g, 0:1], ps[g][:, lo:lo + n], AX_X).then_inc(own["dve"], 1)
                    dve.wait_ge(own["dve"], 1)
                    dve.sem_inc(own["dve"], -1)
                    if window:
                        dve.tensor_scalar(mx[:, g, 0:1], mx[:, g, 0:1], scale, k.vec(V_SINK + 2 * g + x),
                                          ALU.mult, ALU.max).then_inc(own["dve"], 1)
                        dve.wait_ge(own["dve"], 1)
                        dve.sem_inc(own["dve"], -1)
                        ins = dve.tensor_scalar(mx[:, g, 1:2], mx[:, g, 0:1], -1.0, None, ALU.mult)
                    else:
                        ins = dve.tensor_scalar(mx[:, g, 1:2], mx[:, g, 0:1], -scale, None, ALU.mult)
                    ins.then_inc(own["dve"], 1)
                    dve.wait_ge(own["dve"], 1)
                    dve.sem_inc(own["dve"], -1)
                    dve.sem_inc(sem["mx_act"][g], 1)
                for g in range(2):
                    turn(dve, g, 1, kind, dve.tensor_copy, "dve")
                    h = 2 * g + x
                    dve.wait_ge(sem["sum_dve"][g], 1)
                    dve.sem_inc(sem["sum_dve"][g], -1)
                    if window:
                        dve.tensor_tensor(tot[:, g, 0:1], tot[:, g, 0:1], tot[:, g, 1:2], ALU.add)\
                            .then_inc(own["dve"], 1)
                        dve.wait_ge(own["dve"], 1)
                        dve.sem_inc(own["dve"], -1)
                    dve.reciprocal(tot[:, g, 0:1], tot[:, g, 0:1]).then_inc(own["dve"], 1)
                    dve.wait_ge(own["dve"], 1)
                    dve.sem_inc(own["dve"], -1)
                    dve.wait_ge(sem["out_dve"][g], 1)
                    dve.sem_inc(sem["out_dve"][g], -1)
                    dve.tensor_scalar(otok[:, h * HD:(h + 1) * HD], ps[g][:, 0:HD], tot[:, g, 0:1], None,
                                      ALU.mult).then_inc(own["dve"], 1)
                    dve.wait_ge(own["dve"], 1)
                    dve.sem_inc(own["dve"], -1)
                    dve.sem_inc(sem["score_free"][g], 1)
            dve.sem_inc(otok_pe, 1)
            dve.sem_inc(q_act, 1)

        def schedule(eng, step):
            if window:
                step(eng, 0, "first")
                with eng.Fori(1, SEQ // P - 1) as i:
                    step(eng, i, "middle")
                step(eng, SEQ // P - 1, "last")
            else:
                with eng.Fori(0, SEQ // P) as i:
                    step(eng, i, "all")
            if with_ctx:
                for c in range(SEQ // P, NT):
                    step(eng, c, "ctx")

        with k.nc.Block() as block:
            @block.tensor
            def _(pe):
                schedule(pe, tensor_step)

            @block.scalar
            def _(act):
                act.sem_inc(sem["turn_free"][0], 1)
                schedule(act, scalar_step)
                act.wait_ge(q_act, 1)
                act.sem_inc(q_act, -1)
                act.wait_ge(sem["turn_free"][0], 1)
                act.sem_inc(sem["turn_free"][0], -1)

            @block.vector
            def _(dve):
                dve.sem_inc(q_act, 1)
                dve.sem_inc(sem["turn_free"][1], 1)
                for g in range(2):
                    dve.sem_inc(sem["score_free"][g], 1)
                schedule(dve, vector_step)
                for g in range(2):
                    dve.wait_ge(sem["score_free"][g], 1)
                    dve.sem_inc(sem["score_free"][g], -1)
                dve.wait_ge(sem["turn_free"][1], 1)
                dve.sem_inc(sem["turn_free"][1], -1)


def trig_phase(k, a, trig):
    with k.phase() as st:
        came = k.sem(st, "came")
        with k.nc.Block() as block:
            @block.sync
            def _(sp):
                sp.dma_start(trig[:, :], a["consts"][:, N_MIX:NC]).then_inc(came, 16)
                sp.wait_ge(came, 16)
                sp.sem_inc(came, -16)


def attention_groups(k, a, with_ctx):
    with k.phase() as st:
        table = k.sb(st, "trig", [P, NC - N_MIX])
        band, trig = table[:, 0:3 * P], table[:, 3 * P:]
        trig_phase(k, a, table)
        for window, tq, tk, tv, out in ((False, T_BQ, T_BK, T_BV, 2), (True, T_CQ, T_CK, T_CV, 4)):
            with ExitStack() as inner:
                k.count += 1
                q = k.sb(inner, "q", [P, 2, T])
                kT = k.sb(inner, "kT", [P, T])
                vT = k.sb(inner, "vT", [P, T])
                vt = k.sb(inner, "vt", [P, NT, P])
                jobs = [Job(tq, q[:, 0, :], rope=True), Job(tq + 1, q[:, 1, :], rope=True), Job(tk, kT[:, :], rope=True)]
                if not window:
                    for job, col in zip(jobs, (V_QNORM, V_QNORM, V_KNORM)):
                        job.width, job.factor = HD, k.vec(col)
                jobs.append(Job(tv, vT[:, :], to_tokens=vt))
                rows_phase(k, jobs, trig)
                attention_phase(k, q, kT, vt, out, window, band, with_ctx)


def ffn_up_phase(k, a, layer, half, g, n):
    with k.phase() as st:
        w = k.sb(st, "w_up", [P, 2, KD, P])
        y = k.sb(st, "y", [P, 2, T])
        ps = [k.banks(st, f"ps{s}", 3) for s in range(2)]
        w_full, w_free = k.sems(st, "w_full", 2), k.sems(st, "w_free", 2)
        ps_act, ps_free = k.sems(st, "ps_act", 2), k.sems(st, "ps_free", 2)
        centre_dve, taps_act, gate_pool, y_free = (k.sems(st, s, 2) for s in ("centre_dve", "taps_act", "gate_pool", "y_free"))
        own = {e: k.sem(st, f"own_{e}") for e in ("act", "dve", "pool")}
        parts = conv_parts(n)
        with k.nc.Block() as block:
            @block.sync
            def _(sp):
                with sp.Fori(0, KH) as i:
                    for s in range(2):
                        sp.wait_ge(w_free[s], 1)
                        sp.sem_inc(w_free[s], -1)
                        sp.dma_start(w[:, s], a["w_up"][layer, s * KF + half * KH + i]).then_inc(w_full[s], 16)

            @block.tensor
            def _(pe):
                with pe.Fori(0, KH) as i:
                    for s in range(2):
                        pe.wait_ge(w_full[s], 16)
                        pe.sem_inc(w_full[s], -16)
                        pe.wait_ge(ps_free[s], 1)
                        pe.sem_inc(ps_free[s], -1)
                        products(pe, ps[s], w[:, s], k.hT, KD, n).then_inc(ps_act[s], 1)

            @block.scalar
            def _(act):
                for s in range(2):
                    act.sem_inc(w_free[s], 1)
                with act.Fori(0, KH) as i:
                    for s in range(2):
                        tile = s * KF + half * KH + i
                        act.wait_ge(ps_act[s], 1)
                        act.sem_inc(ps_act[s], -1)
                        act.sem_inc(w_free[s], 1)
                        act.wait_ge(y_free[s], 1)
                        act.sem_inc(y_free[s], -1)
                        act.activation(k.taps[:, s, 0:4],
                                       k.vecs[:, bass.ds(V_FCONV + tile, 4, 2 * KF)], ACT.Copy)\
                            .then_inc(own["act"], 1)
                        act.wait_ge(own["act"], 1)
                        act.sem_inc(own["act"], -1)
                        act.activation(y[:, s, 0:n], ps[s][:, 0:n], ACT.Identity,
                                       scale=k.taps[:, s, 1:2], bias=k.taps[:, s, 3:4]).then_inc(own["act"], 1)
                        act.wait_ge(own["act"], 1)
                        act.sem_inc(own["act"], -1)
                        act.sem_inc(centre_dve[s], 1)
                    act.wait_ge(taps_act[0], 1)
                    act.sem_inc(taps_act[0], -1)
                    act.activation(y[:, 0, 0:n], y[:, 0, 0:n], ACT.Silu).then_inc(own["act"], 1)
                    act.wait_ge(own["act"], 1)
                    act.sem_inc(own["act"], -1)
                    act.sem_inc(gate_pool[0], 1)
                for s in range(2):
                    act.wait_ge(w_free[s], 1)
                    act.sem_inc(w_free[s], -1)

            @block.vector
            def _(dve):
                for s in range(2):
                    dve.sem_inc(ps_free[s], 1)
                with dve.Fori(0, KH) as i:
                    for s in range(2):
                        dve.wait_ge(centre_dve[s], 1)
                        dve.sem_inc(centre_dve[s], -1)
                        for lo, hi in parts:
                            dve.scalar_tensor_tensor(y[:, s, lo + 1:hi], ps[s][:, lo:hi - 1],
                                                     k.taps[:, s, 0:1], y[:, s, lo + 1:hi],
                                                     ALU.mult, ALU.add).then_inc(own["dve"], 1)
                            dve.wait_ge(own["dve"], 1)
                            dve.sem_inc(own["dve"], -1)
                            dve.scalar_tensor_tensor(y[:, s, lo:hi - 1], ps[s][:, lo + 1:hi],
                                                     k.taps[:, s, 2:3], y[:, s, lo:hi - 1],
                                                     ALU.mult, ALU.add).then_inc(own["dve"], 1)
                            dve.wait_ge(own["dve"], 1)
                            dve.sem_inc(own["dve"], -1)
                        dve.sem_inc(ps_free[s], 1)
                        dve.sem_inc(taps_act[0] if s == 0 else gate_pool[1], 1)
                for s in range(2):
                    dve.wait_ge(ps_free[s], 1)
                    dve.sem_inc(ps_free[s], -1)

            @block.gpsimd
            def _(pool):
                for s in range(2):
                    pool.sem_inc(y_free[s], 1)
                with pool.Fori(0, KH) as i:
                    pool.wait_ge(gate_pool[0], 1)
                    pool.sem_inc(gate_pool[0], -1)
                    pool.wait_ge(gate_pool[1], 1)
                    pool.sem_inc(gate_pool[1], -1)
                    pool.tensor_tensor(g[:, i, 0:n], y[:, 0, 0:n], y[:, 1, 0:n], ALU.mult).then_inc(own["pool"], 1)
                    pool.wait_ge(own["pool"], 1)
                    pool.sem_inc(own["pool"], -1)
                    pool.sem_inc(y_free[0], 1)
                    pool.sem_inc(y_free[1], 1)
                for s in range(2):
                    pool.wait_ge(y_free[s], 1)
                    pool.sem_inc(y_free[s], -1)


def ffn(k, a, layer, n):
    with k.phase() as st:
        f = k.sb(st, "f", [P, KD, T])
        with ExitStack() as inner:
            g = k.sb(inner, "g", [P, KH, T])
            for half in range(2):
                ffn_up_phase(k, a, layer, half, g, n)
                matmul_into_phase(k, a["w_down"][layer, half], KH, g, f, n, add=half == 1)
        residual_phase(k, f, n, 5)


def store_phase(k, a):
    with k.phase() as st:
        done = k.sem(st, "done")
        with k.nc.Block() as block:
            @block.sync
            def _(sp):
                sp.dma_start(a["out"], k.xT[:, :, 0:SEQ]).then_inc(done, 16)
                sp.wait_ge(done, 16)
                sp.sem_inc(done, -16)


def build(nc, a):
    k = Chip(nc)
    with ExitStack() as st:
        k.rows = nc.dram_tensor("rows", (N_IN, P, T), F32).ap()
        k.consts = k.sb(st, "consts", [P, N_MIX])
        k.vecs = k.sb(st, "vecs", [P, NV])
        k.mods = k.sb(st, "mods", [P, N_MOD * KD, 2])
        k.cact = k.sb(st, "cact", [P, KD, 2])
        k.lb = k.sb(st, "lb", [P, 8])
        k.expa = k.sb(st, "expa", [P, 1])
        k.taps = k.sb(st, "taps", [P, 2, 4])
        k.xT = k.sb(st, "xT", [P, KD, T])
        k.hT = k.sb(st, "hT", [P, KD, T])
        load_phase(k, a)
        for layer in range(DEPTH):
            with_ctx = layer < DEPTH - 1
            n = T if with_ctx else SEQ
            modulation_phase(k, a, layer)
            norm_phase(k, T, 0, 1)
            input_projection_phase(k, a, layer)
            gdn_group(k)
            attention_groups(k, a, with_ctx)
            hgrn_group(k)
            with ExitStack() as inner:
                k.count += 1
                y = k.sb(inner, "mixed", [P, KD, T])
                matmul_into_phase(k, a["w_out"][layer], KD, k.hT, y, n, add=False)
                residual_phase(k, y, n, 2)
            norm_phase(k, n, 3, 4)
            ffn(k, a, layer, n)
        store_phase(k, a)


def layouts(x, c, ctx, c_ctx, ada_w, ada_b, norm_pre_mix, norm_post_mix, norm_pre_ffn, norm_post_ffn,
            w_in, w_out, gdn_conv_w, gdn_a_log, gdn_dt_bias, gdn_norm, attn_q_norm, attn_k_norm,
            swa_sink, hgrn_lb_raw, hgrn_norm, ffn_w_up, ffn_conv_w, ffn_conv_b, ffn_w_down):
    def cols(v):
        return np.asarray(v).reshape(-1, P).T

    def tiles(w, n_k):
        return np.asarray(w).reshape(n_k, P, -1, P).transpose(2, 1, 0, 3)

    out = {"xT": np.concatenate([np.asarray(x)[0], np.asarray(ctx)[0]]).T.reshape(KD, P, T).transpose(1, 0, 2)}
    out["cond"] = np.stack([np.asarray(c)[0], np.asarray(c_ctx)]).reshape(2, KD, P).transpose(2, 1, 0)
    out["ada_w"] = np.asarray(ada_w).reshape(DEPTH, KD, P, -1, 512).transpose(0, 3, 2, 1, 4)
    heads = [0, 2, 1, 3]
    w_in, vecs, ins = np.asarray(w_in), [], []
    for l in range(DEPTH):
        w = w_in[l]
        qkv_z, beta, a, rest = w[:, :1024], w[:, 1024:1032], w[:, 1032:1040], w[:, 1040:].copy()
        for at in (0, 512):
            q = rest[:, at:at + 256].reshape(-1, H, HD)[:, heads]
            rest[:, at:at + 256] = q.reshape(-1, 256)
        last = np.zeros((D_MODEL, P), w.dtype)
        last[:, BETA_ROW:BETA_ROW + 8] = beta
        last[:, G_ROW:G_ROW + 8] = a
        ins.append(tiles(np.concatenate([qkv_z, rest, last], 1), KD))
        v = np.zeros((P, NV), np.float32)
        v[:, V_ADAB:V_ADAB + 48] = cols(ada_b[l])
        for col, vec in ((V_PRE_MIX, norm_pre_mix), (V_POST_MIX, norm_post_mix), (V_PRE_FFN, norm_pre_ffn),
                         (V_POST_FFN, norm_post_ffn)):
            v[:, col:col + KD] = cols(vec[l])
        v[:, V_GCONV:V_GCONV + 18] = cols(gdn_conv_w[l])
        v[:, V_FCONV:V_FCONV + 6 * KF] = cols(ffn_conv_w[l])
        v[:, V_FBIAS:V_FBIAS + 2 * KF] = cols(ffn_conv_b[l])
        for col, vec in ((V_GNORM, gdn_norm), (V_QNORM, attn_q_norm), (V_KNORM, attn_k_norm), (V_HNORM, hgrn_norm)):
            v[:HD, col] = vec[l]
            v[HD:, col] = vec[l]
        v[G_ROW:G_ROW + 8, V_ALOG] = np.asarray(gdn_a_log[l]).reshape(-1)
        v[G_ROW:G_ROW + 8, V_DTB] = np.asarray(gdn_dt_bias[l]).reshape(-1)
        v[:, V_LB:V_LB + 8] = cols(hgrn_lb_raw)
        v[:, V_SINK:V_SINK + H] = np.asarray(swa_sink[l])[None, :]
        vecs.append(v)
    out["w_in"], out["vecs"] = np.stack(ins), np.stack(vecs)
    out["w_out"] = np.stack([tiles(w, KD) for w in np.asarray(w_out)])
    out["w_up"] = np.stack([tiles(w, KD) for w in np.asarray(ffn_w_up)])
    out["w_down"] = np.stack([np.stack([tiles(w[h * KH * P:(h + 1) * KH * P], KH) for h in range(2)])
                              for w in np.asarray(ffn_w_down)])
    out["consts"] = constants()
    return {n: np.ascontiguousarray(v) for n, v in out.items()}


def kernel(**inputs):
    import concourse.bacc as bacc
    from concourse.bass_utils import run_bass_kernel_spmd

    nc = bacc.Bacc("TRN2", target_bir_lowering=False, num_devices=1)
    arrays = {f"in_{n}_dram": v for n, v in layouts(**inputs).items()}
    aps = {n[3:-5]: nc.dram_tensor(n, v.shape, mybir.dt.from_np(v.dtype), kind="ExternalInput").ap()
           for n, v in arrays.items()}
    aps["out"] = nc.dram_tensor("out_0_dram", (P, KD, SEQ), F32, kind="ExternalOutput").ap()
    build(nc, aps)
    r = run_bass_kernel_spmd(nc, [arrays], core_ids=[0])
    got = r.results[0]["out_0_dram"]
    return got.transpose(1, 0, 2).reshape(D_MODEL, SEQ).T.reshape(1, SEQ, D_MODEL)
```

```python
from contextlib import ExitStack

import numpy as np

import concourse.bass as bass
from concourse import mybir

ALU = mybir.AluOpType
ACT = mybir.ActivationFunctionType
F32 = mybir.dt.float32
F32R = mybir.dt.float32r
U32 = mybir.dt.uint32
AX_X = mybir.AxisListType.X

P = 128
D_MODEL = 1024
SEQ = 1024
CTX = 256
T = SEQ + CTX
DEPTH = 2
HD = 64
H = 4
KD = D_MODEL // P
NT = T // P
D_FF = 2816
KF = D_FF // P
FG = 2
N_FG = KF // FG
N_MOD = 6
EPS = 1e-6
NEG = -1e30
LEVELS = 7

T_GDN, T_Z, T_BQ, T_BK, T_BV, T_CQ, T_CK, T_CV, T_HQ, T_HF, T_HI, T_HG, T_BETA = (
    0, 6, 8, 10, 11, 12, 14, 15, 16, 18, 22, 24, 26)
N_IN = 27
BETA_ROW, G_ROW = 0, 32

V_ADAB = 0
V_PRE_MIX = V_ADAB + N_MOD * KD
V_POST_MIX = V_PRE_MIX + KD
V_PRE_FFN = V_POST_MIX + KD
V_POST_FFN = V_PRE_FFN + KD
V_GCONV = V_POST_FFN + KD
V_FCONV = V_GCONV + 18
V_FBIAS = V_FCONV + 3 * 2 * KF
V_GNORM = V_FBIAS + 2 * KF
V_QNORM = V_GNORM + 1
V_KNORM = V_QNORM + 1
V_HNORM = V_KNORM + 1
V_ALOG = V_HNORM + 1
V_DTB = V_ALOG + 1
V_LB = V_DTB + 1
V_SINK = V_LB + DEPTH * 4
NV = V_SINK + H

C_IDENT = 0
C_ONES = C_IDENT + P
C_BLK = C_ONES + P
C_ROT = C_BLK + P
C_CUM = C_ROT + P
C_STR = C_CUM + 2 * P
C_LVL = C_STR + 2 * P
C_BAND = C_LVL + 2 * LEVELS * P
C_COS = C_BAND + 3 * P
C_SIN = C_COS + SEQ
NC = C_SIN + SEQ
N_BASE = C_ROT
N_MIX = C_BAND
SEGS = ((0, 512), (512, 512), (1024, 256))


def constants():
    i = np.arange(P)
    c = np.zeros((P, NC), np.float32)
    c[:, C_IDENT:C_IDENT + P] = np.eye(P)
    c[:, C_ONES:C_ONES + P] = 1
    c[:, C_BLK:C_BLK + P] = (i[:, None] // HD) == (i[None, :] // HD)
    for m in range(0, P, 2):
        c[m + 1, C_ROT + m] = -1
        c[m, C_ROT + m + 1] = 1
    a, b = i[:, None], i[None, :]
    c[:, C_CUM:C_CUM + P] = a <= b
    c[:, C_CUM + P:C_CUM + 2 * P] = a >= b
    c[:, C_STR:C_STR + P] = a > b
    c[:, C_STR + P:C_STR + 2 * P] = a < b
    for l in range(LEVELS):
        x, y = a >> l, b >> l
        even_odd = (x % 2 == 0) & (y == x + 1)
        c[:, C_LVL + l * P:C_LVL + (l + 1) * P] = even_odd
        c[:, C_LVL + (LEVELS + l) * P:C_LVL + (LEVELS + l + 1) * P] = even_odd.T
    c[:, C_BAND:C_BAND + P] = np.where(b >= a, 0, NEG)
    c[:, C_BAND + 2 * P:C_BAND + 3 * P] = np.where(b <= a, 0, NEG)
    n_freq = HD // 4
    inv = (1.0 / (np.float32(10000.0) ** (np.arange(n_freq, dtype=np.float32) / np.float32(n_freq)))).astype(np.float32)
    pos = np.arange(SEQ)
    ang = np.concatenate([(pos // 64).astype(np.float32)[:, None] * inv,
                          (pos % 64).astype(np.float32)[:, None] * inv], axis=-1)
    pair = (i % HD) // 2
    c[:, C_COS:C_COS + SEQ] = np.cos(ang.astype(np.float64))[:, pair].T
    c[:, C_SIN:C_SIN + SEQ] = np.sin(ang.astype(np.float64))[:, pair].T
    return c



class Chip:

    def __init__(self, nc):
        self.nc = nc
        self.count = 0

    def phase(self):
        self.count += 1
        return ExitStack()

    def sb(self, stack, name, shape, dt=F32):
        return stack.enter_context(self.nc.sbuf_tensor(f"{name}_{self.count}", shape, dt))

    def twin(self, stack, name, shape):
        whole = self.sb(stack, name, shape)
        offset = self.nc.sbuf_base - 4 * int(np.prod(shape[1:]))
        return whole, self.nc.alloc_sbuf_tensor_at(f"{name}_rest_{self.count}", shape, F32R, offset=offset)

    def banks(self, stack, name, n):
        return stack.enter_context(self.nc.psum_tensor(f"{name}_{self.count}", [P, n * 512], F32))

    def sem(self, stack, name):
        return stack.enter_context(self.nc.semaphore(f"{name}_{self.count}"))

    def sems(self, stack, name, n):
        return [self.sem(stack, f"{name}{i}") for i in range(n)]

    def const(self, col, n=P):
        if col < N_BASE:
            return self.consts[:, col:col + n]
        return self.mix[:, col - N_BASE:col - N_BASE + n]

    def vec(self, col, n=1):
        return self.vecs[:, col:col + n]


def spread(ap, n):
    return ap.unsqueeze(1).to_broadcast([ap.shape[0], n, ap.shape[1]])


def widen(ap, n):
    return ap.unsqueeze(2).to_broadcast([ap.shape[0], ap.shape[1], n])


def load_phase(k, a):
    with k.phase() as st:
        loaded, own = k.sem(st, "loaded"), k.sem(st, "own")
        with k.nc.Block() as block:
            @block.sync
            def _(sp):
                sp.dma_start(k.consts[:, :], a["consts"][:, 0:N_BASE]).then_inc(loaded, 16)
                sp.dma_start(k.cact[:, :, :], a["cond"]).then_inc(loaded, 16)
                sp.dma_start(k.xT[:, :, :], a["xT"]).then_inc(loaded, 16)

            @block.scalar
            def _(act):
                act.wait_ge(loaded, 48)
                act.sem_inc(loaded, -48)
                act.activation(k.cact[:, :, :], k.cact[:, :, :], ACT.Silu).then_inc(own, 1)
                act.wait_ge(own, 1)
                act.sem_inc(own, -1)


def modulation_phase(k, a, layer):
    n_it = N_MOD * D_MODEL // 512
    with k.phase() as st:
        w = k.sb(st, "ada_w", [P, 2, KD, 512])
        ps = [k.banks(st, f"mod_ps{s}", 1) for s in range(2)]
        vec_in = k.sem(st, "vec_in")
        w_full, w_free = k.sems(st, "w_full", 2), k.sems(st, "w_free", 2)
        ps_full, ps_free = k.sems(st, "ps_full", 2), k.sems(st, "ps_free", 2)
        own = k.sem(st, "own")
        with k.nc.Block() as block:
            @block.sync
            def _(sp):
                sp.dma_start(k.vecs[:, :], a["vecs"][layer]).then_inc(vec_in, 16)
                with sp.Fori(0, n_it // 2) as i:
                    for s in range(2):
                        sp.wait_ge(w_free[s], 1)
                        sp.sem_inc(w_free[s], -1)
                        sp.dma_start(w[:, s], a["ada_w"][layer, i * 2 + s]).then_inc(w_full[s], 16)

            @block.tensor
            def _(pe):
                with pe.Fori(0, n_it // 2) as i:
                    for s in range(2):
                        pe.wait_ge(w_full[s], 16)
                        pe.sem_inc(w_full[s], -16)
                        pe.wait_ge(ps_free[s], 1)
                        pe.sem_inc(ps_free[s], -1)
                        for q in range(4):
                            for t in range(KD):
                                mm = pe.matmul(ps[s][:, 2 * q:2 * q + 2], w[:, s, t, q * P:(q + 1) * P],
                                               k.cact[:, t, :], start=(t == 0), stop=(t == KD - 1))
                        mm.then_inc(ps_full[s], 1)

            @block.vector
            def _(dve):
                for s in range(2):
                    dve.sem_inc(w_free[s], 1)
                    dve.sem_inc(ps_free[s], 1)
                dve.wait_ge(vec_in, 16)
                dve.sem_inc(vec_in, -16)
                with dve.Fori(0, n_it // 2) as i:
                    for s in range(2):
                        dve.wait_ge(ps_full[s], 1)
                        dve.sem_inc(ps_full[s], -1)
                        dve.sem_inc(w_free[s], 1)
                        cols = bass.ds((i * 2 + s) * 4, 4)
                        dve.tensor_tensor(
                            k.mods[:, cols, :], ps[s][:, 0:8].rearrange("p (n s) -> p n s", s=2),
                            widen(k.vecs[:, bass.ds(V_ADAB + (i * 2 + s) * 4, 4)], 2), ALU.add).then_inc(own, 1)
                        dve.wait_ge(own, 1)
                        dve.sem_inc(own, -1)
                        dve.sem_inc(ps_free[s], 1)
                for s in range(2):
                    dve.wait_ge(ps_free[s], 1)
                    dve.sem_inc(ps_free[s], -1)
                for m, col in ((1, V_PRE_MIX), (4, V_PRE_FFN)):
                    part = k.mods[:, m * KD:(m + 1) * KD, :]
                    dve.tensor_scalar(part, part, 1.0, None, ALU.add).then_inc(own, 1)
                    dve.wait_ge(own, 1)
                    dve.sem_inc(own, -1)
                    dve.tensor_tensor(part, part, widen(k.vec(col, KD), 2), ALU.mult).then_inc(own, 1)
                    dve.wait_ge(own, 1)
                    dve.sem_inc(own, -1)
                for m, col in ((2, V_POST_MIX), (5, V_POST_FFN)):
                    part = k.mods[:, m * KD:(m + 1) * KD, :]
                    dve.tensor_tensor(part, part, widen(k.vec(col, KD), 2), ALU.mult).then_inc(own, 1)
                    dve.wait_ge(own, 1)
                    dve.sem_inc(own, -1)
                lb0, lb1 = k.vec(V_LB, 4), k.vec(V_LB + 4, 4)
                if layer == 0:
                    dve.memset(k.lb[:, 0:4], 0.0).then_inc(own, 1)
                    dve.wait_ge(own, 1)
                    dve.sem_inc(own, -1)
                    dve.memset(k.lb[:, 4:8], 1.0).then_inc(own, 1)
                    dve.wait_ge(own, 1)
                    dve.sem_inc(own, -1)
                else:
                    dve.tensor_tensor(k.lb[:, 0:4], lb1, lb0, ALU.subtract).then_inc(own, 1)
                    dve.wait_ge(own, 1)
                    dve.sem_inc(own, -1)
                for s in range(2):
                    dve.wait_ge(w_free[s], 1)
                    dve.sem_inc(w_free[s], -1)

        own_a, go, back = k.sem(st, "own_a"), k.sem(st, "go"), k.sem(st, "back")
        with k.nc.Block() as block:
            @block.scalar
            def _(act):
                if layer:
                    act.activation(k.lb[:, 4:8], k.lb[:, 0:4], ACT.Sigmoid, scale=-1.0)
                    act.activation(k.lb[:, 0:4], k.lb[:, 0:4], ACT.Sigmoid).then_inc(own_a, 1)
                    act.wait_ge(own_a, 1)
                    act.sem_inc(own_a, -1)
                act.activation(k.sink[:, :], k.vec(V_SINK, H), ACT.Copy, scale=float(HD ** 0.5))
                act.activation(k.expa[:, :], k.vec(V_ALOG), ACT.Exp).then_inc(own_a, 1)
                act.wait_ge(own_a, 1)
                act.sem_inc(own_a, -1)
                act.activation(k.expa[:, :], k.expa[:, :], ACT.Copy, scale=-1.0).then_inc(own_a, 1)
                act.wait_ge(own_a, 1)
                act.sem_inc(own_a, -1)


def token_parts(n):
    return [(0, SEQ, 0)] + ([(SEQ, n, 1)] if n > SEQ else [])


def row_factor(k, st, dve, act_sems, ps, r, n, own, width, eps=EPS):
    dve.tensor_scalar(r[:, 0:n], ps[:, 0:n], 1.0 / width, eps, ALU.mult, ALU.add).then_inc(own, 1)
    dve.wait_ge(own, 1)
    dve.sem_inc(own, -1)
    dve.reciprocal(r[:, 0:n], r[:, 0:n]).then_inc(own, 1)
    dve.wait_ge(own, 1)
    dve.sem_inc(own, -1)
    dve.sem_inc(act_sems, 1)


def norm_phase(k, n, m_shift, m_scale, spill=None):
    with k.phase() as st:
        sq = k.sb(st, "sq", [P, 2, T])
        acc = k.sb(st, "acc", [P, T])
        r = k.sb(st, "r", [P, T])
        ps = k.banks(st, "ps", 3)
        sq_full, sq_free = k.sems(st, "sq_full", 2), k.sems(st, "sq_free", 2)
        acc_pe, sum_dve, inv_act, root_dve = (k.sem(st, s) for s in ("acc_pe", "sum_dve", "inv_act", "root_dve"))
        scaled, hi_dve, hi_pool = k.sem(st, "scaled"), k.sem(st, "hi_dve"), k.sem(st, "hi_pool")
        own_a, own_v, own_p, spilled = (k.sem(st, s) for s in ("own_a", "own_v", "own_p", "spilled"))
        whole = k.h

        def rest(eng, t, own):
            eng.tensor_tensor(k.lo[:, t, 0:n], whole[:, t, 0:n], k.hi[:, t, 0:n].bitcast(F32),
                              ALU.subtract).then_inc(own, 1)
            eng.wait_ge(own, 1)
            eng.sem_inc(own, -1)

        with k.nc.Block() as block:
            @block.scalar
            def _(act):
                for t in range(KD):
                    if t >= 2:
                        act.wait_ge(sq_free[t % 2], 1)
                        act.sem_inc(sq_free[t % 2], -1)
                    act.activation(sq[:, t % 2, 0:n], k.xT[:, t, 0:n], ACT.Square).then_inc(sq_full[t % 2], 1)
                act.wait_ge(inv_act, 1)
                act.sem_inc(inv_act, -1)
                act.activation(r[:, 0:n], r[:, 0:n], ACT.Sqrt).then_inc(own_a, 1)
                act.wait_ge(own_a, 1)
                act.sem_inc(own_a, -1)
                act.sem_inc(root_dve, 1)
                for t in range(KD):
                    act.wait_ge(scaled, 1)
                    act.sem_inc(scaled, -1)
                    for lo, hi, s in token_parts(n):
                        shift = k.mods[:, m_shift * KD + t, s:s + 1]
                        act.activation(k.hi[:, t, lo:hi], whole[:, t, lo:hi], ACT.Identity, bias=shift)
                        last = act.activation(whole[:, t, lo:hi], whole[:, t, lo:hi], ACT.Identity, bias=shift)
                    last.then_inc(own_a, 1)
                    act.wait_ge(own_a, 1)
                    act.sem_inc(own_a, -1)
                    act.sem_inc(hi_dve if t % 2 else hi_pool, 1)

            @block.vector
            def _(dve):
                for t in range(KD):
                    dve.wait_ge(sq_full[t % 2], 1)
                    dve.sem_inc(sq_full[t % 2], -1)
                    if t == 0:
                        ins = dve.tensor_copy(acc[:, 0:n], sq[:, 0, 0:n])
                    else:
                        ins = dve.tensor_tensor(acc[:, 0:n], acc[:, 0:n], sq[:, t % 2, 0:n], ALU.add)
                    if t < KD - 2:
                        ins.then_inc(own_v, 1)
                        dve.wait_ge(own_v, 1)
                        dve.sem_inc(own_v, -1)
                        dve.sem_inc(sq_free[t % 2], 1)
                    elif t < KD - 1:
                        ins.then_inc(own_v, 1)
                        dve.wait_ge(own_v, 1)
                        dve.sem_inc(own_v, -1)
                    else:
                        ins.then_inc(own_v, 1)
                        dve.wait_ge(own_v, 1)
                        dve.sem_inc(own_v, -1)
                        dve.sem_inc(acc_pe, 1)
                dve.wait_ge(sum_dve, 1)
                dve.sem_inc(sum_dve, -1)
                row_factor(k, st, dve, inv_act, ps, r, n, own_v, D_MODEL)
                dve.wait_ge(root_dve, 1)
                dve.sem_inc(root_dve, -1)
                for t in range(KD):
                    for lo, hi, s in token_parts(n):
                        ins = dve.scalar_tensor_tensor(whole[:, t, lo:hi], k.xT[:, t, lo:hi],
                                                       k.mods[:, m_scale * KD + t, s:s + 1], r[:, lo:hi],
                                                       ALU.mult, ALU.mult)
                        if hi < n:
                            ins.then_inc(own_v, 1)
                            dve.wait_ge(own_v, 1)
                            dve.sem_inc(own_v, -1)
                    ins.then_inc(scaled, 1)
                for t in range(1, KD, 2):
                    dve.wait_ge(hi_dve, 1)
                    dve.sem_inc(hi_dve, -1)
                    rest(dve, t, own_v)

            @block.gpsimd
            def _(pool):
                for t in range(0, KD, 2):
                    pool.wait_ge(hi_pool, 1)
                    pool.sem_inc(hi_pool, -1)
                    rest(pool, t, own_p)

            @block.tensor
            def _(pe):
                pe.wait_ge(acc_pe, 1)
                pe.sem_inc(acc_pe, -1)
                for lo, w in SEGS:
                    if lo < n:
                        mm = pe.matmul(ps[:, lo:lo + w], k.const(C_ONES), acc[:, lo:lo + w], start=True, stop=True)
                mm.then_inc(sum_dve, 1)

            if spill is not None:
                @block.sync
                def _(sp):
                    sp.dma_start(spill, k.xT[:, :, :]).then_inc(spilled, 16)
                    sp.wait_ge(spilled, 16)
                    sp.sem_inc(spilled, -16)


def products(pe, ps, w, rhs, n_k, n):
    for t in range(n_k):
        for lo, width in SEGS:
            if lo < n:
                mm = pe.matmul(ps[:, lo:lo + width], w[:, t, :], rhs[:, t, lo:lo + width],
                               start=(t == 0), stop=(t == n_k - 1))
    return mm


def split_products(pe, ps, w, rhs, n_k, n):
    for t in range(n_k):
        for i, (a, b) in enumerate(((0, 0), (1, 0), (0, 1))):
            for lo, width in SEGS:
                if lo < n:
                    mm = pe.matmul(ps[:, lo:lo + width], w[a][:, t, :], rhs[b][:, t, lo:lo + width],
                                   start=(t == 0 and i == 0), stop=(t == n_k - 1 and i == 2))
    return mm


def input_projection_phase(k, a, layer):
    with k.phase() as st:
        w_hi = k.sb(st, "w_hi", [P, 2, KD, P], F32R)
        raw, w_lo = k.twin(st, "w_raw", [P, 2, KD, P])
        out = k.sb(st, "rows", [P, 2, T])
        ps = [k.banks(st, f"ps{s}", 3) for s in range(2)]
        w_in, w_free, hi_dve, w_pe = (k.sems(st, s, 2) for s in ("w_in", "w_free", "hi_dve", "w_pe"))
        ps_full, ps_free = k.sems(st, "ps_full", 2), k.sems(st, "ps_free", 2)
        out_free = k.sems(st, "out_free", 2)
        own_a, own_v, mix_in = k.sem(st, "own_a"), k.sem(st, "own_v"), k.sem(st, "mix_in")
        pairs = N_IN // 2

        def load(sp, s, tile):
            sp.wait_ge(w_free[s], 1)
            sp.sem_inc(w_free[s], -1)
            sp.dma_start(raw[:, s], a["w_in"][layer, tile]).then_inc(w_in[s], 16)

        def round_weights(act, s):
            act.wait_ge(w_in[s], 16)
            act.sem_inc(w_in[s], -16)
            act.activation(w_hi[:, s], raw[:, s], ACT.Copy).then_inc(own_a, 1)
            act.wait_ge(own_a, 1)
            act.sem_inc(own_a, -1)
            act.sem_inc(hi_dve[s], 1)

        def rest_of_weights(dve, s):
            dve.wait_ge(hi_dve[s], 1)
            dve.sem_inc(hi_dve[s], -1)
            dve.tensor_tensor(w_lo[:, s], raw[:, s], w_hi[:, s].bitcast(F32), ALU.subtract).then_inc(own_v, 1)
            dve.wait_ge(own_v, 1)
            dve.sem_inc(own_v, -1)
            dve.sem_inc(w_pe[s], 1)

        def multiply(pe, s):
            pe.wait_ge(w_pe[s], 1)
            pe.sem_inc(w_pe[s], -1)
            pe.wait_ge(ps_free[s], 1)
            pe.sem_inc(ps_free[s], -1)
            split_products(pe, ps[s], (w_hi[:, s], w_lo[:, s]), (k.hi, k.lo), KD, T).then_inc(ps_full[s], 1)

        def collect(act, s, tile, more=True):
            act.wait_ge(ps_full[s], 1)
            act.sem_inc(ps_full[s], -1)
            act.sem_inc(w_free[s], 1)
            act.wait_ge(out_free[s], 16)
            act.sem_inc(out_free[s], -16)
            act.activation(out[:, s, :], ps[s][:, 0:T], ACT.Copy).then_inc(own_a, 1)
            act.wait_ge(own_a, 1)
            act.sem_inc(own_a, -1)
            act.sem_inc(ps_free[s], 1)
            act.dma_start(k.rows[tile], out[:, s, :]).then_inc(out_free[s], 16)
            if more:
                round_weights(act, s)

        with k.nc.Block() as block:
            @block.sync
            def _(sp):
                for s in range(2):
                    load(sp, s, s)
                sp.dma_start(k.mix[:, :], a["consts"][:, N_BASE:N_MIX]).then_inc(mix_in, 16)
                with sp.Fori(1, pairs) as i:
                    for s in range(2):
                        load(sp, s, i * 2 + s)
                load(sp, 0, N_IN - 1)
                sp.wait_ge(mix_in, 16)
                sp.sem_inc(mix_in, -16)

            @block.tensor
            def _(pe):
                with pe.Fori(0, pairs) as i:
                    for s in range(2):
                        multiply(pe, s)
                multiply(pe, 0)

            @block.vector
            def _(dve):
                with dve.Fori(0, pairs) as i:
                    for s in range(2):
                        rest_of_weights(dve, s)
                rest_of_weights(dve, 0)

            @block.scalar
            def _(act):
                for s in range(2):
                    act.sem_inc(w_free[s], 1)
                    act.sem_inc(ps_free[s], 1)
                    act.sem_inc(out_free[s], 16)
                for s in range(2):
                    round_weights(act, s)
                with act.Fori(0, pairs - 1) as i:
                    for s in range(2):
                        collect(act, s, i * 2 + s)
                collect(act, 0, N_IN - 3)
                collect(act, 1, N_IN - 2, more=False)
                collect(act, 0, N_IN - 1, more=False)
                for s in range(2):
                    act.wait_ge(w_free[s], 1)
                    act.sem_inc(w_free[s], -1)
                    act.wait_ge(ps_free[s], 1)
                    act.sem_inc(ps_free[s], -1)
                    act.wait_ge(out_free[s], 16)
                    act.sem_inc(out_free[s], -16)


def matmul_into_phase(k, w_dram, n_k, rhs, dest, n, add):
    with k.phase() as st:
        w = k.sb(st, "w", [P, 2, n_k, P])
        ps = [k.banks(st, f"ps{s}", 3) for s in range(2)]
        w_full, w_free = k.sems(st, "w_full", 2), k.sems(st, "w_free", 2)
        ps_full, ps_free = k.sems(st, "ps_full", 2), k.sems(st, "ps_free", 2)
        own = k.sem(st, "own")
        with k.nc.Block() as block:
            @block.sync
            def _(sp):
                with sp.Fori(0, KD // 2) as i:
                    for s in range(2):
                        sp.wait_ge(w_free[s], 1)
                        sp.sem_inc(w_free[s], -1)
                        sp.dma_start(w[:, s], w_dram[i * 2 + s]).then_inc(w_full[s], 16)

            @block.tensor
            def _(pe):
                with pe.Fori(0, KD // 2) as i:
                    for s in range(2):
                        pe.wait_ge(w_full[s], 16)
                        pe.sem_inc(w_full[s], -16)
                        pe.wait_ge(ps_free[s], 1)
                        pe.sem_inc(ps_free[s], -1)
                        products(pe, ps[s], w[:, s], rhs, n_k, n).then_inc(ps_full[s], 1)

            @block.vector
            def _(dve):
                for s in range(2):
                    dve.sem_inc(w_free[s], 1)
                    dve.sem_inc(ps_free[s], 1)
                with dve.Fori(0, KD // 2) as i:
                    for s in range(2):
                        dve.wait_ge(ps_full[s], 1)
                        dve.sem_inc(ps_full[s], -1)
                        dve.sem_inc(w_free[s], 1)
                        target = dest[:, i * 2 + s, 0:n]
                        if add:
                            ins = dve.tensor_tensor(target, ps[s][:, 0:n], target, ALU.add)
                        else:
                            ins = dve.tensor_copy(target, ps[s][:, 0:n])
                        ins.then_inc(own, 1)
                        dve.wait_ge(own, 1)
                        dve.sem_inc(own, -1)
                        dve.sem_inc(ps_free[s], 1)
                for s in range(2):
                    dve.wait_ge(w_free[s], 1)
                    dve.sem_inc(w_free[s], -1)
                    dve.wait_ge(ps_free[s], 1)
                    dve.sem_inc(ps_free[s], -1)


def residual_phase(k, y, x, n, m_gate, reload=None):
    with k.phase() as st:
        sq = k.sb(st, "sq", [P, 2, T])
        acc = k.sb(st, "acc", [P, T])
        r = k.sb(st, "r", [P, T])
        ps = k.banks(st, "ps", 3)
        sq_full, sq_free = k.sems(st, "sq_full", 2), k.sems(st, "sq_free", 2)
        acc_pe, sum_dve, inv_act, root_dve = (k.sem(st, s) for s in ("acc_pe", "sum_dve", "inv_act", "root_dve"))
        own_a, own_v, x_in, scaled = (k.sem(st, s) for s in ("own_a", "own_v", "x_in", "scaled"))
        own_p = k.sem(st, "own_p")
        with k.nc.Block() as block:
            @block.scalar
            def _(act):
                for t in range(KD):
                    if t >= 2:
                        act.wait_ge(sq_free[t % 2], 1)
                        act.sem_inc(sq_free[t % 2], -1)
                    act.activation(sq[:, t % 2, 0:n], y[:, t, 0:n], ACT.Square).then_inc(sq_full[t % 2], 1)
                act.wait_ge(inv_act, 1)
                act.sem_inc(inv_act, -1)
                act.activation(r[:, 0:n], r[:, 0:n], ACT.Sqrt).then_inc(own_a, 1)
                act.wait_ge(own_a, 1)
                act.sem_inc(own_a, -1)
                act.sem_inc(root_dve, 1)

            @block.vector
            def _(dve):
                for t in range(KD):
                    dve.wait_ge(sq_full[t % 2], 1)
                    dve.sem_inc(sq_full[t % 2], -1)
                    if t == 0:
                        ins = dve.tensor_copy(acc[:, 0:n], sq[:, 0, 0:n])
                    else:
                        ins = dve.tensor_tensor(acc[:, 0:n], acc[:, 0:n], sq[:, t % 2, 0:n], ALU.add)
                    if t < KD - 2:
                        ins.then_inc(own_v, 1)
                        dve.wait_ge(own_v, 1)
                        dve.sem_inc(own_v, -1)
                        dve.sem_inc(sq_free[t % 2], 1)
                    elif t < KD - 1:
                        ins.then_inc(own_v, 1)
                        dve.wait_ge(own_v, 1)
                        dve.sem_inc(own_v, -1)
                    else:
                        ins.then_inc(own_v, 1)
                        dve.wait_ge(own_v, 1)
                        dve.sem_inc(own_v, -1)
                        dve.sem_inc(acc_pe, 1)
                dve.wait_ge(sum_dve, 1)
                dve.sem_inc(sum_dve, -1)
                row_factor(k, st, dve, inv_act, ps, r, n, own_v, D_MODEL)
                dve.wait_ge(root_dve, 1)
                dve.sem_inc(root_dve, -1)
                for t in range(KD):
                    for lo, hi, s in token_parts(n):
                        ins = dve.scalar_tensor_tensor(y[:, t, lo:hi], y[:, t, lo:hi],
                                                       k.mods[:, m_gate * KD + t, s:s + 1], r[:, lo:hi],
                                                       ALU.mult, ALU.mult)
                        if hi < n:
                            ins.then_inc(own_v, 1)
                            dve.wait_ge(own_v, 1)
                            dve.sem_inc(own_v, -1)
                    ins.then_inc(scaled, 1)

            @block.gpsimd
            def _(pool):
                if reload is not None:
                    pool.wait_ge(x_in, 16)
                    pool.sem_inc(x_in, -16)
                for t in range(KD):
                    pool.wait_ge(scaled, 1)
                    pool.sem_inc(scaled, -1)
                    last = pool.tensor_tensor(k.xT[:, t, 0:n], x[:, t, 0:n], y[:, t, 0:n], ALU.add)
                last.then_inc(own_p, 1)
                pool.wait_ge(own_p, 1)
                pool.sem_inc(own_p, -1)

            @block.tensor
            def _(pe):
                pe.wait_ge(acc_pe, 1)
                pe.sem_inc(acc_pe, -1)
                for lo, w in SEGS:
                    if lo < n:
                        mm = pe.matmul(ps[:, lo:lo + w], k.const(C_ONES), acc[:, lo:lo + w], start=True, stop=True)
                mm.then_inc(sum_dve, 1)

            if reload is not None:
                @block.sync
                def _(sp):
                    sp.dma_start(x[:, :, :], reload).then_inc(x_in, 16)


def conv_parts(n):
    return [(0, SEQ)] + ([(SEQ, n)] if n > SEQ else [])


class Job:

    def __init__(self, tile, dest, taps=None, silu=False, width=None, factor=None, rope=False, to_tokens=None):
        self.tile, self.dest, self.taps, self.silu = tile, dest, taps, silu
        self.width, self.factor, self.rope, self.to_tokens = width, factor, rope, to_tokens


def rows_phase(k, jobs, trig=None):
    with k.phase() as st:
        raw = k.sb(st, "raw", [P, 2, T])
        sq = k.sb(st, "sq", [P, 2, T])
        r = k.sb(st, "r", [P, 2, T])
        rot = k.sb(st, "rot", [P, SEQ]) if trig is not None else None
        ps = [k.banks(st, f"ps{s}", 3) for s in range(2)]
        ps_rot = k.banks(st, "ps_rot", 2)
        raw_in, raw_free = k.sems(st, "raw_in", 2), k.sems(st, "raw_free", 2)
        centre_dve, taps_act, y_dve, sq_pe, sum_dve, inv_act, root_dve = (
            k.sem(st, s) for s in ("centre_dve", "taps_act", "y_dve", "sq_pe", "sum_dve", "inv_act", "root_dve"))
        y_pe, rot_dve, pass_pe, tok_dve, tok_free = (
            k.sem(st, s) for s in ("y_pe", "rot_dve", "pass_pe", "tok_dve", "tok_free"))
        own_a, own_v = k.sem(st, "own_a"), k.sem(st, "own_v")
        with k.nc.Block() as block:
            @block.sync
            def _(sp):
                for j, job in enumerate(jobs):
                    if j >= 2:
                        sp.wait_ge(raw_free[j % 2], 1)
                        sp.sem_inc(raw_free[j % 2], -1)
                    sp.dma_start(raw[:, j % 2, :], k.rows[job.tile]).then_inc(raw_in[j % 2], 16)

            @block.scalar
            def _(act):
                for j, job in enumerate(jobs):
                    s = j % 2
                    act.wait_ge(raw_in[s], 16)
                    act.sem_inc(raw_in[s], -16)
                    if job.taps is not None:
                        act.activation(job.dest, raw[:, s, :], ACT.Copy,
                                       scale=k.vec(V_GCONV + 6 + job.taps)).then_inc(own_a, 1)
                        act.wait_ge(own_a, 1)
                        act.sem_inc(own_a, -1)
                        act.sem_inc(centre_dve, 1)
                        act.wait_ge(taps_act, 1)
                        act.sem_inc(taps_act, -1)
                        act.activation(job.dest, job.dest, ACT.Silu).then_inc(own_a, 1)
                        act.wait_ge(own_a, 1)
                        act.sem_inc(own_a, -1)
                    else:
                        act.activation(job.dest, raw[:, s, :], ACT.Silu if job.silu else ACT.Copy).then_inc(own_a, 1)
                        act.wait_ge(own_a, 1)
                        act.sem_inc(own_a, -1)
                    act.sem_inc(raw_free[s], 1)
                    if job.width is not None:
                        act.activation(sq[:, s, :], job.dest, ACT.Square).then_inc(own_a, 1)
                        act.wait_ge(own_a, 1)
                        act.sem_inc(own_a, -1)
                        act.sem_inc(sq_pe, 1)
                        act.wait_ge(inv_act, 1)
                        act.sem_inc(inv_act, -1)
                        act.activation(r[:, s, :], r[:, s, :], ACT.Sqrt).then_inc(own_a, 1)
                        act.wait_ge(own_a, 1)
                        act.sem_inc(own_a, -1)
                        act.sem_inc(root_dve, 1)
                    elif job.rope or job.to_tokens is not None:
                        act.sem_inc(y_dve, 1)
                for s in range(min(2, len(jobs))):
                    act.wait_ge(raw_free[s], 1)
                    act.sem_inc(raw_free[s], -1)

            @block.vector
            def _(dve):
                for j, job in enumerate(jobs):
                    s = j % 2
                    if job.taps is not None:
                        dve.wait_ge(centre_dve, 1)
                        dve.sem_inc(centre_dve, -1)
                        for lo, hi in conv_parts(T):
                            dve.scalar_tensor_tensor(
                                job.dest[:, lo + 1:hi], raw[:, s, lo:hi - 1], k.vec(V_GCONV + job.taps),
                                job.dest[:, lo + 1:hi], ALU.mult, ALU.add).then_inc(own_v, 1)
                            dve.wait_ge(own_v, 1)
                            dve.sem_inc(own_v, -1)
                            dve.scalar_tensor_tensor(
                                job.dest[:, lo:hi - 1], raw[:, s, lo + 1:hi], k.vec(V_GCONV + 12 + job.taps),
                                job.dest[:, lo:hi - 1], ALU.mult, ALU.add).then_inc(own_v, 1)
                            dve.wait_ge(own_v, 1)
                            dve.sem_inc(own_v, -1)
                        dve.sem_inc(taps_act, 1)
                    if job.width is not None:
                        dve.wait_ge(sum_dve, 1)
                        dve.sem_inc(sum_dve, -1)
                        row_factor(k, st, dve, inv_act, ps[s], r[:, s, :], T, own_v, job.width)
                        dve.wait_ge(root_dve, 1)
                        dve.sem_inc(root_dve, -1)
                        dve.scalar_tensor_tensor(job.dest, job.dest, job.factor, r[:, s, :],
                                                 ALU.mult, ALU.mult).then_inc(own_v, 1)
                        dve.wait_ge(own_v, 1)
                        dve.sem_inc(own_v, -1)
                    elif job.rope or job.to_tokens is not None:
                        dve.wait_ge(y_dve, 1)
                        dve.sem_inc(y_dve, -1)
                    if job.rope:
                        dve.sem_inc(y_pe, 1)
                        dve.wait_ge(rot_dve, 1)
                        dve.sem_inc(rot_dve, -1)
                        dve.tensor_tensor(rot[:, :], ps_rot[:, 0:SEQ], trig[:, SEQ:], ALU.mult).then_inc(own_v, 1)
                        dve.wait_ge(own_v, 1)
                        dve.sem_inc(own_v, -1)
                        lat = job.dest[:, 0:SEQ]
                        dve.tensor_tensor(lat, lat, trig[:, 0:SEQ], ALU.mult).then_inc(own_v, 1)
                        dve.wait_ge(own_v, 1)
                        dve.sem_inc(own_v, -1)
                        dve.tensor_tensor(lat, lat, rot[:, :], ALU.add).then_inc(own_v, 1)
                        dve.wait_ge(own_v, 1)
                        dve.sem_inc(own_v, -1)
                    if job.to_tokens is not None:
                        dve.sem_inc(pass_pe, 1)
                        for c0 in range(0, NT, 4):
                            n = min(4, NT - c0)
                            dve.wait_ge(tok_dve, 1)
                            dve.sem_inc(tok_dve, -1)
                            dve.tensor_copy(job.to_tokens[:, c0:c0 + n, :],
                                            ps_rot[:, 0:n * P].rearrange("p (c f) -> p c f", f=P)).then_inc(own_v, 1)
                            dve.wait_ge(own_v, 1)
                            dve.sem_inc(own_v, -1)
                            dve.sem_inc(tok_free, 1)

            @block.tensor
            def _(pe):
                for j, job in enumerate(jobs):
                    s = j % 2
                    if job.width is not None:
                        pe.wait_ge(sq_pe, 1)
                        pe.sem_inc(sq_pe, -1)
                        for lo, w in SEGS:
                            mm = pe.matmul(ps[s][:, lo:lo + w], k.const(C_BLK), sq[:, s, lo:lo + w],
                                           start=True, stop=True)
                        mm.then_inc(sum_dve, 1)
                    if job.rope:
                        pe.wait_ge(y_pe, 1)
                        pe.sem_inc(y_pe, -1)
                        for lo, w in SEGS[:2]:
                            mm = pe.matmul(ps_rot[:, lo:lo + w], k.const(C_ROT), job.dest[:, lo:lo + w],
                                           start=True, stop=True)
                        mm.then_inc(rot_dve, 1)
                    if job.to_tokens is not None:
                        pe.wait_ge(pass_pe, 1)
                        pe.sem_inc(pass_pe, -1)
                        for c0 in range(0, NT, 4):
                            if c0:
                                pe.wait_ge(tok_free, 1)
                                pe.sem_inc(tok_free, -1)
                            for c in range(c0, min(c0 + 4, NT)):
                                mm = pe.transpose(ps_rot[:, (c - c0) * P:(c - c0 + 1) * P],
                                                  job.dest[:, c * P:(c + 1) * P], k.const(C_IDENT))
                            mm.then_inc(tok_dve, 1)
                        pe.wait_ge(tok_free, 1)
                        pe.sem_inc(tok_free, -1)


def gate_phase(k, pairs, oT_tile, z_tile, gain_col):
    with k.phase() as st:
        z = k.sb(st, "z", [P, 2, T])
        sq = k.sb(st, "sq", [P, 2, T])
        r = k.sb(st, "r", [P, 2, T])
        ps = [k.banks(st, f"ps{s}", 3) for s in range(2)]
        z_in = k.sems(st, "z_in", 2)
        o_act, sq_pe, sum_dve, inv_act, root_dve = (
            k.sem(st, s) for s in ("o_act", "sq_pe", "sum_dve", "inv_act", "root_dve"))
        own_a, own_v = k.sem(st, "own_a"), k.sem(st, "own_v")
        with k.nc.Block() as block:
            @block.sync
            def _(sp):
                for s in range(2):
                    sp.dma_start(z[:, s, :], k.rows[z_tile + s]).then_inc(z_in[s], 16)

            @block.scalar
            def _(act):
                for s in range(2):
                    act.wait_ge(z_in[s], 16)
                    act.sem_inc(z_in[s], -16)
                    act.activation(z[:, s, :], z[:, s, :], ACT.Silu).then_inc(own_a, 1)
                    act.wait_ge(own_a, 1)
                    act.sem_inc(own_a, -1)
                for s in range(2):
                    act.wait_ge(o_act, 1)
                    act.sem_inc(o_act, -1)
                    act.activation(sq[:, s, :], pairs[:, 0, s, :], ACT.Square).then_inc(own_a, 1)
                    act.wait_ge(own_a, 1)
                    act.sem_inc(own_a, -1)
                    act.sem_inc(sq_pe, 1)
                for s in range(2):
                    act.wait_ge(inv_act, 1)
                    act.sem_inc(inv_act, -1)
                    act.activation(r[:, s, :], r[:, s, :], ACT.Sqrt).then_inc(own_a, 1)
                    act.wait_ge(own_a, 1)
                    act.sem_inc(own_a, -1)
                    act.sem_inc(root_dve, 1)

            @block.tensor
            def _(pe):
                for s in range(2):
                    pe.wait_ge(sq_pe, 1)
                    pe.sem_inc(sq_pe, -1)
                    for lo, w in SEGS:
                        mm = pe.matmul(ps[s][:, lo:lo + w], k.const(C_BLK), sq[:, s, lo:lo + w], start=True, stop=True)
                    mm.then_inc(sum_dve, 1)

            @block.vector
            def _(dve):
                for s in range(2):
                    dve.tensor_tensor(pairs[:, 0, s, :], pairs[:, 0, s, :], pairs[:, 1, s, :], ALU.add)\
                        .then_inc(own_v, 1)
                    dve.wait_ge(own_v, 1)
                    dve.sem_inc(own_v, -1)
                    dve.sem_inc(o_act, 1)
                for s in range(2):
                    dve.wait_ge(sum_dve, 1)
                    dve.sem_inc(sum_dve, -1)
                    row_factor(k, st, dve, inv_act, ps[s], r[:, s, :], T, own_v, HD)
                for s in range(2):
                    dve.wait_ge(root_dve, 1)
                    dve.sem_inc(root_dve, -1)
                    dve.scalar_tensor_tensor(pairs[:, 0, s, :], pairs[:, 0, s, :], k.vec(gain_col),
                                             r[:, s, :], ALU.mult, ALU.mult).then_inc(own_v, 1)
                    dve.wait_ge(own_v, 1)
                    dve.sem_inc(own_v, -1)
                    dve.tensor_tensor(k.oT[:, oT_tile + s, :], pairs[:, 0, s, :], z[:, s, :], ALU.mult)\
                        .then_inc(own_v, 1)
                    dve.wait_ge(own_v, 1)
                    dve.sem_inc(own_v, -1)


def decay_rows_phase(k, bg):
    with k.phase() as st:
        lin = k.sb(st, "lin", [HD, T])
        soft = k.sb(st, "soft", [HD, T])
        came, a_dve, v_act, own_a, own_v = (k.sem(st, s) for s in ("came", "a_dve", "v_act", "own_a", "own_v"))
        g = slice(G_ROW, G_ROW + 2 * H)
        with k.nc.Block() as block:
            @block.sync
            def _(sp):
                sp.dma_start(bg[:, :], k.rows[T_BETA][0:HD]).then_inc(came, 16)

            @block.scalar
            def _(act):
                act.wait_ge(came, 16)
                act.sem_inc(came, -16)
                act.activation(lin[g, :], bg[g, :], ACT.Identity, bias=k.vecs[g, V_DTB:V_DTB + 1]).then_inc(own_a, 1)
                act.wait_ge(own_a, 1)
                act.sem_inc(own_a, -1)
                act.sem_inc(a_dve, 1)
                act.activation(bg[0:2 * H, :], bg[0:2 * H, :], ACT.Sigmoid).then_inc(own_a, 1)
                act.wait_ge(own_a, 1)
                act.sem_inc(own_a, -1)
                act.wait_ge(v_act, 1)
                act.sem_inc(v_act, -1)
                act.activation(soft[g, :], soft[g, :], ACT.Exp).then_inc(own_a, 1)
                act.wait_ge(own_a, 1)
                act.sem_inc(own_a, -1)
                act.activation(soft[g, :], soft[g, :], ACT.Ln, bias=1.0).then_inc(own_a, 1)
                act.wait_ge(own_a, 1)
                act.sem_inc(own_a, -1)
                act.sem_inc(a_dve, 1)

            @block.vector
            def _(dve):
                dve.wait_ge(a_dve, 1)
                dve.sem_inc(a_dve, -1)
                dve.tensor_scalar(soft[g, :], lin[g, :], 0.0, 2.0, ALU.min, ALU.mult).then_inc(own_v, 1)
                dve.wait_ge(own_v, 1)
                dve.sem_inc(own_v, -1)
                dve.tensor_tensor(soft[g, :], soft[g, :], lin[g, :], ALU.subtract).then_inc(own_v, 1)
                dve.wait_ge(own_v, 1)
                dve.sem_inc(own_v, -1)
                dve.sem_inc(v_act, 1)
                dve.tensor_scalar(lin[g, :], lin[g, :], 0.0, None, ALU.max).then_inc(own_v, 1)
                dve.wait_ge(own_v, 1)
                dve.sem_inc(own_v, -1)
                dve.wait_ge(a_dve, 1)
                dve.sem_inc(a_dve, -1)
                dve.tensor_tensor(lin[g, :], lin[g, :], soft[g, :], ALU.add).then_inc(own_v, 1)
                dve.wait_ge(own_v, 1)
                dve.sem_inc(own_v, -1)
                dve.tensor_scalar(bg[g, :], lin[g, :], k.expa[g, 0:1], None, ALU.mult).then_inc(own_v, 1)
                dve.wait_ge(own_v, 1)
                dve.sem_inc(own_v, -1)


def chunk_of(d, i):
    return (i + NT - CTX // P) % NT if d == 0 else NT - 1 - i


def gdn_phase(k, qkv, bg, both):
    with k.phase() as st:
        stg = k.sb(st, "stg", [P, 2, 6, P])
        bgs = k.sb(st, "bgs", [HD, 2, P])
        tok = k.sb(st, "tok", [P, 2, 4, P])
        bgt = k.sb(st, "bgt", [P, 2, HD])
        nb = k.sb(st, "nb", [P, 2, H])
        gm = k.sb(st, "gm", [P, 2, H, P])
        gb = k.sb(st, "gb", [P, 2, H, HD])
        dec = k.sb(st, "dec", [P, 2, H, P])
        ecum = k.sb(st, "ecum", [P, 2, 2 * P + 2 * H])
        dm = dec
        attn = k.sb(st, "attn", [P, 2, H, P])
        nm = k.sb(st, "nm", [P, 2, H, P])
        S = k.sb(st, "S", [P, 2, H, P])
        Ti = k.sb(st, "Ti", [P, 2, H, P])
        vm, nbd = gm, S
        qd = k.sb(st, "qd", [P, 2, 2, P])
        ke = k.sb(st, "ke", [P, 2, H, HD])
        kd = k.sb(st, "kd", [P, 2, H, HD])
        wtn = k.sb(st, "wtn", [P, 2, 2, P])
        vn = k.sb(st, "vn", [P, 2, H, HD])
        state = k.sb(st, "state", [P, 2, 2, P])
        tmp = k.sb(st, "tmp", [P, 2, 2, P])
        B = [[k.banks(st, f"b{d}{b}", 1) for b in range(4)] for d in range(2)]
        names = ("staged_pe tr_act bgt_dve tok_pe gm_pe nb_pool rc_act de_pool dm_dve ke_pe kk_dve s2_pe t2_act "
                 "inv_pe v_dve vm_pe u_dve wt_act wtn_pe vn_dve vn_pe o_act su_dve state_pe").split()
        sem = {n: k.sems(st, n, 2) for n in names}
        own = {e: k.sem(st, f"own_{e}") for e in ("act", "dve", "pool")}
        beta = [bgt[:, d, BETA_ROW + H * d:BETA_ROW + H * (d + 1)] for d in range(2)]
        gcol = [bgt[:, d, G_ROW + H * d:G_ROW + H * (d + 1)] for d in range(2)]
        ident = k.const(C_IDENT)
        cum = [k.const(C_CUM + d * P) for d in range(2)]
        strict = [k.const(C_STR + d * P) for d in range(2)]
        after = [k.const(C_STR + (1 - d) * P) for d in range(2)]

        def heads(b):
            return b[:, :].rearrange("p (h f) -> p h f", f=P)

        def level_ji(d, l):
            return k.const(C_LVL + (d * LEVELS + l) * P)

        def level_ij(d, l):
            return k.const(C_LVL + ((1 - d) * LEVELS + l) * P)

        with k.nc.Block() as block:
            @block.scalar
            def _(act):
                with act.Fori(0, NT) as i:
                    for d in range(2):
                        col = bass.ds(chunk_of(d, i) * P, P)
                        act.activation(stg[:, d], qkv[:, :, col], ACT.Copy)
                        act.activation(bgs[:, d, :], bg[:, col], ACT.Copy).then_inc(own["act"], 1)
                        act.wait_ge(own["act"], 1)
                        act.sem_inc(own["act"], -1)
                        act.sem_inc(sem["staged_pe"][d], 1)
                    for d in range(2):
                        act.wait_ge(sem["tr_act"][d], 1)
                        act.sem_inc(sem["tr_act"][d], -1)
                        act.activation(tok[:, d], heads(B[d][0]), ACT.Copy).then_inc(own["act"], 1)
                        act.wait_ge(own["act"], 1)
                        act.sem_inc(own["act"], -1)
                        act.activation(bgt[:, d, :], B[d][1][:, 0:HD], ACT.Copy).then_inc(own["act"], 1)
                        act.wait_ge(own["act"], 1)
                        act.sem_inc(own["act"], -1)
                        act.sem_inc(sem["bgt_dve"][d], 1)
                        act.sem_inc(sem["tok_pe"][d], 1)
                    for d in range(2):
                        act.wait_ge(sem["rc_act"][d], 1)
                        act.sem_inc(sem["rc_act"][d], -1)
                        act.activation(dec[:, d], heads(B[d][2]), ACT.Exp).then_inc(own["act"], 1)
                        act.wait_ge(own["act"], 1)
                        act.sem_inc(own["act"], -1)
                        act.activation(ecum[:, d, :], B[d][3][:, 0:2 * P + 2 * H], ACT.Exp).then_inc(own["act"], 1)
                        act.wait_ge(own["act"], 1)
                        act.sem_inc(own["act"], -1)
                        act.sem_inc(sem["de_pool"][d], 1)
                    for d in range(2):
                        act.wait_ge(sem["t2_act"][d], 1)
                        act.sem_inc(sem["t2_act"][d], -1)
                        act.activation(Ti[:, d], heads(B[d][2]), ACT.Copy).then_inc(own["act"], 1)
                        act.wait_ge(own["act"], 1)
                        act.sem_inc(own["act"], -1)
                        act.sem_inc(sem["inv_pe"][d], 1)
                    for d in range(2):
                        act.wait_ge(sem["wt_act"][d], 1)
                        act.sem_inc(sem["wt_act"][d], -1)
                        act.activation(wtn[:, d], B[d][0][:, 0:2 * P].rearrange("p (a f) -> p a f", f=P),
                                       ACT.Copy, scale=-1.0).then_inc(own["act"], 1)
                        act.wait_ge(own["act"], 1)
                        act.sem_inc(own["act"], -1)
                        act.sem_inc(sem["wtn_pe"][d], 1)
                    for d in range(2):
                        act.wait_ge(sem["o_act"][d], 1)
                        act.sem_inc(sem["o_act"][d], -1)
                        act.activation(both[:, d, :, bass.ds(chunk_of(d, i) * P, P)],
                                       B[d][2][:, 0:2 * P].rearrange("p (a f) -> p a f", f=P), ACT.Copy)\
                            .then_inc(own["act"], 1)
                        act.wait_ge(own["act"], 1)
                        act.sem_inc(own["act"], -1)

            @block.vector
            def _(dve):
                dve.memset(state[:, :, :, :], 0.0).then_inc(own["dve"], 1)
                dve.wait_ge(own["dve"], 1)
                dve.sem_inc(own["dve"], -1)
                for d in range(2):
                    dve.sem_inc(sem["state_pe"][d], 1)
                with dve.Fori(0, NT):
                    for d in range(2):
                        dve.wait_ge(sem["bgt_dve"][d], 1)
                        dve.sem_inc(sem["bgt_dve"][d], -1)
                        dve.tensor_scalar(nb[:, d, :], beta[d], -1.0, None, ALU.mult).then_inc(own["dve"], 1)
                        dve.wait_ge(own["dve"], 1)
                        dve.sem_inc(own["dve"], -1)
                        dve.sem_inc(sem["nb_pool"][d], 1)
                        dve.tensor_copy(gb[:, d], widen(gcol[d], HD)).then_inc(own["dve"], 1)
                        dve.wait_ge(own["dve"], 1)
                        dve.sem_inc(own["dve"], -1)
                        dve.tensor_tensor(gm[:, d], spread(strict[d], H), widen(gcol[d], P), ALU.mult)\
                            .then_inc(own["dve"], 1)
                        dve.wait_ge(own["dve"], 1)
                        dve.sem_inc(own["dve"], -1)
                        dve.sem_inc(sem["gm_pe"][d], 1)
                    for d in range(2):
                        dve.wait_ge(sem["dm_dve"][d], 1)
                        dve.sem_inc(sem["dm_dve"][d], -1)
                        dve.wait_ge(sem["kk_dve"][d], 1)
                        dve.sem_inc(sem["kk_dve"][d], -1)
                        for p in range(2):
                            pair = B[d][p][:, :].rearrange("p (a x f) -> p a x f", a=2, x=2)
                            dve.tensor_tensor(nm[:, d, p::2, :], pair[:, :, 1, :], nbd[:, d, p::2, :],
                                              ALU.mult).then_inc(own["dve"], 1)
                            dve.wait_ge(own["dve"], 1)
                            dve.sem_inc(own["dve"], -1)
                            dve.tensor_tensor(attn[:, d, p::2, :], pair[:, :, 0, :], dm[:, d, p::2, :],
                                              ALU.mult).then_inc(own["dve"], 1)
                            dve.wait_ge(own["dve"], 1)
                            dve.sem_inc(own["dve"], -1)
                        dve.tensor_tensor(S[:, d], nm[:, d], spread(level_ji(d, 0), H), ALU.mult)\
                            .then_inc(own["dve"], 1)
                        dve.wait_ge(own["dve"], 1)
                        dve.sem_inc(own["dve"], -1)
                        dve.tensor_tensor(S[:, d], S[:, d], spread(ident, H), ALU.add).then_inc(own["dve"], 1)
                        dve.wait_ge(own["dve"], 1)
                        dve.sem_inc(own["dve"], -1)
                        dve.sem_inc(sem["s2_pe"][d], 1)
                    for l in range(1, LEVELS):
                        for d in range(2):
                            dve.wait_ge(sem["v_dve"][d], 1)
                            dve.sem_inc(sem["v_dve"][d], -1)
                            dve.tensor_tensor(vm[:, d], heads(B[d][0]), spread(level_ij(d, l), H),
                                              ALU.mult).then_inc(own["dve"], 1)
                            dve.wait_ge(own["dve"], 1)
                            dve.sem_inc(own["dve"], -1)
                            dve.sem_inc(sem["vm_pe"][d], 1)
                        for d in range(2):
                            dve.wait_ge(sem["u_dve"][d], 1)
                            dve.sem_inc(sem["u_dve"][d], -1)
                            dve.tensor_tensor(S[:, d], heads(B[d][1]), S[:, d], ALU.add).then_inc(own["dve"], 1)
                            dve.wait_ge(own["dve"], 1)
                            dve.sem_inc(own["dve"], -1)
                            if l < LEVELS - 1:
                                dve.tensor_tensor(Ti[:, d], heads(B[d][2]), Ti[:, d], ALU.add)\
                                    .then_inc(own["dve"], 1)
                                dve.wait_ge(own["dve"], 1)
                                dve.sem_inc(own["dve"], -1)
                            dve.sem_inc(sem["inv_pe"][d], 1)
                    for d in range(2):
                        dve.wait_ge(sem["vn_dve"][d], 1)
                        dve.sem_inc(sem["vn_dve"][d], -1)
                        dve.tensor_tensor(vn[:, d], B[d][1][:, 0:2 * P].rearrange("p (h f) -> p h f", f=HD),
                                          widen(beta[d], HD), ALU.mult).then_inc(own["dve"], 1)
                        dve.wait_ge(own["dve"], 1)
                        dve.sem_inc(own["dve"], -1)
                        dve.sem_inc(sem["vn_pe"][d], 1)
                    for d in range(2):
                        dve.wait_ge(sem["su_dve"][d], 1)
                        dve.sem_inc(sem["su_dve"][d], -1)
                        dve.tensor_tensor(tmp[:, d], B[d][3][:, 0:2 * P].rearrange("p (a f) -> p a f", f=P),
                                          spread(k.const(C_BLK), 2), ALU.mult).then_inc(own["dve"], 1)
                        dve.wait_ge(own["dve"], 1)
                        dve.sem_inc(own["dve"], -1)
                        for a in range(2):
                            whole = a * P + (P - 1 if d == 0 else 0)
                            dve.scalar_tensor_tensor(state[:, d, a, :], state[:, d, a, :],
                                                     ecum[:, d, whole:whole + 1], tmp[:, d, a, :],
                                                     ALU.mult, ALU.add).then_inc(own["dve"], 1)
                            dve.wait_ge(own["dve"], 1)
                            dve.sem_inc(own["dve"], -1)
                        dve.sem_inc(sem["state_pe"][d], 1)
                for d in range(2):
                    dve.wait_ge(sem["state_pe"][d], 1)
                    dve.sem_inc(sem["state_pe"][d], -1)

            @block.gpsimd
            def _(pool):
                with pool.Fori(0, NT):
                    for d in range(2):
                        pool.wait_ge(sem["de_pool"][d], 1)
                        pool.sem_inc(sem["de_pool"][d], -1)
                        pool.wait_ge(sem["nb_pool"][d], 1)
                        pool.sem_inc(sem["nb_pool"][d], -1)
                        pool.tensor_tensor(nbd[:, d], dec[:, d], spread(after[d], H), ALU.mult)\
                            .then_inc(own["pool"], 1)
                        pool.wait_ge(own["pool"], 1)
                        pool.sem_inc(own["pool"], -1)
                        pool.tensor_tensor(nbd[:, d], nbd[:, d], widen(nb[:, d, :], P), ALU.mult)\
                            .then_inc(own["pool"], 1)
                        pool.wait_ge(own["pool"], 1)
                        pool.sem_inc(own["pool"], -1)
                        pool.tensor_tensor(dm[:, d], dec[:, d], spread(cum[d], H), ALU.mult).then_inc(own["pool"], 1)
                        pool.wait_ge(own["pool"], 1)
                        pool.sem_inc(own["pool"], -1)
                        pool.sem_inc(sem["dm_dve"][d], 1)
                    for d in range(2):
                        pool.tensor_tensor(qd[:, d], stg[:, d, 0:2, :],
                                           ecum[:, d, 0:2 * P].rearrange("p (a f) -> p a f", f=P), ALU.mult)
                        ktok = tok[:, d, 0:2, :].rearrange("p a (h f) -> p (a h) f", f=HD)
                        pool.tensor_tensor(kd[:, d], ktok, widen(ecum[:, d, 2 * P:2 * P + H], HD), ALU.mult)
                        pool.tensor_tensor(ke[:, d], ktok, widen(ecum[:, d, 2 * P + H:2 * P + 2 * H], HD),
                                           ALU.mult).then_inc(own["pool"], 1)
                        pool.wait_ge(own["pool"], 1)
                        pool.sem_inc(own["pool"], -1)
                        pool.sem_inc(sem["ke_pe"][d], 1)

            @block.tensor
            def _(pe):
                with pe.Fori(0, NT):
                    for d in range(2):
                        pe.wait_ge(sem["staged_pe"][d], 1)
                        pe.sem_inc(sem["staged_pe"][d], -1)
                        for x in range(4):
                            pe.transpose(B[d][0][:, x * P:(x + 1) * P], stg[:, d, 2 + x, :], ident)
                        pe.transpose(B[d][1][:, 0:HD], bgs[:, d, :], k.consts[0:HD, C_IDENT:C_IDENT + HD])\
                            .then_inc(sem["tr_act"][d], 1)
                    for d in range(2):
                        pe.wait_ge(sem["gm_pe"][d], 1)
                        pe.sem_inc(sem["gm_pe"][d], -1)
                        for h in range(H):
                            pe.matmul(B[d][2][:, h * P:(h + 1) * P], gm[:, d, h, :], cum[d], start=True, stop=True)
                        for a in range(2):
                            pe.matmul(B[d][3][:, a * P:(a + 1) * P],
                                      gb[:, d, 2 * a:2 * a + 2, :].rearrange("p h f -> p (h f)"), cum[d],
                                      start=True, stop=True)
                        pe.matmul(B[d][3][:, 2 * P:2 * P + H], strict[d], gcol[d], start=True, stop=True)
                        pe.matmul(B[d][3][:, 2 * P + H:2 * P + 2 * H], cum[d], gcol[d], start=True, stop=True)\
                            .then_inc(sem["rc_act"][d], 1)
                    for d in range(2):
                        pe.wait_ge(sem["tok_pe"][d], 1)
                        pe.sem_inc(sem["tok_pe"][d], -1)
                        for h in range(H):
                            rows, a = slice(HD * (h % 2), HD * (h % 2 + 1)), h // 2
                            mm = pe.matmul(B[d][h % 2][:, 2 * a * P:2 * (a + 1) * P], stg[rows, d, 2 + a, :],
                                           stg[rows, d, a:a + 3:2, :], start=True, stop=True)
                        mm.then_inc(sem["kk_dve"][d], 1)
                    for d in range(2):
                        pe.wait_ge(sem["s2_pe"][d], 1)
                        pe.sem_inc(sem["s2_pe"][d], -1)
                        for h in range(H):
                            mm = pe.transpose(B[d][2][:, h * P:(h + 1) * P], S[:, d, h, :], ident)
                        mm.then_inc(sem["t2_act"][d], 1)
                    for l in range(1, LEVELS):
                        for d in range(2):
                            pe.wait_ge(sem["inv_pe"][d], 1)
                            pe.sem_inc(sem["inv_pe"][d], -1)
                            for h in range(H):
                                mm = pe.matmul(B[d][0][:, h * P:(h + 1) * P], nm[:, d, h, :], Ti[:, d, h, :],
                                               start=True, stop=True)
                            mm.then_inc(sem["v_dve"][d], 1)
                        for d in range(2):
                            pe.wait_ge(sem["vm_pe"][d], 1)
                            pe.sem_inc(sem["vm_pe"][d], -1)
                            for h in range(H):
                                mm = pe.matmul(B[d][1][:, h * P:(h + 1) * P], vm[:, d, h, :], S[:, d, h, :],
                                               start=True, stop=True)
                            if l < LEVELS - 1:
                                for h in range(H):
                                    mm = pe.matmul(B[d][2][:, h * P:(h + 1) * P], S[:, d, h, :], vm[:, d, h, :],
                                                   start=True, stop=True)
                            mm.then_inc(sem["u_dve"][d], 1)
                    for d in range(2):
                        pe.wait_ge(sem["inv_pe"][d], 1)
                        pe.sem_inc(sem["inv_pe"][d], -1)
                        pe.wait_ge(sem["ke_pe"][d], 1)
                        pe.sem_inc(sem["ke_pe"][d], -1)
                        for h in range(H):
                            a, p = h // 2, h % 2
                            mm = pe.matmul(B[d][0][HD * p:HD * (p + 1), a * P:(a + 1) * P], ke[:, d, h, :],
                                           S[:, d, h, :], start=True, stop=True)
                        mm.then_inc(sem["wt_act"][d], 1)
                        for h in range(H):
                            pe.matmul(B[d][1][:, h * HD:(h + 1) * HD], S[:, d, h, :],
                                      tok[:, d, 2 + h // 2, HD * (h % 2):HD * (h % 2 + 1)],
                                      start=(h == 0), stop=False, skip_group_check=True)
                    for d in range(2):
                        pe.wait_ge(sem["wtn_pe"][d], 1)
                        pe.sem_inc(sem["wtn_pe"][d], -1)
                        pe.wait_ge(sem["state_pe"][d], 1)
                        pe.sem_inc(sem["state_pe"][d], -1)
                        for a in range(2):
                            mm = pe.matmul(B[d][1][:, a * P:(a + 1) * P], wtn[:, d, a, :], state[:, d, a, :],
                                           start=False, stop=True, skip_group_check=True)
                        mm.then_inc(sem["vn_dve"][d], 1)
                        for a in range(2):
                            pe.matmul(B[d][2][:, a * P:(a + 1) * P], state[:, d, a, :], qd[:, d, a, :],
                                      start=(a == 0), stop=False, skip_group_check=True)
                    for d in range(2):
                        pe.wait_ge(sem["vn_pe"][d], 1)
                        pe.sem_inc(sem["vn_pe"][d], -1)
                        for h in range(H):
                            a, p = h // 2, h % 2
                            mm = pe.matmul(B[d][2][HD * p:HD * (p + 1), a * P:(a + 1) * P], vn[:, d, h, :],
                                           attn[:, d, h, :], start=False, stop=True, skip_group_check=True)
                        mm.then_inc(sem["o_act"][d], 1)
                        for a in range(2):
                            mm = pe.matmul(B[d][3][:, a * P:(a + 1) * P],
                                           kd[:, d, 2 * a:2 * a + 2, :].rearrange("p h f -> p (h f)"),
                                           vn[:, d, 2 * a:2 * a + 2, :].rearrange("p h f -> p (h f)"),
                                           start=True, stop=True)
                        mm.then_inc(sem["su_dve"][d], 1)


def gdn_group(k):
    with k.phase() as st:
        both = k.sb(st, "both", [P, 2, 2, T])
        with ExitStack() as inner:
            qkv = k.sb(inner, "qkv", [P, 6, T])
            bg = k.sb(inner, "bg", [HD, T])
            decay_rows_phase(k, bg)
            jobs = []
            for m in range(6):
                job = Job(T_GDN + m, qkv[:, m, :], taps=m)
                if m < 4:
                    job.width, job.factor = 1.0, (HD ** -0.5 if m < 2 else 1.0)
                jobs.append(job)
            rows_phase(k, jobs)
            gdn_phase(k, qkv, bg, both)
        gate_phase(k, both, 0, T_Z, V_GNORM)


def hgrn_rows_phase(k, q, f, kk, v):
    with k.phase() as st:
        raw = k.sb(st, "raw", [P, 2, T])
        raw_in, raw_free = k.sems(st, "raw_in", 2), k.sems(st, "raw_free", 2)
        sig_dve, own_a, own_v = k.sem(st, "sig_dve"), k.sem(st, "own_a"), k.sem(st, "own_v")
        tiles = [T_HF, T_HF + 1, T_HF + 2, T_HF + 3, T_HQ, T_HQ + 1]
        direct = k.sem(st, "direct")
        with k.nc.Block() as block:
            @block.sync
            def _(sp):
                for j, t in enumerate(tiles):
                    if j >= 2:
                        sp.wait_ge(raw_free[j % 2], 1)
                        sp.sem_inc(raw_free[j % 2], -1)
                    sp.dma_start(raw[:, j % 2, :], k.rows[t]).then_inc(raw_in[j % 2], 16)
                for a in range(2):
                    sp.dma_start(v[:, a, :], k.rows[T_HI + a]).then_inc(direct, 16)
                sp.wait_ge(direct, 32)
                sp.sem_inc(direct, -32)

            @block.scalar
            def _(act):
                for j in range(6):
                    act.wait_ge(raw_in[j % 2], 16)
                    act.sem_inc(raw_in[j % 2], -16)
                    if j < 4:
                        act.activation(f[:, j, :], raw[:, j % 2, :], ACT.Sigmoid)
                        act.activation(kk[:, j, :], raw[:, j % 2, :], ACT.Sigmoid, scale=-1.0).then_inc(own_a, 1)
                        act.wait_ge(own_a, 1)
                        act.sem_inc(own_a, -1)
                        act.sem_inc(raw_free[j % 2], 1)
                        act.sem_inc(sig_dve, 1)
                    else:
                        act.activation(q[:, j - 4, :], raw[:, j % 2, :], ACT.Silu).then_inc(own_a, 1)
                        act.wait_ge(own_a, 1)
                        act.sem_inc(own_a, -1)
                        act.sem_inc(raw_free[j % 2], 1)
                for s in range(2):
                    act.wait_ge(raw_free[s], 1)
                    act.sem_inc(raw_free[s], -1)

            @block.vector
            def _(dve):
                for j in range(4):
                    dve.wait_ge(sig_dve, 1)
                    dve.sem_inc(sig_dve, -1)
                    one_less = k.lb[:, 4 + j:5 + j]
                    dve.tensor_scalar(kk[:, j, :], kk[:, j, :], one_less, None, ALU.mult)
                    last = dve.tensor_scalar(f[:, j, :], f[:, j, :], one_less, k.lb[:, j:j + 1], ALU.mult, ALU.add)
                last.then_inc(own_v, 1)
                dve.wait_ge(own_v, 1)
                dve.sem_inc(own_v, -1)


def hgrn_phase(k, q, f, kk, v, both):
    with k.phase() as st:
        qp = k.sb(st, "qp", [P, 2, 2, P])
        kr = k.sb(st, "kr", [P, 2, 2, P])
        vs = k.sb(st, "vs", [P, 2, 2, P])
        tot = [k.sb(st, f"tot{l}", [P, 2, 2 * (P >> l)]) for l in range(LEVELS + 1)]
        attn = k.sb(st, "attn", [P, 2, H, P])
        krt = k.sb(st, "krt", [P, 2, 2, P])
        vt = k.sb(st, "vt", [P, 2, 2, P])
        state = k.sb(st, "state", [P, 2, 2, P])
        tmp = k.sb(st, "tmp", [P, 2, 2, P])
        B = [[k.banks(st, f"b{d}{b}", 1) for b in range(4)] for d in range(2)]
        names = "staged_pe staged_pool lv_dve read_pool lvl_pe free0_pe free1_pe tr_act attn_pe tok_pe o_act su_dve state_pe".split()
        sem = {n: k.sems(st, n, 2) for n in names}
        own = {e: k.sem(st, f"own_{e}") for e in ("act", "dve", "pool")}
        ident = k.const(C_IDENT)

        def two(b):
            return b[:, 0:2 * P].rearrange("p (a f) -> p a f", f=P)

        with k.nc.Block() as block:
            @block.scalar
            def _(act):
                with act.Fori(0, NT) as i:
                    for d in range(2):
                        col = bass.ds(chunk_of(d, i) * P, P)
                        act.activation(qp[:, d], q[:, :, col], ACT.Copy)
                        act.activation(kr[:, d], kk[:, 2 * d:2 * d + 2, col], ACT.Copy)
                        act.activation(vs[:, d], v[:, :, col], ACT.Copy)
                        act.activation(tot[0][:, d, :].rearrange("p (a f) -> p a f", f=P),
                                       f[:, 2 * d:2 * d + 2, col], ACT.Copy).then_inc(own["act"], 1)
                        act.wait_ge(own["act"], 1)
                        act.sem_inc(own["act"], -1)
                        act.sem_inc(sem["staged_pe"][d], 1)
                    for d in range(2):
                        act.wait_ge(sem["tr_act"][d], 1)
                        act.sem_inc(sem["tr_act"][d], -1)
                        act.activation(krt[:, d], two(B[d][0]), ACT.Copy)
                        act.activation(vt[:, d], two(B[d][1]), ACT.Copy).then_inc(own["act"], 1)
                        act.wait_ge(own["act"], 1)
                        act.sem_inc(own["act"], -1)
                        act.sem_inc(sem["tok_pe"][d], 1)
                    for d in range(2):
                        act.wait_ge(sem["o_act"][d], 1)
                        act.sem_inc(sem["o_act"][d], -1)
                        act.activation(both[:, d, :, bass.ds(chunk_of(d, i) * P, P)], two(B[d][2]),
                                       ACT.Copy).then_inc(own["act"], 1)
                        act.wait_ge(own["act"], 1)
                        act.sem_inc(own["act"], -1)

            @block.vector
            def _(dve):
                dve.memset(attn[:, :, :, :], 0.0)
                dve.memset(state[:, :, :, :], 0.0).then_inc(own["dve"], 1)
                dve.wait_ge(own["dve"], 1)
                dve.sem_inc(own["dve"], -1)
                for d in range(2):
                    dve.sem_inc(sem["state_pe"][d], 1)
                with dve.Fori(0, NT):
                    for l in range(-1, LEVELS):
                        for d in range(2):
                            mask = ident if l < 0 else k.const(C_LVL + (d * LEVELS + l) * P)
                            dve.wait_ge(sem["lv_dve"][d], 1)
                            dve.sem_inc(sem["lv_dve"][d], -1)
                            dve.sem_inc(sem["read_pool"][d], 1)
                            for p in range(2):
                                ins = dve.copy_predicated(attn[:, d, p::2, :], spread(mask, 2).bitcast(U32),
                                                          two(B[d][2 * ((l + 1) % 2) + p]))
                                ins.then_inc(own["dve"], 1)
                                dve.wait_ge(own["dve"], 1)
                                dve.sem_inc(own["dve"], -1)
                            dve.sem_inc(sem["free1_pe" if l % 2 == 0 else "free0_pe"][d], 1)
                    for d in range(2):
                        dve.sem_inc(sem["attn_pe"][d], 1)
                    for d in range(2):
                        dve.wait_ge(sem["su_dve"][d], 1)
                        dve.sem_inc(sem["su_dve"][d], -1)
                        dve.tensor_tensor(tmp[:, d], two(B[d][3]), spread(k.const(C_BLK), 2), ALU.mult)\
                            .then_inc(own["dve"], 1)
                        dve.wait_ge(own["dve"], 1)
                        dve.sem_inc(own["dve"], -1)
                        for a in range(2):
                            dve.scalar_tensor_tensor(state[:, d, a, :], state[:, d, a, :],
                                                     tot[LEVELS][:, d, a:a + 1], tmp[:, d, a, :],
                                                     ALU.mult, ALU.add).then_inc(own["dve"], 1)
                            dve.wait_ge(own["dve"], 1)
                            dve.sem_inc(own["dve"], -1)
                        dve.sem_inc(sem["state_pe"][d], 1)
                for d in range(2):
                    dve.wait_ge(sem["state_pe"][d], 1)
                    dve.sem_inc(sem["state_pe"][d], -1)

            @block.gpsimd
            def _(pool):
                with pool.Fori(0, NT):
                    for d in range(2):
                        pool.wait_ge(sem["read_pool"][d], 1)
                        pool.sem_inc(sem["read_pool"][d], -1)
                        pool.tensor_tensor(qp[:, d].rearrange("p a f -> p (a f)"),
                                           qp[:, d].rearrange("p a f -> p (a f)"), tot[0][:, d, :],
                                           ALU.mult).then_inc(own["pool"], 1)
                        pool.wait_ge(own["pool"], 1)
                        pool.sem_inc(own["pool"], -1)
                        pool.sem_inc(sem["lvl_pe"][d], 1)
                    for l in range(LEVELS):
                        w = 1 << l
                        for d in range(2):
                            late, early = (1, 0) if d == 0 else (0, 1)
                            blocks = tot[l][:, d, :].rearrange("p (n x) -> p n x", x=2)
                            qv = qp[:, d].rearrange("p a f -> p (a f)").rearrange("p (n x w) -> p n x w", x=2, w=w)
                            kv = kr[:, d].rearrange("p a f -> p (a f)").rearrange("p (n x w) -> p n x w", x=2, w=w)
                            pool.wait_ge(sem["read_pool"][d], 1)
                            pool.sem_inc(sem["read_pool"][d], -1)
                            pool.tensor_tensor(qv[:, :, late, :], qv[:, :, late, :], widen(blocks[:, :, early], w),
                                               ALU.mult)
                            pool.tensor_tensor(kv[:, :, early, :], kv[:, :, early, :], widen(blocks[:, :, late], w),
                                               ALU.mult)
                            pool.tensor_tensor(tot[l + 1][:, d, :], blocks[:, :, 0], blocks[:, :, 1],
                                               ALU.mult).then_inc(own["pool"], 1)
                            pool.wait_ge(own["pool"], 1)
                            pool.sem_inc(own["pool"], -1)
                            pool.sem_inc(sem["lvl_pe"][d], 1)

            @block.tensor
            def _(pe):
                with pe.Fori(0, NT):
                    for l in range(-1, LEVELS):
                        for d in range(2):
                            if l < 0:
                                pe.wait_ge(sem["staged_pe"][d], 1)
                                pe.sem_inc(sem["staged_pe"][d], -1)
                            else:
                                pe.wait_ge(sem["lvl_pe"][d], 1)
                                pe.sem_inc(sem["lvl_pe"][d], -1)
                            if l >= 1:
                                pe.wait_ge(sem["free0_pe" if l % 2 else "free1_pe"][d], 1)
                                pe.sem_inc(sem["free0_pe" if l % 2 else "free1_pe"][d], -1)
                            for h in range(H):
                                rows, a = slice(HD * (h % 2), HD * (h % 2 + 1)), h // 2
                                mm = pe.matmul(B[d][2 * ((l + 1) % 2) + h % 2][:, a * P:(a + 1) * P], kr[rows, d, a, :],
                                               qp[rows, d, a, :], start=True, stop=True)
                            mm.then_inc(sem["lv_dve"][d], 1)
                    for d in range(2):
                        pe.wait_ge(sem["lvl_pe"][d], 1)
                        pe.sem_inc(sem["lvl_pe"][d], -1)
                        pe.wait_ge(sem["free0_pe"][d], 1)
                        pe.sem_inc(sem["free0_pe"][d], -1)
                        pe.wait_ge(sem["free1_pe"][d], 1)
                        pe.sem_inc(sem["free1_pe"][d], -1)
                        for a in range(2):
                            pe.transpose(B[d][0][:, a * P:(a + 1) * P], kr[:, d, a, :], ident)
                        for a in range(2):
                            mm = pe.transpose(B[d][1][:, a * P:(a + 1) * P], vs[:, d, a, :], ident)
                        mm.then_inc(sem["tr_act"][d], 1)
                    for d in range(2):
                        pe.wait_ge(sem["state_pe"][d], 1)
                        pe.sem_inc(sem["state_pe"][d], -1)
                        for a in range(2):
                            pe.matmul(B[d][2][:, a * P:(a + 1) * P], state[:, d, a, :], qp[:, d, a, :],
                                      start=(a == 0), stop=False, skip_group_check=True)
                        pe.wait_ge(sem["attn_pe"][d], 1)
                        pe.sem_inc(sem["attn_pe"][d], -1)
                        pe.wait_ge(sem["tok_pe"][d], 1)
                        pe.sem_inc(sem["tok_pe"][d], -1)
                        for h in range(H):
                            a, p = h // 2, h % 2
                            mm = pe.matmul(B[d][2][HD * p:HD * (p + 1), a * P:(a + 1) * P],
                                           vt[:, d, a, HD * p:HD * (p + 1)], attn[:, d, h, :],
                                           start=False, stop=True, skip_group_check=True)
                        mm.then_inc(sem["o_act"][d], 1)
                        for a in range(2):
                            mm = pe.matmul(B[d][3][:, a * P:(a + 1) * P], krt[:, d, a, :], vt[:, d, a, :],
                                           start=True, stop=True)
                        mm.then_inc(sem["su_dve"][d], 1)


def hgrn_group(k):
    with k.phase() as st:
        both = k.sb(st, "both", [P, 2, 2, T])
        with ExitStack() as inner:
            q, v = k.sb(inner, "q", [P, 2, T]), k.sb(inner, "v", [P, 2, T])
            f, kk = k.sb(inner, "f", [P, 4, T]), k.sb(inner, "kk", [P, 4, T])
            hgrn_rows_phase(k, q, f, kk, v)
            hgrn_phase(k, q, f, kk, v, both)
        gate_phase(k, both, 6, T_HG, V_HNORM)


def attention_phase(k, q, kT, vt, oT_tile, window, band, sink, with_ctx):
    with k.phase() as st:
        qs = k.sb(st, "qs", [P, 2, P])
        near = k.sb(st, "near", [P, 2, 3 * P])
        prob = k.sb(st, "prob", [P, 2, T])
        probT = k.sb(st, "probT", [P, 2, NT, P])
        otok = k.sb(st, "otok", [P, 2 * P])
        mx = k.sb(st, "mx", [P, 2, 2])
        tot = k.sb(st, "tot", [P, 2, 2])
        ps = [k.banks(st, f"score{s}", 3) for s in range(2)]
        turned_ps = k.banks(st, "turned", 1)
        out_ps = k.banks(st, "out", 1)
        q_pe = k.sem(st, "q_pe")
        names = "score_dve mx_act prob_pe sum_dve turn_full turn_free".split()
        sem = {n: k.sems(st, n, 2) for n in names}
        out_dve, out_free, otok_pe, turn_out, out_taken = (
            k.sem(st, n) for n in ("out_dve", "out_free", "otok_pe", "turn_out", "out_taken"))
        own = {e: k.sem(st, f"own_{e}") for e in ("act", "dve")}
        scale = HD ** -0.5

        def width(kind):
            return {"ctx": CTX, "all": T, "first": CTX + 2 * P, "last": CTX + 2 * P, "middle": CTX + 3 * P}[kind]

        def score_parts(x, g, parity, kind):
            rows = slice(HD * g, HD * (g + 1))
            query = qs[rows, x, :]
            if kind == "all":
                return [(lo, query, kT[rows, lo:lo + w]) for lo, w in SEGS]
            parts = [(256, query, kT[rows, SEQ:T])]
            if kind != "ctx":
                parts.append((512, query, near[rows, parity, 0:width(kind) - CTX]))
            if window:
                parts.append((256 + width(kind), k.consts[rows, C_ONES:C_ONES + P], sink[rows, 2 * g + x:2 * g + x + 1]))
            return parts

        def span(kind):
            lo = 0 if kind == "all" else 256
            return lo, lo + width(kind) + (1 if window else 0)

        def key_chunk(chunk, kind, j):
            if kind == "all":
                return j
            if j < CTX // P:
                return SEQ // P + j
            return chunk + j - CTX // P - (0 if kind == "first" else 1)

        def batches(kind):
            n = width(kind) // P
            size = 4 if n > 5 else (n + 1) // 2 if n > 2 else n
            return [(c, min(size, n - c), i % 2) for i, c in enumerate(range(0, n, size))]

        def columns(chunk):
            return bass.ds(chunk * P, P)

        def score_product(pe, part, g, last):
            col, stationary, moving = part
            mm = pe.matmul(ps[g][:, col:col + moving.shape[1]], stationary, moving, start=True, stop=True)
            if last:
                mm.then_inc(sem["score_dve"][g], 1)

        def tensor_first(pe, chunk, parity, kind):
            pe.wait_ge(q_pe, 1)
            pe.sem_inc(q_pe, -1)
            for g in range(2):
                parts = score_parts(0, g, parity, kind)
                for i, part in enumerate(parts):
                    score_product(pe, part, g, i == len(parts) - 1)

        def tensor_out(pe):
            pe.wait_ge(otok_pe, 1)
            pe.sem_inc(otok_pe, -1)
            for a in range(2):
                mm = pe.transpose(turned_ps[:, a * P:(a + 1) * P], otok[:, a * P:(a + 1) * P], k.const(C_IDENT))
            mm.then_inc(turn_out, 1)
            pe.wait_ge(out_taken, 1)
            pe.sem_inc(out_taken, -1)

        def tensor_step(pe, prev, cur, nxt):
            chunk, parity, kind = cur
            for h in range(4):
                x, g = h // 2, h % 2
                if h < 2:
                    parts = score_parts(1, g, parity, kind)
                else:
                    parts = score_parts(0, g, nxt[1], nxt[2]) if nxt else []
                if h % 2 == 0 and parts:
                    pe.wait_ge(q_pe, 1)
                    pe.sem_inc(q_pe, -1)
                pe.wait_ge(sem["prob_pe"][g], 1)
                pe.sem_inc(sem["prob_pe"][g], -1)
                turns = batches(kind)
                done = 0
                for i, (c, n, b) in enumerate(turns):
                    for j in range(c, c + n):
                        mm = pe.transpose(turned_ps[:, (j - c) * P:(j - c + 1) * P], prob[:, g, j * P:(j + 1) * P],
                                          k.const(C_IDENT))
                    mm.then_inc(sem["turn_full"][b], 1)
                    if done < len(parts):
                        score_product(pe, parts[done], g, done == len(parts) - 1)
                        done += 1
                    pe.wait_ge(sem["turn_free"][b], 1)
                    pe.sem_inc(sem["turn_free"][b], -1)
                if h == 0 and prev is not None:
                    tensor_out(pe)
                while done < len(parts):
                    score_product(pe, parts[done], g, done == len(parts) - 1)
                    done += 1
                pe.wait_ge(out_free, 1)
                pe.sem_inc(out_free, -1)
                for j in range(width(kind) // P):
                    mm = pe.matmul(out_ps[:, 0:HD], probT[:, g, j, :],
                                   vt[:, key_chunk(chunk, kind, j), HD * g:HD * (g + 1)],
                                   start=(j == 0), stop=(j == width(kind) // P - 1))
                mm.then_inc(out_dve, 1)

        def exponentials(act, g, kind):
            lo, hi = span(kind)
            act.wait_ge(sem["mx_act"][g], 1)
            act.sem_inc(sem["mx_act"][g], -1)
            act.activation(prob[:, g, 0:hi - lo], ps[g][:, lo:hi], ACT.Exp, bias=mx[:, g, 1:2],
                           scale=scale, accum_out=tot[:, g, 0:1]).then_inc(own["act"], 1)
            act.wait_ge(own["act"], 1)
            act.sem_inc(own["act"], -1)
            act.sem_inc(sem["prob_pe"][g], 1)
            act.sem_inc(sem["sum_dve"][g], 1)

        def copy_near(act, cur):
            chunk, parity, kind = cur
            if window and kind != "ctx":
                start = (chunk if kind == "first" else chunk - 1) * P
                w = width(kind) - CTX
                act.activation(near[:, parity, 0:w], kT[:, bass.ds(start, w)], ACT.Copy)

        def scalar_first(act, cur):
            copy_near(act, cur)
            act.activation(qs[:, 1, :], q[:, 1, columns(cur[0])], ACT.Copy)
            act.activation(qs[:, 0, :], q[:, 0, columns(cur[0])], ACT.Copy).then_inc(own["act"], 1)
            act.wait_ge(own["act"], 1)
            act.sem_inc(own["act"], -1)
            act.sem_inc(q_pe, 1)
            act.sem_inc(q_pe, 1)
            for g in range(2):
                exponentials(act, g, cur[2])

        def scalar_out(act, prev):
            act.wait_ge(turn_out, 1)
            act.sem_inc(turn_out, -1)
            act.activation(k.oT[:, oT_tile:oT_tile + 2, columns(prev[0])],
                           turned_ps[:, 0:2 * P].rearrange("p (a f) -> p a f", f=P), ACT.Copy)\
                .then_inc(own["act"], 1)
            act.wait_ge(own["act"], 1)
            act.sem_inc(own["act"], -1)
            act.sem_inc(out_taken, 1)

        def turn(eng, g, b, kind, copy, name):
            for c, n, bb in batches(kind):
                if bb == b:
                    eng.wait_ge(sem["turn_full"][b], 1)
                    eng.sem_inc(sem["turn_full"][b], -1)
                    copy(probT[:, g, c:c + n, :],
                         turned_ps[:, 0:n * P].rearrange("p (c f) -> p c f", f=P)).then_inc(own[name], 1)
                    eng.wait_ge(own[name], 1)
                    eng.sem_inc(own[name], -1)
                    eng.sem_inc(sem["turn_free"][b], 1)

        def scalar_step(act, prev, cur, nxt):
            for h in range(4):
                g = h % 2
                turn(act, g, 0, cur[2], lambda o, s: act.activation(o, s, ACT.Copy), "act")
                if h == 0 and prev is not None:
                    scalar_out(act, prev)
                if h == 0 and nxt:
                    copy_near(act, nxt)
                if h < 2:
                    exponentials(act, g, cur[2])
                elif nxt:
                    exponentials(act, g, nxt[2])
                if h % 2 and nxt:
                    act.activation(qs[:, h // 2, :], q[:, h // 2, columns(nxt[0])], ACT.Copy).then_inc(own["act"], 1)
                    act.wait_ge(own["act"], 1)
                    act.sem_inc(own["act"], -1)
                    act.sem_inc(q_pe, 1)

        def maximum(dve, g, kind):
            lo, hi = span(kind)
            dve.wait_ge(sem["score_dve"][g], 1)
            dve.sem_inc(sem["score_dve"][g], -1)
            for col, m in {"first": [(512 + P, 2)], "last": [(512, 0)],
                           "middle": [(512, 0), (512 + 2 * P, 2)]}.get(kind, []):
                part = ps[g][:, col:col + P]
                dve.tensor_tensor(part, part, band[:, m * P:(m + 1) * P], ALU.add).then_inc(own["dve"], 1)
                dve.wait_ge(own["dve"], 1)
                dve.sem_inc(own["dve"], -1)
            dve.reduce_max(mx[:, g, 0:1], ps[g][:, lo:hi], AX_X).then_inc(own["dve"], 1)
            dve.wait_ge(own["dve"], 1)
            dve.sem_inc(own["dve"], -1)
            dve.tensor_scalar(mx[:, g, 1:2], mx[:, g, 0:1], -scale, None, ALU.mult).then_inc(own["dve"], 1)
            dve.wait_ge(own["dve"], 1)
            dve.sem_inc(own["dve"], -1)
            dve.sem_inc(sem["mx_act"][g], 1)

        def vector_first(dve, cur):
            for g in range(2):
                maximum(dve, g, cur[2])

        def vector_step(dve, prev, cur, nxt):
            for h in range(4):
                x, g = h // 2, h % 2
                head = 2 * g + x
                dve.wait_ge(sem["sum_dve"][g], 1)
                dve.sem_inc(sem["sum_dve"][g], -1)
                dve.reciprocal(tot[:, g, 1:2], tot[:, g, 0:1]).then_inc(own["dve"], 1)
                dve.wait_ge(own["dve"], 1)
                dve.sem_inc(own["dve"], -1)
                turn(dve, g, 1, cur[2], dve.tensor_copy, "dve")
                if h < 2:
                    maximum(dve, g, cur[2])
                elif nxt:
                    maximum(dve, g, nxt[2])
                dve.wait_ge(out_dve, 1)
                dve.sem_inc(out_dve, -1)
                dve.tensor_scalar(otok[:, head * HD:(head + 1) * HD], out_ps[:, 0:HD], tot[:, g, 1:2],
                                  None, ALU.mult).then_inc(own["dve"], 1)
                dve.wait_ge(own["dve"], 1)
                dve.sem_inc(own["dve"], -1)
                dve.sem_inc(out_free, 1)
            dve.sem_inc(otok_pe, 1)

        last_latent = SEQ // P - 1
        tail = [(c, 0, "ctx") for c in range(SEQ // P, NT)] if with_ctx else []

        def chunks(eng, step):
            if window:
                step(eng, None, (0, 0, "first"), (1, 1, "middle"))
                with eng.Fori(0, 2) as i:
                    for u in range(2):
                        step(eng, (2 * i + u, u, ""), (2 * i + u + 1, 1 - u, "middle"), (2 * i + u + 2, u, "middle"))
                step(eng, (4, 0, ""), (5, 1, "middle"), (6, 0, "middle"))
                step(eng, (5, 1, ""), (6, 0, "middle"), (7, 1, "last"))
                step(eng, (6, 0, ""), (7, 1, "last"), tail[0] if tail else None)
            else:
                step(eng, None, (0, 0, "all"), (1, 0, "all"))
                with eng.Fori(1, last_latent) as i:
                    step(eng, (i - 1, 0, ""), (i, 0, "all"), (i + 1, 0, "all"))
                step(eng, (last_latent - 1, 0, ""), (last_latent, 0, "all"), tail[0] if tail else None)
            for n, cur in enumerate(tail):
                step(eng, (cur[0] - 1, 0, ""), cur, tail[n + 1] if n + 1 < len(tail) else None)

        first = (0, 0, "first" if window else "all")
        final = (tail[-1] if tail else (last_latent, 0, ""))
        with k.nc.Block() as block:
            @block.tensor
            def _(pe):
                tensor_first(pe, *first)
                chunks(pe, tensor_step)
                tensor_out(pe)

            @block.scalar
            def _(act):
                scalar_first(act, first)
                chunks(act, scalar_step)
                scalar_out(act, final)

            @block.vector
            def _(dve):
                dve.sem_inc(out_free, 1)
                vector_first(dve, first)
                chunks(dve, vector_step)
                dve.wait_ge(out_free, 1)
                dve.sem_inc(out_free, -1)


def trig_phase(k, a, trig):
    with k.phase() as st:
        came = k.sem(st, "came")
        with k.nc.Block() as block:
            @block.sync
            def _(sp):
                sp.dma_start(trig[:, :], a["consts"][:, N_MIX:NC]).then_inc(came, 16)
                sp.wait_ge(came, 16)
                sp.sem_inc(came, -16)


def attention_groups(k, a, with_ctx):
    with k.phase() as st:
        table = k.sb(st, "trig", [P, NC - N_MIX])
        band, trig = table[:, 0:3 * P], table[:, 3 * P:]
        trig_phase(k, a, table)
        for window, tq, tk, tv, out in ((False, T_BQ, T_BK, T_BV, 2), (True, T_CQ, T_CK, T_CV, 4)):
            with ExitStack() as inner:
                k.count += 1
                q = k.sb(inner, "q", [P, 2, T])
                kT = k.sb(inner, "kT", [P, T])
                vT = k.sb(inner, "vT", [P, T])
                vt = k.sb(inner, "vt", [P, NT, P])
                jobs = [Job(tq, q[:, 0, :], rope=True), Job(tq + 1, q[:, 1, :], rope=True), Job(tk, kT[:, :], rope=True)]
                if not window:
                    for job, col in zip(jobs, (V_QNORM, V_QNORM, V_KNORM)):
                        job.width, job.factor = HD, k.vec(col)
                jobs.append(Job(tv, vT[:, :], to_tokens=vt))
                rows_phase(k, jobs, trig)
                attention_phase(k, q, kT, vt, out, window, band, k.sink, with_ctx)


def ffn_phase(k, a, layer, n):
    with k.phase() as st:
        f = k.xT
        wu_hi = k.sb(st, "wu_hi", [P, 2, KD, P], F32R)
        wu_raw, wu_lo = k.twin(st, "wu_raw", [P, 2, KD, P])
        wd_hi = k.sb(st, "wd_hi", [P, FG, D_MODEL], F32R)
        wd_raw, wd_lo = k.twin(st, "wd_raw", [P, FG, D_MODEL])
        g_hi = k.sb(st, "g_hi", [P, 2, FG, T], F32R)
        g_whole, g_lo = k.twin(st, "g_whole", [P, 2, FG, T])
        y = k.sb(st, "y", [P, 2, T])
        ps = [k.banks(st, f"ps{s}", 3) for s in range(2)]
        wu_in, wu_free, wu_pool, wu_pe = (k.sems(st, s, 2) for s in ("wu_in", "wu_free", "wu_pool", "wu_pe"))
        wd_in, wd_free, wd_pool, wd_pe = (k.sems(st, s, 2) for s in ("wd_in", "wd_free", "wd_pool", "wd_pe"))
        up_act, down_dve, ps_free, centre_dve, y_free = (
            k.sems(st, s, 2) for s in ("up_act", "down_dve", "ps_free", "centre_dve", "y_free"))
        taps_act, gate_pool, value_pool, whole_act, hi_pool, g_pe = (
            k.sem(st, s) for s in ("taps_act", "gate_pool", "value_pool", "whole_act", "hi_pool", "g_pe"))
        own = {e: k.sem(st, f"own_{e}") for e in ("act", "dve", "pool")}
        parts = conv_parts(n)

        def load_up(sp, j, u, s):
            sp.wait_ge(wu_free[s], 1)
            sp.sem_inc(wu_free[s], -1)
            sp.dma_start(wu_raw[:, s], a["w_up"][layer, s * KF + j * FG + u]).then_inc(wu_in[s], 16)

        def load_down(sp, j):
            for u in range(FG):
                sp.wait_ge(wd_free[u], 1)
                sp.sem_inc(wd_free[u], -1)
                sp.dma_start(wd_raw[:, u], a["w_down"][layer, j * FG + u]).then_inc(wd_in[u], 16)

        def sync_group(sp, j, first=False, last=False):
            if not first:
                load_down(sp, j - 1)
            for s in range(2):
                load_up(sp, j, 1, s)
            if not last:
                for s in range(2):
                    load_up(sp, j + 1, 0, s)

        def tensor_up(pe):
            for u in range(FG):
                for s in range(2):
                    pe.wait_ge(wu_pe[s], 1)
                    pe.sem_inc(wu_pe[s], -1)
                    pe.wait_ge(ps_free[s], 1)
                    pe.sem_inc(ps_free[s], -1)
                    split_products(pe, ps[s], (wu_hi[:, s], wu_lo[:, s]), (k.hi, k.lo), KD, n)\
                        .then_inc(up_act[s], 1)

        def tensor_down(pe, parity):
            for u in range(FG):
                pe.wait_ge(wd_pe[u], 1)
                pe.sem_inc(wd_pe[u], -1)
            pe.wait_ge(g_pe, FG)
            pe.sem_inc(g_pe, -FG)
            for o in range(KD):
                s, cols = o % 2, slice(o * P, (o + 1) * P)
                pe.wait_ge(ps_free[s], 1)
                pe.sem_inc(ps_free[s], -1)
                split_products(pe, ps[s], (wd_hi[:, :, cols], wd_lo[:, :, cols]), (g_hi[:, parity], g_lo[:, parity]),
                               FG, n).then_inc(down_dve[s], 1)

        def round_up(act, s):
            act.wait_ge(wu_in[s], 16)
            act.sem_inc(wu_in[s], -16)
            act.activation(wu_hi[:, s], wu_raw[:, s], ACT.Copy).then_inc(own["act"], 1)
            act.wait_ge(own["act"], 1)
            act.sem_inc(own["act"], -1)
            act.sem_inc(wu_pool[s], 1)

        def round_down(act):
            for u in range(FG):
                act.wait_ge(wd_in[u], 16)
                act.sem_inc(wd_in[u], -16)
                act.activation(wd_hi[:, u], wd_raw[:, u], ACT.Copy).then_inc(own["act"], 1)
                act.wait_ge(own["act"], 1)
                act.sem_inc(own["act"], -1)
                act.sem_inc(wd_pool[u], 1)

        def centre(act, j, u, s):
            act.wait_ge(up_act[s], 1)
            act.sem_inc(up_act[s], -1)
            act.sem_inc(wu_free[s], 1)
            act.wait_ge(y_free[s], 1)
            act.sem_inc(y_free[s], -1)
            act.activation(k.taps[:, s, 0:4], k.vecs[:, bass.ds(V_FCONV + s * KF + j * FG + u, 4, 2 * KF)],
                           ACT.Copy).then_inc(own["act"], 1)
            act.wait_ge(own["act"], 1)
            act.sem_inc(own["act"], -1)
            act.activation(y[:, s, 0:n], ps[s][:, 0:n], ACT.Identity, scale=k.taps[:, s, 1:2],
                           bias=k.taps[:, s, 3:4]).then_inc(own["act"], 1)
            act.wait_ge(own["act"], 1)
            act.sem_inc(own["act"], -1)
            act.sem_inc(centre_dve[s], 1)

        def scalar_group(act, j, parity, first=False, last=False):
            for u in range(FG):
                more = u == 0 or not last
                centre(act, j, u, 0)
                if more:
                    round_up(act, 0)
                act.wait_ge(taps_act, 1)
                act.sem_inc(taps_act, -1)
                act.activation(y[:, 0, 0:n], y[:, 0, 0:n], ACT.Silu).then_inc(own["act"], 1)
                act.wait_ge(own["act"], 1)
                act.sem_inc(own["act"], -1)
                act.sem_inc(gate_pool, 1)
                centre(act, j, u, 1)
                if more:
                    round_up(act, 1)
                if u == 0 and not first:
                    round_down(act)
                act.wait_ge(whole_act, 1)
                act.sem_inc(whole_act, -1)
                act.activation(g_hi[:, parity, u, 0:n], g_whole[:, parity, u, 0:n], ACT.Copy).then_inc(own["act"], 1)
                act.wait_ge(own["act"], 1)
                act.sem_inc(own["act"], -1)
                act.sem_inc(hi_pool, 1)

        def vector_up(dve):
            for u in range(FG):
                for s in range(2):
                    dve.wait_ge(centre_dve[s], 1)
                    dve.sem_inc(centre_dve[s], -1)
                    for lo, hi in parts:
                        dve.scalar_tensor_tensor(y[:, s, lo + 1:hi], ps[s][:, lo:hi - 1],
                                                 k.taps[:, s, 0:1], y[:, s, lo + 1:hi],
                                                 ALU.mult, ALU.add).then_inc(own["dve"], 1)
                        dve.wait_ge(own["dve"], 1)
                        dve.sem_inc(own["dve"], -1)
                        dve.scalar_tensor_tensor(y[:, s, lo:hi - 1], ps[s][:, lo + 1:hi],
                                                 k.taps[:, s, 2:3], y[:, s, lo:hi - 1],
                                                 ALU.mult, ALU.add).then_inc(own["dve"], 1)
                        dve.wait_ge(own["dve"], 1)
                        dve.sem_inc(own["dve"], -1)
                    dve.sem_inc(ps_free[s], 1)
                    dve.sem_inc(value_pool if s else taps_act, 1)

        def vector_down(dve):
            for o in range(KD):
                s = o % 2
                dve.wait_ge(down_dve[s], 1)
                dve.sem_inc(down_dve[s], -1)
                if o == KD - 1:
                    for u in range(FG):
                        dve.sem_inc(wd_free[u], 1)
                dve.tensor_tensor(f[:, o, 0:n], ps[s][:, 0:n], f[:, o, 0:n], ALU.add).then_inc(own["dve"], 1)
                dve.wait_ge(own["dve"], 1)
                dve.sem_inc(own["dve"], -1)
                dve.sem_inc(ps_free[s], 1)

        def rest_up(pool, s):
            pool.wait_ge(wu_pool[s], 1)
            pool.sem_inc(wu_pool[s], -1)
            pool.tensor_tensor(wu_lo[:, s], wu_raw[:, s], wu_hi[:, s].bitcast(F32), ALU.subtract)\
                .then_inc(own["pool"], 1)
            pool.wait_ge(own["pool"], 1)
            pool.sem_inc(own["pool"], -1)
            pool.sem_inc(wu_pe[s], 1)

        def rest_down(pool):
            for u in range(FG):
                pool.wait_ge(wd_pool[u], 1)
                pool.sem_inc(wd_pool[u], -1)
                pool.tensor_tensor(wd_lo[:, u], wd_raw[:, u], wd_hi[:, u].bitcast(F32), ALU.subtract)\
                    .then_inc(own["pool"], 1)
                pool.wait_ge(own["pool"], 1)
                pool.sem_inc(own["pool"], -1)
                pool.sem_inc(wd_pe[u], 1)

        def pool_group(pool, parity, first=False, last=False):
            for u in range(FG):
                if u == 0 or not last:
                    for s in range(2):
                        rest_up(pool, s)
                pool.wait_ge(gate_pool, 1)
                pool.sem_inc(gate_pool, -1)
                pool.wait_ge(value_pool, 1)
                pool.sem_inc(value_pool, -1)
                pool.tensor_tensor(g_whole[:, parity, u, 0:n], y[:, 0, 0:n], y[:, 1, 0:n], ALU.mult)\
                    .then_inc(own["pool"], 1)
                pool.wait_ge(own["pool"], 1)
                pool.sem_inc(own["pool"], -1)
                pool.sem_inc(y_free[0], 1)
                pool.sem_inc(y_free[1], 1)
                pool.sem_inc(whole_act, 1)
                if u == 0 and not first:
                    rest_down(pool)
                pool.wait_ge(hi_pool, 1)
                pool.sem_inc(hi_pool, -1)
                pool.tensor_tensor(g_lo[:, parity, u, 0:n], g_whole[:, parity, u, 0:n],
                                   g_hi[:, parity, u, 0:n].bitcast(F32), ALU.subtract).then_inc(own["pool"], 1)
                pool.wait_ge(own["pool"], 1)
                pool.sem_inc(own["pool"], -1)
                pool.sem_inc(g_pe, 1)

        with k.nc.Block() as block:
            @block.sync
            def _(sp):
                for s in range(2):
                    load_up(sp, 0, 0, s)
                sync_group(sp, 0, first=True)
                with sp.Fori(0, N_FG // 2 - 1) as i:
                    for b in range(2):
                        sync_group(sp, i * 2 + (1 + b))
                sync_group(sp, N_FG - 2)
                sync_group(sp, N_FG - 1, last=True)
                load_down(sp, N_FG - 1)

            @block.tensor
            def _(pe):
                tensor_up(pe)
                with pe.Fori(0, N_FG // 2) as i:
                    for b in range(2):
                        tensor_up(pe)
                        tensor_down(pe, b)
                tensor_down(pe, 0)

            @block.scalar
            def _(act):
                for s in range(2):
                    act.sem_inc(wu_free[s], 1)
                for s in range(2):
                    round_up(act, s)
                scalar_group(act, 0, 0, first=True)
                with act.Fori(0, N_FG // 2 - 1) as i:
                    for b in range(2):
                        scalar_group(act, i * 2 + (1 + b), 1 - b)
                scalar_group(act, N_FG - 2, 1)
                scalar_group(act, N_FG - 1, 0, last=True)
                round_down(act)
                for s in range(2):
                    act.wait_ge(wu_free[s], 1)
                    act.sem_inc(wu_free[s], -1)

            @block.vector
            def _(dve):
                for s in range(2):
                    dve.sem_inc(ps_free[s], 1)
                    dve.sem_inc(wd_free[s], 1)
                dve.memset(f[:, :, :], 0.0).then_inc(own["dve"], 1)
                dve.wait_ge(own["dve"], 1)
                dve.sem_inc(own["dve"], -1)
                vector_up(dve)
                with dve.Fori(0, N_FG // 2) as i:
                    for b in range(2):
                        vector_up(dve)
                        vector_down(dve)
                vector_down(dve)
                for s in range(2):
                    dve.wait_ge(ps_free[s], 1)
                    dve.sem_inc(ps_free[s], -1)
                    dve.wait_ge(wd_free[s], 1)
                    dve.sem_inc(wd_free[s], -1)

            @block.gpsimd
            def _(pool):
                for s in range(2):
                    pool.sem_inc(y_free[s], 1)
                for s in range(2):
                    rest_up(pool, s)
                pool_group(pool, 0, first=True)
                with pool.Fori(0, N_FG // 2 - 1) as i:
                    for b in range(2):
                        pool_group(pool, 1 - b)
                pool_group(pool, 1)
                pool_group(pool, 0, last=True)
                rest_down(pool)
                for s in range(2):
                    pool.wait_ge(y_free[s], 1)
                    pool.sem_inc(y_free[s], -1)


def store_phase(k, a):
    with k.phase() as st:
        done = k.sem(st, "done")
        with k.nc.Block() as block:
            @block.sync
            def _(sp):
                sp.dma_start(a["out"], k.xT[:, :, 0:SEQ]).then_inc(done, 16)
                sp.wait_ge(done, 16)
                sp.sem_inc(done, -16)


def build(nc, a):
    k = Chip(nc)
    with ExitStack() as st:
        k.rows = nc.dram_tensor("rows", (N_IN, P, T), F32).ap()
        k.x_dram = nc.dram_tensor("x_spilled", (P, KD, T), F32).ap()
        k.consts = k.sb(st, "consts", [P, N_BASE])
        k.vecs = k.sb(st, "vecs", [P, NV])
        k.mods = k.sb(st, "mods", [P, N_MOD * KD, 2])
        k.cact = k.sb(st, "cact", [P, KD, 2])
        k.lb = k.sb(st, "lb", [P, 8])
        k.expa = k.sb(st, "expa", [P, 1])
        k.sink = k.sb(st, "sink", [P, H])
        k.taps = k.sb(st, "taps", [P, 2, 4])
        k.xT = k.sb(st, "xT", [P, KD, T])
        load_phase(k, a)
        for layer in range(DEPTH):
            with_ctx = layer < DEPTH - 1
            n = T if with_ctx else SEQ
            modulation_phase(k, a, layer)
            with ExitStack() as mixers:
                k.count += 1
                k.mix = k.sb(mixers, "mix", [P, N_MIX - N_BASE])
                with ExitStack() as inner:
                    k.hi = k.sb(inner, "h_hi", [P, KD, T], F32R)
                    k.h, k.lo = k.twin(inner, "h_whole", [P, KD, T])
                    norm_phase(k, T, 0, 1)
                    input_projection_phase(k, a, layer)
                k.oT = k.sb(mixers, "oT", [P, KD, T])
                gdn_group(k)
                attention_groups(k, a, with_ctx)
                hgrn_group(k)
                with ExitStack() as inner:
                    k.count += 1
                    y = k.sb(inner, "mixed", [P, KD, T])
                    matmul_into_phase(k, a["w_out"][layer], KD, k.oT, y, n, add=False)
                    residual_phase(k, y, k.xT, n, 2)
            with ExitStack() as inner:
                k.count += 1
                k.hi = k.sb(inner, "h_hi", [P, KD, T], F32R)
                k.h, k.lo = k.twin(inner, "h_whole", [P, KD, T])
                norm_phase(k, n, 3, 4, spill=k.x_dram)
                ffn_phase(k, a, layer, n)
            with ExitStack() as inner:
                k.count += 1
                x = k.sb(inner, "x_old", [P, KD, T])
                residual_phase(k, k.xT, x, n, 5, reload=k.x_dram)
        store_phase(k, a)


def layouts(x, c, ctx, c_ctx, ada_w, ada_b, norm_pre_mix, norm_post_mix, norm_pre_ffn, norm_post_ffn,
            w_in, w_out, gdn_conv_w, gdn_a_log, gdn_dt_bias, gdn_norm, attn_q_norm, attn_k_norm,
            swa_sink, hgrn_lb_raw, hgrn_norm, ffn_w_up, ffn_conv_w, ffn_conv_b, ffn_w_down):
    def cols(v):
        return np.asarray(v).reshape(-1, P).T

    def tiles(w, n_k):
        return np.asarray(w).reshape(n_k, P, -1, P).transpose(2, 1, 0, 3)

    out = {"xT": np.concatenate([np.asarray(x)[0], np.asarray(ctx)[0]]).T.reshape(KD, P, T).transpose(1, 0, 2)}
    out["cond"] = np.stack([np.asarray(c)[0], np.asarray(c_ctx)]).reshape(2, KD, P).transpose(2, 1, 0)
    out["ada_w"] = np.asarray(ada_w).reshape(DEPTH, KD, P, -1, 512).transpose(0, 3, 2, 1, 4)
    heads = [0, 2, 1, 3]
    w_in, vecs, ins = np.asarray(w_in), [], []
    for l in range(DEPTH):
        w = w_in[l]
        qkv_z, beta, a, rest = w[:, :1024], w[:, 1024:1032], w[:, 1032:1040], w[:, 1040:].copy()
        for at in (0, 512):
            q = rest[:, at:at + 256].reshape(-1, H, HD)[:, heads]
            rest[:, at:at + 256] = q.reshape(-1, 256)
        last = np.zeros((D_MODEL, P), w.dtype)
        last[:, BETA_ROW:BETA_ROW + 8] = beta
        last[:, G_ROW:G_ROW + 8] = a
        ins.append(tiles(np.concatenate([qkv_z, rest, last], 1), KD))
        v = np.zeros((P, NV), np.float32)
        v[:, V_ADAB:V_ADAB + 48] = cols(ada_b[l])
        for col, vec in ((V_PRE_MIX, norm_pre_mix), (V_POST_MIX, norm_post_mix), (V_PRE_FFN, norm_pre_ffn),
                         (V_POST_FFN, norm_post_ffn)):
            v[:, col:col + KD] = cols(vec[l])
        v[:, V_GCONV:V_GCONV + 18] = cols(gdn_conv_w[l])
        v[:, V_FCONV:V_FCONV + 6 * KF] = cols(ffn_conv_w[l])
        v[:, V_FBIAS:V_FBIAS + 2 * KF] = cols(ffn_conv_b[l])
        for col, vec in ((V_GNORM, gdn_norm), (V_QNORM, attn_q_norm), (V_KNORM, attn_k_norm), (V_HNORM, hgrn_norm)):
            v[:HD, col] = vec[l]
            v[HD:, col] = vec[l]
        v[G_ROW:G_ROW + 8, V_ALOG] = np.asarray(gdn_a_log[l]).reshape(-1)
        v[G_ROW:G_ROW + 8, V_DTB] = np.asarray(gdn_dt_bias[l]).reshape(-1)
        v[:, V_LB:V_LB + 8] = cols(hgrn_lb_raw)
        v[::HD, V_SINK:V_SINK + H] = np.asarray(swa_sink[l])[None, :]
        vecs.append(v)
    out["w_in"], out["vecs"] = np.stack(ins), np.stack(vecs)
    out["w_out"] = np.stack([tiles(w, KD) for w in np.asarray(w_out)])
    out["w_up"] = np.stack([tiles(w, KD) for w in np.asarray(ffn_w_up)])
    out["w_down"] = np.asarray(ffn_w_down).reshape(DEPTH, KF, P, D_MODEL)
    out["consts"] = constants()
    return {n: np.ascontiguousarray(v) for n, v in out.items()}


def kernel(**inputs):
    import concourse.bacc as bacc
    from concourse.bass_utils import run_bass_kernel_spmd

    nc = bacc.Bacc("TRN2", target_bir_lowering=False, num_devices=1)
    arrays = {f"in_{n}_dram": v for n, v in layouts(**inputs).items()}
    aps = {n[3:-5]: nc.dram_tensor(n, v.shape, mybir.dt.from_np(v.dtype), kind="ExternalInput").ap()
           for n, v in arrays.items()}
    aps["out"] = nc.dram_tensor("out_0_dram", (P, KD, SEQ), F32, kind="ExternalOutput").ap()
    build(nc, aps)
    r = run_bass_kernel_spmd(nc, [arrays], core_ids=[0])
    got = r.results[0]["out_0_dram"]
    return got.transpose(1, 0, 2).reshape(D_MODEL, SEQ).T.reshape(1, SEQ, D_MODEL)
```

```python
from contextlib import ExitStack

import numpy as np

import concourse.bass as bass
from concourse import mybir

ALU = mybir.AluOpType
ACT = mybir.ActivationFunctionType
F32 = mybir.dt.float32
F32R = mybir.dt.float32r
U32 = mybir.dt.uint32
AX_X = mybir.AxisListType.X

P = 128
D_MODEL = 1024
SEQ = 1024
CTX = 256
T = SEQ + CTX
DEPTH = 2
HD = 64
H = 4
KD = D_MODEL // P
NT = T // P
D_FF = 2816
KF = D_FF // P
FG = 2
N_FG = KF // FG
N_MOD = 6
EPS = 1e-6
NEG = -1e30
LEVELS = 7

T_GDN, T_Z, T_BQ, T_BK, T_BV, T_CQ, T_CK, T_CV, T_HQ, T_HF, T_HI, T_HG, T_BETA = (
    0, 6, 8, 10, 11, 12, 14, 15, 16, 18, 22, 24, 26)
N_IN = 27
BETA_ROW, G_ROW = 0, 32

V_PRE_MIX = 0
V_POST_MIX = V_PRE_MIX + KD
V_PRE_FFN = V_POST_MIX + KD
V_POST_FFN = V_PRE_FFN + KD
V_GCONV = V_POST_FFN + KD
V_FCONV = V_GCONV + 18
V_FBIAS = V_FCONV + 3 * 2 * KF
V_GNORM = V_FBIAS + 2 * KF
V_QNORM = V_GNORM + 1
V_KNORM = V_QNORM + 1
V_HNORM = V_KNORM + 1
V_ALOG = V_HNORM + 1
V_DTB = V_ALOG + 1
V_LB = V_DTB + 1
V_SINK = V_LB + DEPTH * 4
NV = V_SINK + H

N_FIRST = 2 * KD
ITEM = (2, 1)
ITEM_START = (N_FIRST, N_FIRST + N_IN * ITEM[0])
N_BLOCKS = ITEM_START[1] + N_IN * ITEM[1]

C_IDENT = 0
C_ONES = C_IDENT + P
C_BLK = C_ONES + P
C_ROT = C_BLK + P
C_CUM = C_ROT + P
C_STR = C_CUM + 2 * P
C_LVL = C_STR + 2 * P
C_BAND = C_LVL + 2 * LEVELS * P
C_COS = C_BAND + 3 * P
C_SIN = C_COS + SEQ
NC = C_SIN + SEQ
N_BASE = C_ROT
N_MIX = C_BAND
SEGS = ((0, 512), (512, 512), (1024, 256))


def constants():
    i = np.arange(P)
    c = np.zeros((P, NC), np.float32)
    c[:, C_IDENT:C_IDENT + P] = np.eye(P)
    c[:, C_ONES:C_ONES + P] = 1
    c[:, C_BLK:C_BLK + P] = (i[:, None] // HD) == (i[None, :] // HD)
    for m in range(0, P, 2):
        c[m + 1, C_ROT + m] = -1
        c[m, C_ROT + m + 1] = 1
    a, b = i[:, None], i[None, :]
    c[:, C_CUM:C_CUM + P] = a <= b
    c[:, C_CUM + P:C_CUM + 2 * P] = a >= b
    c[:, C_STR:C_STR + P] = a > b
    c[:, C_STR + P:C_STR + 2 * P] = a < b
    for l in range(LEVELS):
        x, y = a >> l, b >> l
        even_odd = (x % 2 == 0) & (y == x + 1)
        c[:, C_LVL + l * P:C_LVL + (l + 1) * P] = even_odd
        c[:, C_LVL + (LEVELS + l) * P:C_LVL + (LEVELS + l + 1) * P] = even_odd.T
    c[:, C_BAND:C_BAND + P] = np.where(b >= a, 0, NEG)
    c[:, C_BAND + 2 * P:C_BAND + 3 * P] = np.where(b <= a, 0, NEG)
    n_freq = HD // 4
    inv = (1.0 / (np.float32(10000.0) ** (np.arange(n_freq, dtype=np.float32) / np.float32(n_freq)))).astype(np.float32)
    pos = np.arange(SEQ)
    ang = np.concatenate([(pos // 64).astype(np.float32)[:, None] * inv,
                          (pos % 64).astype(np.float32)[:, None] * inv], axis=-1)
    pair = (i % HD) // 2
    c[:, C_COS:C_COS + SEQ] = np.cos(ang.astype(np.float64))[:, pair].T
    c[:, C_SIN:C_SIN + SEQ] = np.sin(ang.astype(np.float64))[:, pair].T
    return c



class Chip:

    def __init__(self, nc):
        self.nc = nc
        self.count = 0

    def phase(self):
        self.count += 1
        return ExitStack()

    def sb(self, stack, name, shape, dt=F32):
        return stack.enter_context(self.nc.sbuf_tensor(f"{name}_{self.count}", shape, dt))

    def twin(self, stack, name, shape):
        whole = self.sb(stack, name, shape)
        offset = self.nc.sbuf_base - 4 * int(np.prod(shape[1:]))
        return whole, self.nc.alloc_sbuf_tensor_at(f"{name}_rest_{self.count}", shape, F32R, offset=offset)

    def banks(self, stack, name, n):
        return stack.enter_context(self.nc.psum_tensor(f"{name}_{self.count}", [P, n * 512], F32))

    def sem(self, stack, name):
        return stack.enter_context(self.nc.semaphore(f"{name}_{self.count}"))

    def sems(self, stack, name, n):
        return [self.sem(stack, f"{name}{i}") for i in range(n)]

    def const(self, col, n=P):
        if col < N_BASE:
            return self.consts[:, col:col + n]
        return self.mix[:, col - N_BASE:col - N_BASE + n]

    def vec(self, col, n=1):
        return self.vecs[:, col:col + n]


def spread(ap, n):
    return ap.unsqueeze(1).to_broadcast([ap.shape[0], n, ap.shape[1]])


def widen(ap, n):
    return ap.unsqueeze(2).to_broadcast([ap.shape[0], ap.shape[1], n])


def load_phase(k, a):
    with k.phase() as st:
        own_a, vecs_dve, diff_act, own_v = (k.sem(st, s) for s in ("own_a", "vecs_dve", "diff_act", "own_v"))
        vecs_in, x_in = k.sem(st, "vecs_in"), k.sem(st, "x_in")
        with k.nc.Block() as block:
            @block.sync
            def _(sp):
                sp.dma_start(k.all_vecs[:, :, :], a["vecs"]).then_inc(vecs_in, 16)
                sp.dma_start(k.consts[:, :], a["consts"][:, 0:N_BASE]).then_inc(x_in, 16)
                sp.dma_start(k.ada_b[:, :], a["ada_b"]).then_inc(x_in, 16)
                sp.dma_start(k.xT[:, :, :], a["xT"]).then_inc(x_in, 16)
                sp.wait_ge(x_in, 48)
                sp.sem_inc(x_in, -48)

            @block.scalar
            def _(act):
                act.wait_ge(vecs_in, 16)
                act.sem_inc(vecs_in, -16)
                act.sem_inc(vecs_dve, 1)
                for l in range(DEPTH):
                    act.activation(k.all_sink[:, l], k.all_vecs[:, l, V_SINK:V_SINK + H], ACT.Copy,
                                   scale=float(HD ** 0.5))
                    act.activation(k.all_expa[:, l], k.all_vecs[:, l, V_ALOG:V_ALOG + 1], ACT.Exp).then_inc(own_a, 1)
                    act.wait_ge(own_a, 1)
                    act.sem_inc(own_a, -1)
                act.activation(k.all_expa[:, :, :], k.all_expa[:, :, :], ACT.Copy, scale=-1.0).then_inc(own_a, 1)
                act.wait_ge(own_a, 1)
                act.sem_inc(own_a, -1)
                act.wait_ge(diff_act, 1)
                act.sem_inc(diff_act, -1)
                act.activation(k.all_lb[:, 1, 4:8], k.all_lb[:, 1, 0:4], ACT.Sigmoid, scale=-1.0)
                act.activation(k.all_lb[:, 1, 0:4], k.all_lb[:, 1, 0:4], ACT.Sigmoid).then_inc(own_a, 1)
                act.wait_ge(own_a, 1)
                act.sem_inc(own_a, -1)

            @block.vector
            def _(dve):
                dve.memset(k.eps[:, :], EPS)
                dve.memset(k.all_lb[:, 0, 0:4], 0.0)
                dve.memset(k.all_lb[:, 0, 4:8], 1.0).then_inc(own_v, 1)
                dve.wait_ge(own_v, 1)
                dve.sem_inc(own_v, -1)
                dve.wait_ge(vecs_dve, 1)
                dve.sem_inc(vecs_dve, -1)
                dve.tensor_tensor(k.all_lb[:, 1, 0:4], k.all_vecs[:, 1, V_LB + 4:V_LB + 8],
                                  k.all_vecs[:, 1, V_LB:V_LB + 4], ALU.subtract).then_inc(own_v, 1)
                dve.wait_ge(own_v, 1)
                dve.sem_inc(own_v, -1)
                dve.sem_inc(diff_act, 1)


def modulation_blocks(dve, k, w, block, n, own):
    for q in range(n):
        for s in range(2):
            ins = dve.tensor_tensor_reduce(k.scratch[:, :], w[:, q, :], k.cact[:, s, :], 1.0, 0.0, ALU.mult, ALU.add,
                                           k.dots[:, q, s:s + 1])
            ins.then_inc(own, 1)
            dve.wait_ge(own, 1)
            dve.sem_inc(own, -1)
    dve.tensor_tensor(k.all_mods[:, bass.ds(block, n), :], k.dots[:, 0:n, :],
                      widen(k.ada_b[:, bass.ds(block, n)], 2), ALU.add).then_inc(own, 1)
    dve.wait_ge(own, 1)
    dve.sem_inc(own, -1)


def combine_gain(dve, k, layer, m, own):
    part = k.all_mods[:, (layer * N_MOD + m) * KD:(layer * N_MOD + m + 1) * KD, :]
    col = {1: V_PRE_MIX, 4: V_PRE_FFN, 2: V_POST_MIX, 5: V_POST_FFN}[m]
    if m in (1, 4):
        dve.tensor_scalar(part, part, 1.0, None, ALU.add).then_inc(own, 1)
        dve.wait_ge(own, 1)
        dve.sem_inc(own, -1)
    dve.tensor_tensor(part, part, widen(k.all_vecs[:, layer, col:col + KD], 2), ALU.mult).then_inc(own, 1)
    dve.wait_ge(own, 1)
    dve.sem_inc(own, -1)


def token_parts(n):
    return [(0, SEQ, 0)] + ([(SEQ, n, 1)] if n > SEQ else [])


def row_factor(k, act, own, out, sums, width):
    act.activation(out, sums, ACT.Ln, scale=1.0 / width, bias=k.eps[:, 0:1]).then_inc(own, 1)
    act.wait_ge(own, 1)
    act.sem_inc(own, -1)
    act.activation(out, out, ACT.Exp, scale=-0.5).then_inc(own, 1)
    act.wait_ge(own, 1)
    act.sem_inc(own, -1)


class Norm:

    def __init__(self, k, st, n, m_shift, m_scale, sq, acc, r, ps, spill=None, ada=None):
        self.k, self.n, self.m_shift, self.m_scale = k, n, m_shift, m_scale
        self.sq, self.acc, self.r, self.ps, self.spill, self.ada = sq, acc, r, ps, spill, ada
        self.sq_full, self.sq_free = k.sems(st, "sq_full", 2), k.sems(st, "sq_free", 2)
        self.acc_pe, self.sum_act, self.root_dve = (k.sem(st, s) for s in ("acc_pe", "sum_act", "root_dve"))
        self.scaled, self.hi_dve, self.hi_pool = (k.sem(st, s) for s in ("scaled", "round_dve", "round_pool"))
        self.even_pe, self.odd_pe, self.spilled = k.sem(st, "even_pe"), k.sem(st, "odd_pe"), k.sem(st, "spilled")
        self.ada_in = k.sems(st, "ada_in", 4)
        self.own_a, self.own_v, self.own_p = (k.sem(st, s) for s in ("norm_act", "norm_dve", "norm_pool"))

    def load_ada(self, eng, quarters):
        for i in quarters:
            place, first, n = self.ada_parts[i]
            eng.dma_start(place, self.ada[:, first:first + n]).then_inc(self.ada_in[i], 16)

    def sync(self, sp):
        if self.ada is not None:
            self.load_ada(sp, (0, 2))
        if self.spill is not None:
            sp.dma_start(self.spill, self.k.xT[:, :, :]).then_inc(self.spilled, 16)

    def scalar(self, act, between):
        k, n, r = self.k, self.n, self.r
        if self.ada is not None:
            self.load_ada(act, (1, 3))
        for t in range(KD):
            if t >= 2:
                act.wait_ge(self.sq_free[t % 2], 1)
                act.sem_inc(self.sq_free[t % 2], -1)
            act.activation(self.sq[:, t % 2, 0:n], k.xT[:, t, 0:n], ACT.Square).then_inc(self.sq_full[t % 2], 1)
        between()
        act.wait_ge(self.sum_act, 1)
        act.sem_inc(self.sum_act, -1)
        row_factor(k, act, self.own_a, r[:, 0:n], self.ps[:, 0:n], D_MODEL)
        act.sem_inc(self.root_dve, 1)
        for t in range(KD):
            act.wait_ge(self.scaled, 1)
            act.sem_inc(self.scaled, -1)
            for lo, hi, s in token_parts(n):
                shift = k.mods[:, self.m_shift * KD + t, s:s + 1]
                act.activation(k.hi[:, t, lo:hi], k.h[:, t, lo:hi], ACT.Identity, bias=shift)
                last = act.activation(k.h[:, t, lo:hi], k.h[:, t, lo:hi], ACT.Identity, bias=shift)
            last.then_inc(self.own_a, 1)
            act.wait_ge(self.own_a, 1)
            act.sem_inc(self.own_a, -1)
            act.sem_inc(self.hi_dve if t % 2 else self.hi_pool, 1)

    def rest(self, eng, t, own, ready):
        k, n = self.k, self.n
        eng.tensor_tensor(k.lo[:, t, 0:n], k.h[:, t, 0:n], k.hi[:, t, 0:n].bitcast(F32), ALU.subtract)\
            .then_inc(own, 1)
        eng.wait_ge(own, 1)
        eng.sem_inc(own, -1)
        eng.sem_inc(ready, 1)

    def vector(self, dve, between):
        k, n, acc, r, own = self.k, self.n, self.acc, self.r, self.own_v
        for t in range(KD):
            dve.wait_ge(self.sq_full[t % 2], 1)
            dve.sem_inc(self.sq_full[t % 2], -1)
            if t == 0:
                ins = dve.tensor_copy(acc[:, 0:n], self.sq[:, 0, 0:n])
            else:
                ins = dve.tensor_tensor(acc[:, 0:n], acc[:, 0:n], self.sq[:, t % 2, 0:n], ALU.add)
            if t < KD - 2:
                ins.then_inc(own, 1)
                dve.wait_ge(own, 1)
                dve.sem_inc(own, -1)
                dve.sem_inc(self.sq_free[t % 2], 1)
            elif t < KD - 1:
                ins.then_inc(own, 1)
                dve.wait_ge(own, 1)
                dve.sem_inc(own, -1)
            else:
                ins.then_inc(own, 1)
                dve.wait_ge(own, 1)
                dve.sem_inc(own, -1)
                dve.sem_inc(self.acc_pe, 1)
        if self.ada is not None:
            dve.wait_ge(self.cond_dve, 1)
            dve.sem_inc(self.cond_dve, -1)
            for i in (0, 2, 1, 3):
                dve.wait_ge(self.ada_in[i], 16)
                dve.sem_inc(self.ada_in[i], -16)
                place, first, blocks = self.ada_parts[i]
                modulation_blocks(dve, k, place, first, blocks, own)
            combine_gain(dve, k, 0, 1, own)
        between()
        dve.wait_ge(self.root_dve, 1)
        dve.sem_inc(self.root_dve, -1)
        for t in range(KD):
            for lo, hi, s in token_parts(n):
                ins = dve.scalar_tensor_tensor(k.h[:, t, lo:hi], k.xT[:, t, lo:hi],
                                               k.mods[:, self.m_scale * KD + t, s:s + 1], r[:, lo:hi],
                                               ALU.mult, ALU.mult)
                if hi < n:
                    ins.then_inc(own, 1)
                    dve.wait_ge(own, 1)
                    dve.sem_inc(own, -1)
            ins.then_inc(self.scaled, 1)
            if t % 2 and t > 2:
                dve.wait_ge(self.hi_dve, 1)
                dve.sem_inc(self.hi_dve, -1)
                self.rest(dve, t - 2, own, self.odd_pe)
        dve.wait_ge(self.hi_dve, 1)
        dve.sem_inc(self.hi_dve, -1)
        self.rest(dve, KD - 1, own, self.odd_pe)

    def gpsimd(self, pool, between):
        between()
        for t in range(0, KD, 2):
            pool.wait_ge(self.hi_pool, 1)
            pool.sem_inc(self.hi_pool, -1)
            self.rest(pool, t, self.own_p, self.even_pe)

    def tensor(self, pe):
        pe.wait_ge(self.acc_pe, 1)
        pe.sem_inc(self.acc_pe, -1)
        for lo, w in SEGS:
            if lo < self.n:
                mm = pe.matmul(self.ps[:, lo:lo + w], self.k.const(C_ONES), self.acc[:, lo:lo + w],
                               start=True, stop=True)
        mm.then_inc(self.sum_act, 1)


def split_products(pe, ps, w, rhs, n_k, n, ready=None):
    for t in range(n_k):
        if ready is not None:
            pe.wait_ge(ready[t % 2], 1)
            pe.sem_inc(ready[t % 2], -1)
        for i, (a, b) in enumerate(((0, 0), (1, 0), (0, 1))):
            for lo, width in SEGS:
                if lo < n:
                    mm = pe.matmul(ps[:, lo:lo + width], w[a][:, t, :], rhs[b][:, t, lo:lo + width],
                                   start=(t == 0 and i == 0), stop=(t == n_k - 1 and i == 2))
    return mm


def input_projection_phase(k, a, layer):
    with k.phase() as st:
        w_hi = k.sb(st, "w_hi", [P, 2, KD, P], F32R)
        raw, w_lo = k.twin(st, "w_raw", [P, 2, KD, P])
        out = k.sb(st, "rows", [P, 2, T])
        sq, acc = k.sb(st, "sq", [P, 2, T]), k.sb(st, "acc", [P, T])
        ps = [k.banks(st, f"ps{s}", 3) for s in range(2)]
        w_in, w_free, hi_dve, w_pe = (k.sems(st, s, 2) for s in ("w_in", "w_free", "hi_dve", "w_pe"))
        ps_full, ps_free = k.sems(st, "ps_full", 2), k.sems(st, "ps_free", 2)
        out_free = k.sems(st, "out_free", 2)
        own_a, own_v, mix_in = k.sem(st, "own_a"), k.sem(st, "own_v"), k.sem(st, "mix_in")
        pairs = N_IN // 2
        first_tile = N_IN - 1
        item, start = ITEM[layer], ITEM_START[layer]
        ada_w = k.sb(st, "ada_w", [P, 2, item, D_MODEL])
        k.cact, k.scratch = k.sb(st, "cact", [P, 2, D_MODEL]), k.sb(st, "scratch", [P, D_MODEL])
        ada_in, ada_free = k.sems(st, "item_in", 2), k.sems(st, "item_free", 2)
        cond_in, cond_dve = k.sem(st, "cond_in"), k.sem(st, "cond_dve")
        norm = Norm(k, st, T, 0, 1, sq, acc, out[:, 0, :], ps[1], ada=a["ada_first"] if layer == 0 else None)
        if layer == 0:
            early = k.h[:, :, :].rearrange("p t n -> p (t n)").rearrange("p (n c) -> p n c", c=D_MODEL)
            late = ada_w[:, :, :, :].rearrange("p s n c -> p (s n) c")
            spare = k.mix[:, 0:2 * D_MODEL].rearrange("p (n c) -> p n c", c=D_MODEL)
            norm.ada_parts = [(early[:, 0:5], 0, 5), (early[:, 5:10], 5, 5), (late, 10, 4),
                              (spare, 14, 2)]
        norm.cond_dve = cond_dve

        def load(sp, s, tile):
            sp.wait_ge(w_free[s], 1)
            sp.sem_inc(w_free[s], -1)
            sp.dma_start(raw[:, s], a["w_in"][layer, tile]).then_inc(w_in[s], 16)

        def load_item(act, s, tile):
            act.wait_ge(ada_free[s], 1)
            act.sem_inc(ada_free[s], -1)
            act.dma_start(ada_w[:, s], a[f"ada_rest{layer}"][tile]).then_inc(ada_in[s], 16)

        def round_weights(act, s):
            act.wait_ge(w_in[s], 16)
            act.sem_inc(w_in[s], -16)
            act.activation(w_hi[:, s], raw[:, s], ACT.Copy).then_inc(own_a, 1)
            act.wait_ge(own_a, 1)
            act.sem_inc(own_a, -1)
            act.sem_inc(hi_dve[s], 1)

        def rest_of_weights(dve, s):
            dve.wait_ge(hi_dve[s], 1)
            dve.sem_inc(hi_dve[s], -1)
            dve.tensor_tensor(w_lo[:, s], raw[:, s], w_hi[:, s].bitcast(F32), ALU.subtract).then_inc(own_v, 1)
            dve.wait_ge(own_v, 1)
            dve.sem_inc(own_v, -1)
            dve.sem_inc(w_pe[s], 1)

        def vector_item(dve, s, tile):
            dve.wait_ge(ada_in[s], 16)
            dve.sem_inc(ada_in[s], -16)
            modulation_blocks(dve, k, ada_w[:, s], start + tile * item, item, own_v)
            dve.sem_inc(ada_free[s], 1)

        def multiply(pe, s, ready=None):
            pe.wait_ge(w_pe[s], 1)
            pe.sem_inc(w_pe[s], -1)
            pe.wait_ge(ps_free[s], 1)
            pe.sem_inc(ps_free[s], -1)
            split_products(pe, ps[s], (w_hi[:, s], w_lo[:, s]), (k.hi, k.lo), KD, T, ready).then_inc(ps_full[s], 1)

        def collect(act, s, tile, more=True, next_item=None):
            act.wait_ge(ps_full[s], 1)
            act.sem_inc(ps_full[s], -1)
            act.sem_inc(w_free[s], 1)
            if next_item is not None:
                load_item(act, 1 - s, next_item)
            act.wait_ge(out_free[s], 16)
            act.sem_inc(out_free[s], -16)
            act.activation(out[:, s, :], ps[s][:, 0:T], ACT.Copy).then_inc(own_a, 1)
            act.wait_ge(own_a, 1)
            act.sem_inc(own_a, -1)
            act.sem_inc(ps_free[s], 1)
            act.dma_start(k.rows[tile], out[:, s, :]).then_inc(out_free[s], 16)
            if more:
                round_weights(act, s)

        with k.nc.Block() as block:
            @block.sync
            def _(sp):
                sp.dma_start(k.cact[:, :, :], a["cond"]).then_inc(cond_in, 16)
                norm.sync(sp)
                load(sp, 0, N_IN - 1)
                load(sp, 1, 0)
                with sp.Fori(0, pairs - 1) as i:
                    load(sp, 0, i * 2 + 1)
                    load(sp, 1, i * 2 + 2)
                load(sp, 0, N_IN - 2)
                sp.dma_start(k.mix[:, :], a["consts"][:, N_BASE:N_MIX]).then_inc(mix_in, 16)
                sp.wait_ge(mix_in, 16)
                sp.sem_inc(mix_in, -16)

            @block.tensor
            def _(pe):
                norm.tensor(pe)
                multiply(pe, 0, (norm.even_pe, norm.odd_pe))
                with pe.Fori(0, pairs) as i:
                    multiply(pe, 1)
                    multiply(pe, 0)

            @block.gpsimd
            def _(pool):
                norm.gpsimd(pool, lambda: None)

            @block.vector
            def _(dve):
                norm.vector(dve, lambda: [rest_of_weights(dve, s) for s in range(2)])
                for s in range(2):
                    dve.sem_inc(ada_free[s], 1)
                if layer:
                    dve.wait_ge(cond_dve, 1)
                    dve.sem_inc(cond_dve, -1)
                rest_of_weights(dve, 0)
                vector_item(dve, 0, first_tile)
                with dve.Fori(0, pairs - 1) as i:
                    rest_of_weights(dve, 1)
                    vector_item(dve, 1, i * 2)
                    rest_of_weights(dve, 0)
                    vector_item(dve, 0, i * 2 + 1)
                vector_item(dve, 1, N_IN - 3)
                vector_item(dve, 0, N_IN - 2)
                for l, m in ((0, 2), (0, 4), (0, 5), (1, 1)) if layer == 0 else ((1, 2), (1, 4), (1, 5)):
                    combine_gain(dve, k, l, m, own_v)
                for s in range(2):
                    dve.wait_ge(ada_free[s], 1)
                    dve.sem_inc(ada_free[s], -1)

            @block.scalar
            def _(act):
                for s in range(2):
                    act.sem_inc(w_free[s], 1)
                    act.sem_inc(ps_free[s], 1)
                    act.sem_inc(out_free[s], 16)
                act.wait_ge(cond_in, 16)
                act.sem_inc(cond_in, -16)
                act.activation(k.cact[:, :, :], k.cact[:, :, :], ACT.Silu).then_inc(own_a, 1)
                act.wait_ge(own_a, 1)
                act.sem_inc(own_a, -1)
                act.sem_inc(cond_dve, 1)
                norm.scalar(act, lambda: [round_weights(act, s) for s in range(2)])
                load_item(act, 0, first_tile)
                collect(act, 0, first_tile, next_item=0)
                with act.Fori(0, pairs - 1) as i:
                    collect(act, 1, i * 2, next_item=i * 2 + 1)
                    collect(act, 0, i * 2 + 1, next_item=i * 2 + 2)
                collect(act, 1, N_IN - 3, more=False, next_item=N_IN - 2)
                collect(act, 0, N_IN - 2, more=False)
                for s in range(2):
                    act.wait_ge(w_free[s], 1)
                    act.sem_inc(w_free[s], -1)
                    act.wait_ge(ps_free[s], 1)
                    act.sem_inc(ps_free[s], -1)
                    act.wait_ge(out_free[s], 16)
                    act.sem_inc(out_free[s], -16)


def output_projection_phase(k, a, layer, dest, n):
    with k.phase() as st:
        w_hi = k.sb(st, "w_hi", [P, 2, KD, P], F32R)
        raw, w_lo = k.twin(st, "w_raw", [P, 2, KD, P])
        o_hi = k.sb(st, "o_hi", [P, KD, T], F32R)
        ps = [k.banks(st, f"ps{s}", 3) for s in range(2)]
        w_in, w_free, hi_dve, w_pe = (k.sems(st, s, 2) for s in ("w_in", "w_free", "hi_dve", "w_pe"))
        ps_full, ps_free, o_pe = (k.sems(st, s, 2) for s in ("ps_full", "ps_free", "o_pe"))
        o_dve, own_a, own_v = k.sem(st, "o_dve"), k.sem(st, "own_a"), k.sem(st, "own_v")
        more = KD // 2 - 1

        def load(sp, s, tile):
            sp.wait_ge(w_free[s], 1)
            sp.sem_inc(w_free[s], -1)
            sp.dma_start(raw[:, s], a["w_out"][layer, tile]).then_inc(w_in[s], 16)

        def round_weights(act, s):
            act.wait_ge(w_in[s], 16)
            act.sem_inc(w_in[s], -16)
            act.activation(w_hi[:, s], raw[:, s], ACT.Copy).then_inc(own_a, 1)
            act.wait_ge(own_a, 1)
            act.sem_inc(own_a, -1)
            act.sem_inc(hi_dve[s], 1)

        def rest_of_weights(dve, s):
            dve.wait_ge(hi_dve[s], 1)
            dve.sem_inc(hi_dve[s], -1)
            dve.tensor_tensor(w_lo[:, s], raw[:, s], w_hi[:, s].bitcast(F32), ALU.subtract).then_inc(own_v, 1)
            dve.wait_ge(own_v, 1)
            dve.sem_inc(own_v, -1)
            dve.sem_inc(w_pe[s], 1)

        def collect(dve, s, tile):
            dve.wait_ge(ps_full[s], 1)
            dve.sem_inc(ps_full[s], -1)
            dve.sem_inc(w_free[s], 1)
            dve.tensor_copy(dest[:, tile, 0:n], ps[s][:, 0:n]).then_inc(own_v, 1)
            dve.wait_ge(own_v, 1)
            dve.sem_inc(own_v, -1)
            dve.sem_inc(ps_free[s], 1)

        def multiply(pe, s, ready=None):
            pe.wait_ge(w_pe[s], 1)
            pe.sem_inc(w_pe[s], -1)
            pe.wait_ge(ps_free[s], 1)
            pe.sem_inc(ps_free[s], -1)
            split_products(pe, ps[s], (w_hi[:, s], w_lo[:, s]), (o_hi, k.o_lo), KD, n, ready).then_inc(ps_full[s], 1)

        with k.nc.Block() as block:
            @block.sync
            def _(sp):
                with sp.Fori(0, KD // 2) as i:
                    for s in range(2):
                        load(sp, s, i * 2 + s)

            @block.tensor
            def _(pe):
                multiply(pe, 0, o_pe)
                multiply(pe, 1)
                with pe.Fori(0, more):
                    for s in range(2):
                        multiply(pe, s)

            @block.scalar
            def _(act):
                for t in range(KD):
                    act.activation(o_hi[:, t, 0:n], k.oT[:, t, 0:n], ACT.Copy).then_inc(own_a, 1)
                    act.wait_ge(own_a, 1)
                    act.sem_inc(own_a, -1)
                    act.sem_inc(o_dve, 1)
                    if t < 2:
                        round_weights(act, t)
                with act.Fori(0, more):
                    for s in range(2):
                        round_weights(act, s)

            @block.vector
            def _(dve):
                for s in range(2):
                    dve.sem_inc(w_free[s], 1)
                    dve.sem_inc(ps_free[s], 1)
                for t in range(KD):
                    dve.wait_ge(o_dve, 1)
                    dve.sem_inc(o_dve, -1)
                    dve.tensor_tensor(k.o_lo[:, t, 0:n], k.oT[:, t, 0:n], o_hi[:, t, 0:n].bitcast(F32),
                                      ALU.subtract).then_inc(own_v, 1)
                    dve.wait_ge(own_v, 1)
                    dve.sem_inc(own_v, -1)
                    dve.sem_inc(o_pe[t % 2], 1)
                    if t < 2:
                        rest_of_weights(dve, t)
                with dve.Fori(0, more) as i:
                    for s in range(2):
                        collect(dve, s, i * 2 + s)
                        rest_of_weights(dve, s)
                for s in range(2):
                    collect(dve, s, KD - 2 + s)
                for s in range(2):
                    dve.wait_ge(w_free[s], 1)
                    dve.sem_inc(w_free[s], -1)
                    dve.wait_ge(ps_free[s], 1)
                    dve.sem_inc(ps_free[s], -1)


def residual_phase(k, y, x, n, m_gate, reload=None):
    with k.phase() as st:
        sq = k.sb(st, "sq", [P, 2, T])
        acc = k.sb(st, "acc", [P, T])
        r = k.sb(st, "r", [P, T])
        ps = k.banks(st, "ps", 3)
        sq_full, sq_free = k.sems(st, "sq_full", 2), k.sems(st, "sq_free", 2)
        acc_pe, sum_act, root_dve = (k.sem(st, s) for s in ("acc_pe", "sum_act", "root_dve"))
        own_a, own_v, x_in, scaled = (k.sem(st, s) for s in ("own_a", "own_v", "x_in", "scaled"))
        own_p, x_dve = k.sem(st, "own_p"), k.sem(st, "x_dve")
        with k.nc.Block() as block:
            @block.scalar
            def _(act):
                for t in range(KD):
                    if t >= 2:
                        act.wait_ge(sq_free[t % 2], 1)
                        act.sem_inc(sq_free[t % 2], -1)
                    act.activation(sq[:, t % 2, 0:n], y[:, t, 0:n], ACT.Square).then_inc(sq_full[t % 2], 1)
                act.wait_ge(sum_act, 1)
                act.sem_inc(sum_act, -1)
                row_factor(k, act, own_a, r[:, 0:n], ps[:, 0:n], D_MODEL)
                act.sem_inc(root_dve, 1)

            @block.vector
            def _(dve):
                for t in range(KD):
                    dve.wait_ge(sq_full[t % 2], 1)
                    dve.sem_inc(sq_full[t % 2], -1)
                    if t == 0:
                        ins = dve.tensor_copy(acc[:, 0:n], sq[:, 0, 0:n])
                    else:
                        ins = dve.tensor_tensor(acc[:, 0:n], acc[:, 0:n], sq[:, t % 2, 0:n], ALU.add)
                    if t < KD - 2:
                        ins.then_inc(own_v, 1)
                        dve.wait_ge(own_v, 1)
                        dve.sem_inc(own_v, -1)
                        dve.sem_inc(sq_free[t % 2], 1)
                    elif t < KD - 1:
                        ins.then_inc(own_v, 1)
                        dve.wait_ge(own_v, 1)
                        dve.sem_inc(own_v, -1)
                    else:
                        ins.then_inc(own_v, 1)
                        dve.wait_ge(own_v, 1)
                        dve.sem_inc(own_v, -1)
                        dve.sem_inc(acc_pe, 1)
                dve.wait_ge(root_dve, 1)
                dve.sem_inc(root_dve, -1)
                for t in range(KD):
                    for lo, hi, s in token_parts(n):
                        ins = dve.scalar_tensor_tensor(y[:, t, lo:hi], y[:, t, lo:hi],
                                                       k.mods[:, m_gate * KD + t, s:s + 1], r[:, lo:hi],
                                                       ALU.mult, ALU.mult)
                        if hi < n or t % 2:
                            ins.then_inc(own_v, 1)
                            dve.wait_ge(own_v, 1)
                            dve.sem_inc(own_v, -1)
                    if t % 2 == 0:
                        ins.then_inc(scaled, 1)
                if reload is not None:
                    dve.wait_ge(x_dve, 16)
                    dve.sem_inc(x_dve, -16)
                for t in range(1, KD, 2):
                    last = dve.tensor_tensor(k.xT[:, t, 0:n], x[:, t, 0:n], y[:, t, 0:n], ALU.add)
                last.then_inc(own_v, 1)
                dve.wait_ge(own_v, 1)
                dve.sem_inc(own_v, -1)

            @block.gpsimd
            def _(pool):
                if reload is not None:
                    pool.wait_ge(x_in, 16)
                    pool.sem_inc(x_in, -16)
                for t in range(0, KD, 2):
                    pool.wait_ge(scaled, 1)
                    pool.sem_inc(scaled, -1)
                    last = pool.tensor_tensor(k.xT[:, t, 0:n], x[:, t, 0:n], y[:, t, 0:n], ALU.add)
                last.then_inc(own_p, 1)
                pool.wait_ge(own_p, 1)
                pool.sem_inc(own_p, -1)

            @block.tensor
            def _(pe):
                pe.wait_ge(acc_pe, 1)
                pe.sem_inc(acc_pe, -1)
                for lo, w in SEGS:
                    if lo < n:
                        mm = pe.matmul(ps[:, lo:lo + w], k.const(C_ONES), acc[:, lo:lo + w], start=True, stop=True)
                mm.then_inc(sum_act, 1)

            if reload is not None:
                @block.sync
                def _(sp):
                    sp.dma_start(x[:, 0:KD:2, :], reload[:, 0:KD:2, :]).then_inc(x_in, 16)
                    sp.dma_start(x[:, 1:KD:2, :], reload[:, 1:KD:2, :]).then_inc(x_dve, 16)


def conv_parts(n):
    return [(0, SEQ)] + ([(SEQ, n)] if n > SEQ else [])


class Job:

    def __init__(self, tile, dest, taps=None, silu=False, width=None, factor=None, rope=False, to_tokens=None):
        self.tile, self.dest, self.taps, self.silu = tile, dest, taps, silu
        self.width, self.factor, self.rope, self.to_tokens = width, factor, rope, to_tokens


def rows_phase(k, jobs, trig=None):
    with k.phase() as st:
        raw = k.sb(st, "raw", [P, 2, T])
        sq = k.sb(st, "sq", [P, 2, T])
        r = k.sb(st, "r", [P, 2, T])
        rot = k.sb(st, "rot", [P, SEQ]) if trig is not None else None
        ps = [k.banks(st, f"ps{s}", 3) for s in range(2)]
        ps_rot = k.banks(st, "ps_rot", 2)
        raw_in, raw_free = k.sems(st, "raw_in", 2), k.sems(st, "raw_free", 2)
        centre_dve, taps_act, y_dve, sq_pe, sum_act, root_dve = (
            k.sem(st, s) for s in ("centre_dve", "taps_act", "y_dve", "sq_pe", "sum_act", "root_dve"))
        r_free = k.sems(st, "r_free", 2)
        y_pe, rot_dve, pass_pe, tok_dve, tok_free = (
            k.sem(st, s) for s in ("y_pe", "rot_dve", "pass_pe", "tok_dve", "tok_free"))
        own_a, own_v = k.sem(st, "own_a"), k.sem(st, "own_v")

        def in_steps(front, back):
            for j, job in enumerate(jobs):
                front(j % 2, job)
                if j:
                    back((j - 1) % 2, jobs[j - 1])
            back((len(jobs) - 1) % 2, jobs[-1])

        def scalar_front(act, s, job):
            act.wait_ge(raw_in[s], 16)
            act.sem_inc(raw_in[s], -16)
            if job.taps is not None:
                act.activation(job.dest, raw[:, s, :], ACT.Copy,
                               scale=k.vec(V_GCONV + 6 + job.taps)).then_inc(own_a, 1)
                act.wait_ge(own_a, 1)
                act.sem_inc(own_a, -1)
                act.sem_inc(centre_dve, 1)
                act.wait_ge(taps_act, 1)
                act.sem_inc(taps_act, -1)
                act.activation(job.dest, job.dest, ACT.Silu).then_inc(own_a, 1)
                act.wait_ge(own_a, 1)
                act.sem_inc(own_a, -1)
            else:
                act.activation(job.dest, raw[:, s, :], ACT.Silu if job.silu else ACT.Copy).then_inc(own_a, 1)
                act.wait_ge(own_a, 1)
                act.sem_inc(own_a, -1)
            act.sem_inc(raw_free[s], 1)
            if job.width is not None:
                act.activation(sq[:, s, :], job.dest, ACT.Square).then_inc(own_a, 1)
                act.wait_ge(own_a, 1)
                act.sem_inc(own_a, -1)
                act.sem_inc(sq_pe, 1)
            elif job.rope or job.to_tokens is not None:
                act.sem_inc(y_dve, 1)

        def scalar_back(act, s, job):
            if job.width is not None:
                act.wait_ge(sum_act, 1)
                act.sem_inc(sum_act, -1)
                act.wait_ge(r_free[s], 1)
                act.sem_inc(r_free[s], -1)
                act.activation(r[:, s, :], ps[s][:, 0:T], ACT.Sqrt, scale=1.0 / job.width,
                               bias=k.eps[:, 0:1]).then_inc(own_a, 1)
                act.wait_ge(own_a, 1)
                act.sem_inc(own_a, -1)
                act.sem_inc(root_dve, 1)

        def vector_front(dve, s, job):
            if job.taps is not None:
                dve.wait_ge(centre_dve, 1)
                dve.sem_inc(centre_dve, -1)
                for lo, hi in conv_parts(T):
                    dve.scalar_tensor_tensor(
                        job.dest[:, lo + 1:hi], raw[:, s, lo:hi - 1], k.vec(V_GCONV + job.taps),
                        job.dest[:, lo + 1:hi], ALU.mult, ALU.add).then_inc(own_v, 1)
                    dve.wait_ge(own_v, 1)
                    dve.sem_inc(own_v, -1)
                    dve.scalar_tensor_tensor(
                        job.dest[:, lo:hi - 1], raw[:, s, lo + 1:hi], k.vec(V_GCONV + 12 + job.taps),
                        job.dest[:, lo:hi - 1], ALU.mult, ALU.add).then_inc(own_v, 1)
                    dve.wait_ge(own_v, 1)
                    dve.sem_inc(own_v, -1)
                dve.sem_inc(taps_act, 1)

        def vector_back(dve, s, job):
            if job.width is not None:
                dve.wait_ge(root_dve, 1)
                dve.sem_inc(root_dve, -1)
                dve.reciprocal(r[:, s, :], r[:, s, :]).then_inc(own_v, 1)
                dve.wait_ge(own_v, 1)
                dve.sem_inc(own_v, -1)
                dve.scalar_tensor_tensor(job.dest, job.dest, job.factor, r[:, s, :],
                                         ALU.mult, ALU.mult).then_inc(own_v, 1)
                dve.wait_ge(own_v, 1)
                dve.sem_inc(own_v, -1)
                dve.sem_inc(r_free[s], 1)
            elif job.rope or job.to_tokens is not None:
                dve.wait_ge(y_dve, 1)
                dve.sem_inc(y_dve, -1)
            if job.rope:
                dve.sem_inc(y_pe, 1)
                dve.wait_ge(rot_dve, 1)
                dve.sem_inc(rot_dve, -1)
                dve.tensor_tensor(rot[:, :], ps_rot[:, 0:SEQ], trig[:, SEQ:], ALU.mult).then_inc(own_v, 1)
                dve.wait_ge(own_v, 1)
                dve.sem_inc(own_v, -1)
                lat = job.dest[:, 0:SEQ]
                dve.tensor_tensor(lat, lat, trig[:, 0:SEQ], ALU.mult).then_inc(own_v, 1)
                dve.wait_ge(own_v, 1)
                dve.sem_inc(own_v, -1)
                dve.tensor_tensor(lat, lat, rot[:, :], ALU.add).then_inc(own_v, 1)
                dve.wait_ge(own_v, 1)
                dve.sem_inc(own_v, -1)
            if job.to_tokens is not None:
                dve.sem_inc(pass_pe, 1)
                for c0 in range(0, NT, 4):
                    n = min(4, NT - c0)
                    dve.wait_ge(tok_dve, 1)
                    dve.sem_inc(tok_dve, -1)
                    dve.tensor_copy(job.to_tokens[:, c0:c0 + n, :],
                                    ps_rot[:, 0:n * P].rearrange("p (c f) -> p c f", f=P)).then_inc(own_v, 1)
                    dve.wait_ge(own_v, 1)
                    dve.sem_inc(own_v, -1)
                    dve.sem_inc(tok_free, 1)

        def tensor_front(pe, s, job):
            if job.width is not None:
                pe.wait_ge(sq_pe, 1)
                pe.sem_inc(sq_pe, -1)
                for lo, w in SEGS:
                    mm = pe.matmul(ps[s][:, lo:lo + w], k.const(C_BLK), sq[:, s, lo:lo + w], start=True, stop=True)
                mm.then_inc(sum_act, 1)

        def tensor_back(pe, s, job):
            if job.rope:
                pe.wait_ge(y_pe, 1)
                pe.sem_inc(y_pe, -1)
                for lo, w in SEGS[:2]:
                    mm = pe.matmul(ps_rot[:, lo:lo + w], k.const(C_ROT), job.dest[:, lo:lo + w],
                                   start=True, stop=True)
                mm.then_inc(rot_dve, 1)
            if job.to_tokens is not None:
                pe.wait_ge(pass_pe, 1)
                pe.sem_inc(pass_pe, -1)
                for c0 in range(0, NT, 4):
                    if c0:
                        pe.wait_ge(tok_free, 1)
                        pe.sem_inc(tok_free, -1)
                    for c in range(c0, min(c0 + 4, NT)):
                        mm = pe.transpose(ps_rot[:, (c - c0) * P:(c - c0 + 1) * P],
                                          job.dest[:, c * P:(c + 1) * P], k.const(C_IDENT))
                    mm.then_inc(tok_dve, 1)
                pe.wait_ge(tok_free, 1)
                pe.sem_inc(tok_free, -1)

        with k.nc.Block() as block:
            @block.sync
            def _(sp):
                for j, job in enumerate(jobs):
                    if j >= 2:
                        sp.wait_ge(raw_free[j % 2], 1)
                        sp.sem_inc(raw_free[j % 2], -1)
                    sp.dma_start(raw[:, j % 2, :], k.rows[job.tile]).then_inc(raw_in[j % 2], 16)

            @block.scalar
            def _(act):
                in_steps(lambda s, job: scalar_front(act, s, job), lambda s, job: scalar_back(act, s, job))
                for s in range(2):
                    act.wait_ge(raw_free[s], 1)
                    act.sem_inc(raw_free[s], -1)

            @block.vector
            def _(dve):
                for s in range(2):
                    dve.sem_inc(r_free[s], 1)
                in_steps(lambda s, job: vector_front(dve, s, job), lambda s, job: vector_back(dve, s, job))
                for s in range(2):
                    dve.wait_ge(r_free[s], 1)
                    dve.sem_inc(r_free[s], -1)

            @block.tensor
            def _(pe):
                in_steps(lambda s, job: tensor_front(pe, s, job), lambda s, job: tensor_back(pe, s, job))


def gate_phase(k, pairs, oT_tile, z_tile, gain_col):
    with k.phase() as st:
        z = k.sb(st, "z", [P, 2, T])
        sq = k.sb(st, "sq", [P, 2, T])
        r = k.sb(st, "r", [P, 2, T])
        ps = [k.banks(st, f"ps{s}", 3) for s in range(2)]
        z_in = k.sems(st, "z_in", 2)
        o_act, sq_pe, sum_act, root_dve = (k.sem(st, s) for s in ("o_act", "sq_pe", "sum_act", "root_dve"))
        own_a, own_v = k.sem(st, "own_a"), k.sem(st, "own_v")
        with k.nc.Block() as block:
            @block.sync
            def _(sp):
                for s in range(2):
                    sp.dma_start(z[:, s, :], k.rows[z_tile + s]).then_inc(z_in[s], 16)

            @block.scalar
            def _(act):
                for s in range(2):
                    act.wait_ge(z_in[s], 16)
                    act.sem_inc(z_in[s], -16)
                    act.activation(z[:, s, :], z[:, s, :], ACT.Silu).then_inc(own_a, 1)
                    act.wait_ge(own_a, 1)
                    act.sem_inc(own_a, -1)
                for s in range(2):
                    act.wait_ge(o_act, 1)
                    act.sem_inc(o_act, -1)
                    act.activation(sq[:, s, :], pairs[:, 0, s, :], ACT.Square).then_inc(own_a, 1)
                    act.wait_ge(own_a, 1)
                    act.sem_inc(own_a, -1)
                    act.sem_inc(sq_pe, 1)
                for s in range(2):
                    act.wait_ge(sum_act, 1)
                    act.sem_inc(sum_act, -1)
                    row_factor(k, act, own_a, r[:, s, :], ps[s][:, 0:T], HD)
                    act.sem_inc(root_dve, 1)

            @block.tensor
            def _(pe):
                for s in range(2):
                    pe.wait_ge(sq_pe, 1)
                    pe.sem_inc(sq_pe, -1)
                    for lo, w in SEGS:
                        mm = pe.matmul(ps[s][:, lo:lo + w], k.const(C_BLK), sq[:, s, lo:lo + w], start=True, stop=True)
                    mm.then_inc(sum_act, 1)

            @block.vector
            def _(dve):
                for s in range(2):
                    dve.tensor_tensor(pairs[:, 0, s, :], pairs[:, 0, s, :], pairs[:, 1, s, :], ALU.add)\
                        .then_inc(own_v, 1)
                    dve.wait_ge(own_v, 1)
                    dve.sem_inc(own_v, -1)
                    dve.sem_inc(o_act, 1)
                for s in range(2):
                    dve.wait_ge(root_dve, 1)
                    dve.sem_inc(root_dve, -1)
                    dve.scalar_tensor_tensor(pairs[:, 0, s, :], pairs[:, 0, s, :], k.vec(gain_col),
                                             r[:, s, :], ALU.mult, ALU.mult).then_inc(own_v, 1)
                    dve.wait_ge(own_v, 1)
                    dve.sem_inc(own_v, -1)
                    dve.tensor_tensor(k.oT[:, oT_tile + s, :], pairs[:, 0, s, :], z[:, s, :], ALU.mult)\
                        .then_inc(own_v, 1)
                    dve.wait_ge(own_v, 1)
                    dve.sem_inc(own_v, -1)


def decay_rows_phase(k, bg):
    with k.phase() as st:
        lin = k.sb(st, "lin", [HD, T])
        soft = k.sb(st, "soft", [HD, T])
        came, a_dve, v_act, own_a, own_v = (k.sem(st, s) for s in ("came", "a_dve", "v_act", "own_a", "own_v"))
        g = slice(G_ROW, G_ROW + 2 * H)
        with k.nc.Block() as block:
            @block.sync
            def _(sp):
                sp.dma_start(bg[:, :], k.rows[T_BETA][0:HD]).then_inc(came, 16)

            @block.scalar
            def _(act):
                act.wait_ge(came, 16)
                act.sem_inc(came, -16)
                act.activation(lin[g, :], bg[g, :], ACT.Identity, bias=k.vecs[g, V_DTB:V_DTB + 1]).then_inc(own_a, 1)
                act.wait_ge(own_a, 1)
                act.sem_inc(own_a, -1)
                act.sem_inc(a_dve, 1)
                act.activation(bg[0:2 * H, :], bg[0:2 * H, :], ACT.Sigmoid).then_inc(own_a, 1)
                act.wait_ge(own_a, 1)
                act.sem_inc(own_a, -1)
                act.wait_ge(v_act, 1)
                act.sem_inc(v_act, -1)
                act.activation(soft[g, :], soft[g, :], ACT.Exp).then_inc(own_a, 1)
                act.wait_ge(own_a, 1)
                act.sem_inc(own_a, -1)
                act.activation(soft[g, :], soft[g, :], ACT.Ln, bias=1.0).then_inc(own_a, 1)
                act.wait_ge(own_a, 1)
                act.sem_inc(own_a, -1)
                act.sem_inc(a_dve, 1)

            @block.vector
            def _(dve):
                dve.wait_ge(a_dve, 1)
                dve.sem_inc(a_dve, -1)
                dve.tensor_scalar(soft[g, :], lin[g, :], 0.0, 2.0, ALU.min, ALU.mult).then_inc(own_v, 1)
                dve.wait_ge(own_v, 1)
                dve.sem_inc(own_v, -1)
                dve.tensor_tensor(soft[g, :], soft[g, :], lin[g, :], ALU.subtract).then_inc(own_v, 1)
                dve.wait_ge(own_v, 1)
                dve.sem_inc(own_v, -1)
                dve.sem_inc(v_act, 1)
                dve.tensor_scalar(lin[g, :], lin[g, :], 0.0, None, ALU.max).then_inc(own_v, 1)
                dve.wait_ge(own_v, 1)
                dve.sem_inc(own_v, -1)
                dve.wait_ge(a_dve, 1)
                dve.sem_inc(a_dve, -1)
                dve.tensor_tensor(lin[g, :], lin[g, :], soft[g, :], ALU.add).then_inc(own_v, 1)
                dve.wait_ge(own_v, 1)
                dve.sem_inc(own_v, -1)
                dve.tensor_scalar(bg[g, :], lin[g, :], k.expa[g, 0:1], None, ALU.mult).then_inc(own_v, 1)
                dve.wait_ge(own_v, 1)
                dve.sem_inc(own_v, -1)


def chunk_of(d, i):
    return (i + NT - CTX // P) % NT if d == 0 else NT - 1 - i


def gdn_phase(k, qkv, bg, both):
    with k.phase() as st:
        stg = k.sb(st, "stg", [P, 2, 6, P])
        bgs = k.sb(st, "bgs", [HD, 2, P])
        tok = k.sb(st, "tok", [P, 2, 4, P])
        bgt = k.sb(st, "bgt", [P, 2, HD])
        nb = k.sb(st, "nb", [P, 2, H])
        gm = k.sb(st, "gm", [P, 2, H, P])
        gb = k.sb(st, "gb", [P, 2, H, HD])
        dec = k.sb(st, "dec", [P, 2, H, P])
        ecum = k.sb(st, "ecum", [P, 2, 2 * P + 2 * H])
        dm = dec
        attn = k.sb(st, "attn", [P, 2, H, P])
        nm = k.sb(st, "nm", [P, 2, H, P])
        S = k.sb(st, "S", [P, 2, H, P])
        Ti = k.sb(st, "Ti", [P, 2, H, P])
        vm, nbd = gm, S
        qd = k.sb(st, "qd", [P, 2, 2, P])
        ke = k.sb(st, "ke", [P, 2, H, HD])
        kd = k.sb(st, "kd", [P, 2, H, HD])
        wtn = k.sb(st, "wtn", [P, 2, 2, P])
        vn = k.sb(st, "vn", [P, 2, H, HD])
        state = k.sb(st, "state", [P, 2, 2, P])
        tmp = k.sb(st, "tmp", [P, 2, 2, P])
        B = [[k.banks(st, f"b{d}{b}", 1) for b in range(4)] for d in range(2)]
        names = ("staged_pe tr_act bgt_dve tok_pe gm_pe nb_pool rc_act de_pool dm_dve ke_pe kk_dve s2_pe t2_act "
                 "ti_pe inv_pe v_dve vm_pe x_dve u_dve wt_act wtn_pe vn_dve vn_pe o_act su_dve state_pe").split()
        sem = {n: k.sems(st, n, 2) for n in names}
        own = {e: k.sem(st, f"own_{e}") for e in ("act", "dve", "pool")}
        beta = [bgt[:, d, BETA_ROW + H * d:BETA_ROW + H * (d + 1)] for d in range(2)]
        gcol = [bgt[:, d, G_ROW + H * d:G_ROW + H * (d + 1)] for d in range(2)]
        ident = k.const(C_IDENT)
        cum = [k.const(C_CUM + d * P) for d in range(2)]
        strict = [k.const(C_STR + d * P) for d in range(2)]
        after = [k.const(C_STR + (1 - d) * P) for d in range(2)]

        def heads(b):
            return b[:, :].rearrange("p (h f) -> p h f", f=P)

        def level_ji(d, l):
            return k.const(C_LVL + (d * LEVELS + l) * P)

        def level_ij(d, l):
            return k.const(C_LVL + ((1 - d) * LEVELS + l) * P)

        with k.nc.Block() as block:
            @block.scalar
            def _(act):
                with act.Fori(0, NT) as i:
                    for d in range(2):
                        col = bass.ds(chunk_of(d, i) * P, P)
                        act.activation(stg[:, d], qkv[:, :, col], ACT.Copy)
                        act.activation(bgs[:, d, :], bg[:, col], ACT.Copy).then_inc(own["act"], 1)
                        act.wait_ge(own["act"], 1)
                        act.sem_inc(own["act"], -1)
                        act.sem_inc(sem["staged_pe"][d], 1)
                    for d in range(2):
                        act.wait_ge(sem["tr_act"][d], 1)
                        act.sem_inc(sem["tr_act"][d], -1)
                        act.activation(tok[:, d], heads(B[d][0]), ACT.Copy).then_inc(own["act"], 1)
                        act.wait_ge(own["act"], 1)
                        act.sem_inc(own["act"], -1)
                        act.activation(bgt[:, d, :], B[d][1][:, 0:HD], ACT.Copy).then_inc(own["act"], 1)
                        act.wait_ge(own["act"], 1)
                        act.sem_inc(own["act"], -1)
                        act.sem_inc(sem["bgt_dve"][d], 1)
                        act.sem_inc(sem["tok_pe"][d], 1)
                    for d in range(2):
                        act.wait_ge(sem["rc_act"][d], 1)
                        act.sem_inc(sem["rc_act"][d], -1)
                        act.activation(dec[:, d], heads(B[d][2]), ACT.Exp).then_inc(own["act"], 1)
                        act.wait_ge(own["act"], 1)
                        act.sem_inc(own["act"], -1)
                        act.activation(ecum[:, d, :], B[d][3][:, 0:2 * P + 2 * H], ACT.Exp).then_inc(own["act"], 1)
                        act.wait_ge(own["act"], 1)
                        act.sem_inc(own["act"], -1)
                        act.sem_inc(sem["de_pool"][d], 1)
                    for d in range(2):
                        act.wait_ge(sem["t2_act"][d], 1)
                        act.sem_inc(sem["t2_act"][d], -1)
                        act.activation(Ti[:, d], heads(B[d][2]), ACT.Copy).then_inc(own["act"], 1)
                        act.wait_ge(own["act"], 1)
                        act.sem_inc(own["act"], -1)
                        act.sem_inc(sem["ti_pe"][d], 1)
                    for d in range(2):
                        act.wait_ge(sem["wt_act"][d], 1)
                        act.sem_inc(sem["wt_act"][d], -1)
                        act.activation(wtn[:, d], B[d][0][:, 0:2 * P].rearrange("p (a f) -> p a f", f=P),
                                       ACT.Copy, scale=-1.0).then_inc(own["act"], 1)
                        act.wait_ge(own["act"], 1)
                        act.sem_inc(own["act"], -1)
                        act.sem_inc(sem["wtn_pe"][d], 1)
                    for d in range(2):
                        act.wait_ge(sem["o_act"][d], 1)
                        act.sem_inc(sem["o_act"][d], -1)
                        act.activation(both[:, d, :, bass.ds(chunk_of(d, i) * P, P)],
                                       B[d][2][:, 0:2 * P].rearrange("p (a f) -> p a f", f=P), ACT.Copy)\
                            .then_inc(own["act"], 1)
                        act.wait_ge(own["act"], 1)
                        act.sem_inc(own["act"], -1)

            @block.vector
            def _(dve):
                dve.memset(state[:, :, :, :], 0.0).then_inc(own["dve"], 1)
                dve.wait_ge(own["dve"], 1)
                dve.sem_inc(own["dve"], -1)
                for d in range(2):
                    dve.sem_inc(sem["state_pe"][d], 1)
                with dve.Fori(0, NT):
                    for d in range(2):
                        dve.wait_ge(sem["bgt_dve"][d], 1)
                        dve.sem_inc(sem["bgt_dve"][d], -1)
                        dve.tensor_scalar(nb[:, d, :], beta[d], -1.0, None, ALU.mult).then_inc(own["dve"], 1)
                        dve.wait_ge(own["dve"], 1)
                        dve.sem_inc(own["dve"], -1)
                        dve.sem_inc(sem["nb_pool"][d], 1)
                        dve.tensor_copy(gb[:, d], widen(gcol[d], HD)).then_inc(own["dve"], 1)
                        dve.wait_ge(own["dve"], 1)
                        dve.sem_inc(own["dve"], -1)
                        dve.tensor_tensor(gm[:, d], spread(strict[d], H), widen(gcol[d], P), ALU.mult)\
                            .then_inc(own["dve"], 1)
                        dve.wait_ge(own["dve"], 1)
                        dve.sem_inc(own["dve"], -1)
                        dve.sem_inc(sem["gm_pe"][d], 1)
                    for d in range(2):
                        dve.wait_ge(sem["dm_dve"][d], 1)
                        dve.sem_inc(sem["dm_dve"][d], -1)
                        dve.wait_ge(sem["kk_dve"][d], 1)
                        dve.sem_inc(sem["kk_dve"][d], -1)
                        for p in range(2):
                            pair = B[d][p][:, :].rearrange("p (a x f) -> p a x f", a=2, x=2)
                            dve.tensor_tensor(nm[:, d, p::2, :], pair[:, :, 1, :], nbd[:, d, p::2, :],
                                              ALU.mult).then_inc(own["dve"], 1)
                            dve.wait_ge(own["dve"], 1)
                            dve.sem_inc(own["dve"], -1)
                            dve.tensor_tensor(attn[:, d, p::2, :], pair[:, :, 0, :], dm[:, d, p::2, :],
                                              ALU.mult).then_inc(own["dve"], 1)
                            dve.wait_ge(own["dve"], 1)
                            dve.sem_inc(own["dve"], -1)
                        dve.tensor_tensor(S[:, d], nm[:, d], spread(level_ji(d, 0), H), ALU.mult)\
                            .then_inc(own["dve"], 1)
                        dve.wait_ge(own["dve"], 1)
                        dve.sem_inc(own["dve"], -1)
                        dve.tensor_tensor(S[:, d], S[:, d], spread(ident, H), ALU.add).then_inc(own["dve"], 1)
                        dve.wait_ge(own["dve"], 1)
                        dve.sem_inc(own["dve"], -1)
                        dve.sem_inc(sem["s2_pe"][d], 1)
                    for l in range(1, LEVELS):
                        for d in range(2):
                            dve.wait_ge(sem["v_dve"][d], 1)
                            dve.sem_inc(sem["v_dve"][d], -1)
                            dve.tensor_tensor(vm[:, d], heads(B[d][0]), spread(level_ij(d, l), H),
                                              ALU.mult).then_inc(own["dve"], 1)
                            dve.wait_ge(own["dve"], 1)
                            dve.sem_inc(own["dve"], -1)
                            dve.sem_inc(sem["vm_pe"][d], 1)
                        for d in range(2):
                            if l < LEVELS - 1:
                                dve.wait_ge(sem["x_dve"][d], 1)
                                dve.sem_inc(sem["x_dve"][d], -1)
                                dve.tensor_tensor(Ti[:, d], heads(B[d][2]), Ti[:, d], ALU.add)\
                                    .then_inc(own["dve"], 1)
                                dve.wait_ge(own["dve"], 1)
                                dve.sem_inc(own["dve"], -1)
                                dve.sem_inc(sem["ti_pe"][d], 1)
                            dve.wait_ge(sem["u_dve"][d], 1)
                            dve.sem_inc(sem["u_dve"][d], -1)
                            dve.tensor_tensor(S[:, d], heads(B[d][1]), S[:, d], ALU.add).then_inc(own["dve"], 1)
                            dve.wait_ge(own["dve"], 1)
                            dve.sem_inc(own["dve"], -1)
                            dve.sem_inc(sem["inv_pe"][d], 1)
                    for d in range(2):
                        dve.wait_ge(sem["vn_dve"][d], 1)
                        dve.sem_inc(sem["vn_dve"][d], -1)
                        dve.tensor_tensor(vn[:, d], B[d][1][:, 0:2 * P].rearrange("p (h f) -> p h f", f=HD),
                                          widen(beta[d], HD), ALU.mult).then_inc(own["dve"], 1)
                        dve.wait_ge(own["dve"], 1)
                        dve.sem_inc(own["dve"], -1)
                        dve.sem_inc(sem["vn_pe"][d], 1)
                    for d in range(2):
                        dve.wait_ge(sem["su_dve"][d], 1)
                        dve.sem_inc(sem["su_dve"][d], -1)
                        dve.tensor_tensor(tmp[:, d], B[d][3][:, 0:2 * P].rearrange("p (a f) -> p a f", f=P),
                                          spread(k.const(C_BLK), 2), ALU.mult).then_inc(own["dve"], 1)
                        dve.wait_ge(own["dve"], 1)
                        dve.sem_inc(own["dve"], -1)
                        for a in range(2):
                            whole = a * P + (P - 1 if d == 0 else 0)
                            dve.scalar_tensor_tensor(state[:, d, a, :], state[:, d, a, :],
                                                     ecum[:, d, whole:whole + 1], tmp[:, d, a, :],
                                                     ALU.mult, ALU.add).then_inc(own["dve"], 1)
                            dve.wait_ge(own["dve"], 1)
                            dve.sem_inc(own["dve"], -1)
                        dve.sem_inc(sem["state_pe"][d], 1)
                for d in range(2):
                    dve.wait_ge(sem["state_pe"][d], 1)
                    dve.sem_inc(sem["state_pe"][d], -1)

            @block.gpsimd
            def _(pool):
                with pool.Fori(0, NT):
                    for d in range(2):
                        pool.wait_ge(sem["de_pool"][d], 1)
                        pool.sem_inc(sem["de_pool"][d], -1)
                        pool.wait_ge(sem["nb_pool"][d], 1)
                        pool.sem_inc(sem["nb_pool"][d], -1)
                        pool.tensor_tensor(nbd[:, d], dec[:, d], spread(after[d], H), ALU.mult)\
                            .then_inc(own["pool"], 1)
                        pool.wait_ge(own["pool"], 1)
                        pool.sem_inc(own["pool"], -1)
                        pool.tensor_tensor(nbd[:, d], nbd[:, d], widen(nb[:, d, :], P), ALU.mult)\
                            .then_inc(own["pool"], 1)
                        pool.wait_ge(own["pool"], 1)
                        pool.sem_inc(own["pool"], -1)
                        pool.tensor_tensor(dm[:, d], dec[:, d], spread(cum[d], H), ALU.mult).then_inc(own["pool"], 1)
                        pool.wait_ge(own["pool"], 1)
                        pool.sem_inc(own["pool"], -1)
                        pool.sem_inc(sem["dm_dve"][d], 1)
                    for d in range(2):
                        pool.tensor_tensor(qd[:, d], stg[:, d, 0:2, :],
                                           ecum[:, d, 0:2 * P].rearrange("p (a f) -> p a f", f=P), ALU.mult)
                        ktok = tok[:, d, 0:2, :].rearrange("p a (h f) -> p (a h) f", f=HD)
                        pool.tensor_tensor(kd[:, d], ktok, widen(ecum[:, d, 2 * P:2 * P + H], HD), ALU.mult)
                        pool.tensor_tensor(ke[:, d], ktok, widen(ecum[:, d, 2 * P + H:2 * P + 2 * H], HD),
                                           ALU.mult).then_inc(own["pool"], 1)
                        pool.wait_ge(own["pool"], 1)
                        pool.sem_inc(own["pool"], -1)
                        pool.sem_inc(sem["ke_pe"][d], 1)

            @block.tensor
            def _(pe):
                with pe.Fori(0, NT):
                    for d in range(2):
                        pe.wait_ge(sem["staged_pe"][d], 1)
                        pe.sem_inc(sem["staged_pe"][d], -1)
                        for x in range(4):
                            pe.transpose(B[d][0][:, x * P:(x + 1) * P], stg[:, d, 2 + x, :], ident)
                        pe.transpose(B[d][1][:, 0:HD], bgs[:, d, :], k.consts[0:HD, C_IDENT:C_IDENT + HD])\
                            .then_inc(sem["tr_act"][d], 1)
                    for d in range(2):
                        pe.wait_ge(sem["gm_pe"][d], 1)
                        pe.sem_inc(sem["gm_pe"][d], -1)
                        for h in range(H):
                            pe.matmul(B[d][2][:, h * P:(h + 1) * P], gm[:, d, h, :], cum[d], start=True, stop=True)
                        for a in range(2):
                            pe.matmul(B[d][3][:, a * P:(a + 1) * P],
                                      gb[:, d, 2 * a:2 * a + 2, :].rearrange("p h f -> p (h f)"), cum[d],
                                      start=True, stop=True)
                        pe.matmul(B[d][3][:, 2 * P:2 * P + H], strict[d], gcol[d], start=True, stop=True)
                        pe.matmul(B[d][3][:, 2 * P + H:2 * P + 2 * H], cum[d], gcol[d], start=True, stop=True)\
                            .then_inc(sem["rc_act"][d], 1)
                    for d in range(2):
                        pe.wait_ge(sem["tok_pe"][d], 1)
                        pe.sem_inc(sem["tok_pe"][d], -1)
                        for h in range(H):
                            rows, a = slice(HD * (h % 2), HD * (h % 2 + 1)), h // 2
                            mm = pe.matmul(B[d][h % 2][:, 2 * a * P:2 * (a + 1) * P], stg[rows, d, 2 + a, :],
                                           stg[rows, d, a:a + 3:2, :], start=True, stop=True)
                        mm.then_inc(sem["kk_dve"][d], 1)
                    for d in range(2):
                        pe.wait_ge(sem["s2_pe"][d], 1)
                        pe.sem_inc(sem["s2_pe"][d], -1)
                        for h in range(H):
                            mm = pe.transpose(B[d][2][:, h * P:(h + 1) * P], S[:, d, h, :], ident)
                        mm.then_inc(sem["t2_act"][d], 1)
                    for l in range(1, LEVELS):
                        for d in range(2):
                            pe.wait_ge(sem["ti_pe"][d], 1)
                            pe.sem_inc(sem["ti_pe"][d], -1)
                            for h in range(H):
                                mm = pe.matmul(B[d][0][:, h * P:(h + 1) * P], nm[:, d, h, :], Ti[:, d, h, :],
                                               start=True, stop=True)
                            mm.then_inc(sem["v_dve"][d], 1)
                        for d in range(2):
                            if l > 1:
                                pe.wait_ge(sem["inv_pe"][d], 1)
                                pe.sem_inc(sem["inv_pe"][d], -1)
                            pe.wait_ge(sem["vm_pe"][d], 1)
                            pe.sem_inc(sem["vm_pe"][d], -1)
                            if l < LEVELS - 1:
                                for h in range(H):
                                    mm = pe.matmul(B[d][2][:, h * P:(h + 1) * P], S[:, d, h, :], vm[:, d, h, :],
                                                   start=True, stop=True)
                                mm.then_inc(sem["x_dve"][d], 1)
                            for h in range(H):
                                mm = pe.matmul(B[d][1][:, h * P:(h + 1) * P], vm[:, d, h, :], S[:, d, h, :],
                                               start=True, stop=True)
                            mm.then_inc(sem["u_dve"][d], 1)
                    for d in range(2):
                        pe.wait_ge(sem["inv_pe"][d], 1)
                        pe.sem_inc(sem["inv_pe"][d], -1)
                        pe.wait_ge(sem["ke_pe"][d], 1)
                        pe.sem_inc(sem["ke_pe"][d], -1)
                        for h in range(H):
                            a, p = h // 2, h % 2
                            mm = pe.matmul(B[d][0][HD * p:HD * (p + 1), a * P:(a + 1) * P], ke[:, d, h, :],
                                           S[:, d, h, :], start=True, stop=True)
                        mm.then_inc(sem["wt_act"][d], 1)
                        for h in range(H):
                            pe.matmul(B[d][1][:, h * HD:(h + 1) * HD], S[:, d, h, :],
                                      tok[:, d, 2 + h // 2, HD * (h % 2):HD * (h % 2 + 1)],
                                      start=(h == 0), stop=False, skip_group_check=True)
                    for d in range(2):
                        pe.wait_ge(sem["wtn_pe"][d], 1)
                        pe.sem_inc(sem["wtn_pe"][d], -1)
                        pe.wait_ge(sem["state_pe"][d], 1)
                        pe.sem_inc(sem["state_pe"][d], -1)
                        for a in range(2):
                            mm = pe.matmul(B[d][1][:, a * P:(a + 1) * P], wtn[:, d, a, :], state[:, d, a, :],
                                           start=False, stop=True, skip_group_check=True)
                        mm.then_inc(sem["vn_dve"][d], 1)
                        for a in range(2):
                            pe.matmul(B[d][2][:, a * P:(a + 1) * P], state[:, d, a, :], qd[:, d, a, :],
                                      start=(a == 0), stop=False, skip_group_check=True)
                    for d in range(2):
                        pe.wait_ge(sem["vn_pe"][d], 1)
                        pe.sem_inc(sem["vn_pe"][d], -1)
                        for h in range(H):
                            a, p = h // 2, h % 2
                            mm = pe.matmul(B[d][2][HD * p:HD * (p + 1), a * P:(a + 1) * P], vn[:, d, h, :],
                                           attn[:, d, h, :], start=False, stop=True, skip_group_check=True)
                        mm.then_inc(sem["o_act"][d], 1)
                        for a in range(2):
                            mm = pe.matmul(B[d][3][:, a * P:(a + 1) * P],
                                           kd[:, d, 2 * a:2 * a + 2, :].rearrange("p h f -> p (h f)"),
                                           vn[:, d, 2 * a:2 * a + 2, :].rearrange("p h f -> p (h f)"),
                                           start=True, stop=True)
                        mm.then_inc(sem["su_dve"][d], 1)


def gdn_group(k):
    with k.phase() as st:
        both = k.sb(st, "both", [P, 2, 2, T])
        with ExitStack() as inner:
            qkv = k.sb(inner, "qkv", [P, 6, T])
            bg = k.sb(inner, "bg", [HD, T])
            decay_rows_phase(k, bg)
            jobs = []
            for m in range(6):
                job = Job(T_GDN + m, qkv[:, m, :], taps=m)
                if m < 4:
                    job.width, job.factor = 1.0, (HD ** -0.5 if m < 2 else 1.0)
                jobs.append(job)
            rows_phase(k, jobs)
            gdn_phase(k, qkv, bg, both)
        gate_phase(k, both, 0, T_Z, V_GNORM)


def hgrn_rows_phase(k, q, f, kk, v):
    with k.phase() as st:
        raw = k.sb(st, "raw", [P, 2, T])
        raw_in, raw_free = k.sems(st, "raw_in", 2), k.sems(st, "raw_free", 2)
        sig_dve, own_a, own_v = k.sem(st, "sig_dve"), k.sem(st, "own_a"), k.sem(st, "own_v")
        tiles = [T_HF, T_HF + 1, T_HF + 2, T_HF + 3, T_HQ, T_HQ + 1]
        direct = k.sem(st, "direct")
        with k.nc.Block() as block:
            @block.sync
            def _(sp):
                for j, t in enumerate(tiles):
                    if j >= 2:
                        sp.wait_ge(raw_free[j % 2], 1)
                        sp.sem_inc(raw_free[j % 2], -1)
                    sp.dma_start(raw[:, j % 2, :], k.rows[t]).then_inc(raw_in[j % 2], 16)
                for a in range(2):
                    sp.dma_start(v[:, a, :], k.rows[T_HI + a]).then_inc(direct, 16)
                sp.wait_ge(direct, 32)
                sp.sem_inc(direct, -32)

            @block.scalar
            def _(act):
                for j in range(6):
                    act.wait_ge(raw_in[j % 2], 16)
                    act.sem_inc(raw_in[j % 2], -16)
                    if j < 4:
                        act.activation(f[:, j, :], raw[:, j % 2, :], ACT.Sigmoid)
                        act.activation(kk[:, j, :], raw[:, j % 2, :], ACT.Sigmoid, scale=-1.0).then_inc(own_a, 1)
                        act.wait_ge(own_a, 1)
                        act.sem_inc(own_a, -1)
                        act.sem_inc(raw_free[j % 2], 1)
                        act.sem_inc(sig_dve, 1)
                    else:
                        act.activation(q[:, j - 4, :], raw[:, j % 2, :], ACT.Silu).then_inc(own_a, 1)
                        act.wait_ge(own_a, 1)
                        act.sem_inc(own_a, -1)
                        act.sem_inc(raw_free[j % 2], 1)
                for s in range(2):
                    act.wait_ge(raw_free[s], 1)
                    act.sem_inc(raw_free[s], -1)

            @block.vector
            def _(dve):
                for j in range(4):
                    dve.wait_ge(sig_dve, 1)
                    dve.sem_inc(sig_dve, -1)
                    one_less = k.lb[:, 4 + j:5 + j]
                    dve.tensor_scalar(kk[:, j, :], kk[:, j, :], one_less, None, ALU.mult)
                    last = dve.tensor_scalar(f[:, j, :], f[:, j, :], one_less, k.lb[:, j:j + 1], ALU.mult, ALU.add)
                last.then_inc(own_v, 1)
                dve.wait_ge(own_v, 1)
                dve.sem_inc(own_v, -1)


def hgrn_phase(k, q, f, kk, v, both):
    with k.phase() as st:
        qp = k.sb(st, "qp", [P, 2, 2, P])
        kr = k.sb(st, "kr", [P, 2, 2, P])
        vs = k.sb(st, "vs", [P, 2, 2, P])
        tot = [k.sb(st, f"tot{l}", [P, 2, 2 * (P >> l)]) for l in range(LEVELS + 1)]
        attn = k.sb(st, "attn", [P, 2, H, P])
        krt = k.sb(st, "krt", [P, 2, 2, P])
        vt = k.sb(st, "vt", [P, 2, 2, P])
        state = k.sb(st, "state", [P, 2, 2, P])
        tmp = k.sb(st, "tmp", [P, 2, 2, P])
        B = [[k.banks(st, f"b{d}{b}", 1) for b in range(4)] for d in range(2)]
        names = "staged_pe staged_pool lv_dve read_pool lvl_pe free0_pe free1_pe tr_act attn_pe tok_pe o_act su_dve state_pe".split()
        sem = {n: k.sems(st, n, 2) for n in names}
        own = {e: k.sem(st, f"own_{e}") for e in ("act", "dve", "pool")}
        ident = k.const(C_IDENT)

        def two(b):
            return b[:, 0:2 * P].rearrange("p (a f) -> p a f", f=P)

        with k.nc.Block() as block:
            @block.scalar
            def _(act):
                with act.Fori(0, NT) as i:
                    for d in range(2):
                        col = bass.ds(chunk_of(d, i) * P, P)
                        act.activation(qp[:, d], q[:, :, col], ACT.Copy)
                        act.activation(kr[:, d], kk[:, 2 * d:2 * d + 2, col], ACT.Copy)
                        act.activation(vs[:, d], v[:, :, col], ACT.Copy)
                        act.activation(tot[0][:, d, :].rearrange("p (a f) -> p a f", f=P),
                                       f[:, 2 * d:2 * d + 2, col], ACT.Copy).then_inc(own["act"], 1)
                        act.wait_ge(own["act"], 1)
                        act.sem_inc(own["act"], -1)
                        act.sem_inc(sem["staged_pe"][d], 1)
                    for d in range(2):
                        act.wait_ge(sem["tr_act"][d], 1)
                        act.sem_inc(sem["tr_act"][d], -1)
                        act.activation(krt[:, d], two(B[d][0]), ACT.Copy)
                        act.activation(vt[:, d], two(B[d][1]), ACT.Copy).then_inc(own["act"], 1)
                        act.wait_ge(own["act"], 1)
                        act.sem_inc(own["act"], -1)
                        act.sem_inc(sem["tok_pe"][d], 1)
                    for d in range(2):
                        act.wait_ge(sem["o_act"][d], 1)
                        act.sem_inc(sem["o_act"][d], -1)
                        act.activation(both[:, d, :, bass.ds(chunk_of(d, i) * P, P)], two(B[d][2]),
                                       ACT.Copy).then_inc(own["act"], 1)
                        act.wait_ge(own["act"], 1)
                        act.sem_inc(own["act"], -1)

            @block.vector
            def _(dve):
                dve.memset(attn[:, :, :, :], 0.0)
                dve.memset(state[:, :, :, :], 0.0).then_inc(own["dve"], 1)
                dve.wait_ge(own["dve"], 1)
                dve.sem_inc(own["dve"], -1)
                for d in range(2):
                    dve.sem_inc(sem["state_pe"][d], 1)
                with dve.Fori(0, NT):
                    for l in range(-1, LEVELS):
                        for d in range(2):
                            mask = ident if l < 0 else k.const(C_LVL + (d * LEVELS + l) * P)
                            dve.wait_ge(sem["lv_dve"][d], 1)
                            dve.sem_inc(sem["lv_dve"][d], -1)
                            dve.sem_inc(sem["read_pool"][d], 1)
                            for p in range(2):
                                ins = dve.copy_predicated(attn[:, d, p::2, :], spread(mask, 2).bitcast(U32),
                                                          two(B[d][2 * ((l + 1) % 2) + p]))
                                ins.then_inc(own["dve"], 1)
                                dve.wait_ge(own["dve"], 1)
                                dve.sem_inc(own["dve"], -1)
                            dve.sem_inc(sem["free1_pe" if l % 2 == 0 else "free0_pe"][d], 1)
                    for d in range(2):
                        dve.sem_inc(sem["attn_pe"][d], 1)
                    for d in range(2):
                        dve.wait_ge(sem["su_dve"][d], 1)
                        dve.sem_inc(sem["su_dve"][d], -1)
                        dve.tensor_tensor(tmp[:, d], two(B[d][3]), spread(k.const(C_BLK), 2), ALU.mult)\
                            .then_inc(own["dve"], 1)
                        dve.wait_ge(own["dve"], 1)
                        dve.sem_inc(own["dve"], -1)
                        for a in range(2):
                            dve.scalar_tensor_tensor(state[:, d, a, :], state[:, d, a, :],
                                                     tot[LEVELS][:, d, a:a + 1], tmp[:, d, a, :],
                                                     ALU.mult, ALU.add).then_inc(own["dve"], 1)
                            dve.wait_ge(own["dve"], 1)
                            dve.sem_inc(own["dve"], -1)
                        dve.sem_inc(sem["state_pe"][d], 1)
                for d in range(2):
                    dve.wait_ge(sem["state_pe"][d], 1)
                    dve.sem_inc(sem["state_pe"][d], -1)

            @block.gpsimd
            def _(pool):
                with pool.Fori(0, NT):
                    for d in range(2):
                        pool.wait_ge(sem["read_pool"][d], 1)
                        pool.sem_inc(sem["read_pool"][d], -1)
                        pool.tensor_tensor(qp[:, d].rearrange("p a f -> p (a f)"),
                                           qp[:, d].rearrange("p a f -> p (a f)"), tot[0][:, d, :],
                                           ALU.mult).then_inc(own["pool"], 1)
                        pool.wait_ge(own["pool"], 1)
                        pool.sem_inc(own["pool"], -1)
                        pool.sem_inc(sem["lvl_pe"][d], 1)
                    for l in range(LEVELS):
                        w = 1 << l
                        for d in range(2):
                            late, early = (1, 0) if d == 0 else (0, 1)
                            blocks = tot[l][:, d, :].rearrange("p (n x) -> p n x", x=2)
                            qv = qp[:, d].rearrange("p a f -> p (a f)").rearrange("p (n x w) -> p n x w", x=2, w=w)
                            kv = kr[:, d].rearrange("p a f -> p (a f)").rearrange("p (n x w) -> p n x w", x=2, w=w)
                            pool.wait_ge(sem["read_pool"][d], 1)
                            pool.sem_inc(sem["read_pool"][d], -1)
                            pool.tensor_tensor(qv[:, :, late, :], qv[:, :, late, :], widen(blocks[:, :, early], w),
                                               ALU.mult)
                            pool.tensor_tensor(kv[:, :, early, :], kv[:, :, early, :], widen(blocks[:, :, late], w),
                                               ALU.mult)
                            pool.tensor_tensor(tot[l + 1][:, d, :], blocks[:, :, 0], blocks[:, :, 1],
                                               ALU.mult).then_inc(own["pool"], 1)
                            pool.wait_ge(own["pool"], 1)
                            pool.sem_inc(own["pool"], -1)
                            pool.sem_inc(sem["lvl_pe"][d], 1)

            @block.tensor
            def _(pe):
                with pe.Fori(0, NT):
                    for l in range(-1, LEVELS):
                        for d in range(2):
                            if l < 0:
                                pe.wait_ge(sem["staged_pe"][d], 1)
                                pe.sem_inc(sem["staged_pe"][d], -1)
                            else:
                                pe.wait_ge(sem["lvl_pe"][d], 1)
                                pe.sem_inc(sem["lvl_pe"][d], -1)
                            if l >= 1:
                                pe.wait_ge(sem["free0_pe" if l % 2 else "free1_pe"][d], 1)
                                pe.sem_inc(sem["free0_pe" if l % 2 else "free1_pe"][d], -1)
                            for h in range(H):
                                rows, a = slice(HD * (h % 2), HD * (h % 2 + 1)), h // 2
                                mm = pe.matmul(B[d][2 * ((l + 1) % 2) + h % 2][:, a * P:(a + 1) * P], kr[rows, d, a, :],
                                               qp[rows, d, a, :], start=True, stop=True)
                            mm.then_inc(sem["lv_dve"][d], 1)
                    for d in range(2):
                        pe.wait_ge(sem["lvl_pe"][d], 1)
                        pe.sem_inc(sem["lvl_pe"][d], -1)
                        pe.wait_ge(sem["free0_pe"][d], 1)
                        pe.sem_inc(sem["free0_pe"][d], -1)
                        pe.wait_ge(sem["free1_pe"][d], 1)
                        pe.sem_inc(sem["free1_pe"][d], -1)
                        for a in range(2):
                            pe.transpose(B[d][0][:, a * P:(a + 1) * P], kr[:, d, a, :], ident)
                        for a in range(2):
                            mm = pe.transpose(B[d][1][:, a * P:(a + 1) * P], vs[:, d, a, :], ident)
                        mm.then_inc(sem["tr_act"][d], 1)
                    for d in range(2):
                        pe.wait_ge(sem["state_pe"][d], 1)
                        pe.sem_inc(sem["state_pe"][d], -1)
                        for a in range(2):
                            pe.matmul(B[d][2][:, a * P:(a + 1) * P], state[:, d, a, :], qp[:, d, a, :],
                                      start=(a == 0), stop=False, skip_group_check=True)
                        pe.wait_ge(sem["attn_pe"][d], 1)
                        pe.sem_inc(sem["attn_pe"][d], -1)
                        pe.wait_ge(sem["tok_pe"][d], 1)
                        pe.sem_inc(sem["tok_pe"][d], -1)
                        for h in range(H):
                            a, p = h // 2, h % 2
                            mm = pe.matmul(B[d][2][HD * p:HD * (p + 1), a * P:(a + 1) * P],
                                           vt[:, d, a, HD * p:HD * (p + 1)], attn[:, d, h, :],
                                           start=False, stop=True, skip_group_check=True)
                        mm.then_inc(sem["o_act"][d], 1)
                        for a in range(2):
                            mm = pe.matmul(B[d][3][:, a * P:(a + 1) * P], krt[:, d, a, :], vt[:, d, a, :],
                                           start=True, stop=True)
                        mm.then_inc(sem["su_dve"][d], 1)


def hgrn_group(k):
    with k.phase() as st:
        both = k.sb(st, "both", [P, 2, 2, T])
        with ExitStack() as inner:
            q, v = k.sb(inner, "q", [P, 2, T]), k.sb(inner, "v", [P, 2, T])
            f, kk = k.sb(inner, "f", [P, 4, T]), k.sb(inner, "kk", [P, 4, T])
            hgrn_rows_phase(k, q, f, kk, v)
            hgrn_phase(k, q, f, kk, v, both)
        gate_phase(k, both, 6, T_HG, V_HNORM)


def attention_phase(k, q, kT, vt, oT_tile, window, band, sink, with_ctx):
    with k.phase() as st:
        qs = k.sb(st, "qs", [P, 2, P])
        near = k.sb(st, "near", [P, 2, 3 * P])
        prob = k.sb(st, "prob", [P, 2, T])
        probT = k.sb(st, "probT", [P, 2, NT, P])
        otok = k.sb(st, "otok", [P, 2 * P])
        mx = k.sb(st, "mx", [P, 2, 2])
        tot = k.sb(st, "tot", [P, 2, 2])
        ps = [k.banks(st, f"score{s}", 3) for s in range(2)]
        turned_ps = k.banks(st, "turned", 1)
        out_ps = k.banks(st, "out", 1)
        q_pe = k.sem(st, "q_pe")
        names = "score_dve mx_act prob_pe sum_dve turn_full turn_free".split()
        sem = {n: k.sems(st, n, 2) for n in names}
        out_dve, out_free, otok_pe, turn_out, out_taken = (
            k.sem(st, n) for n in ("out_dve", "out_free", "otok_pe", "turn_out", "out_taken"))
        own = {e: k.sem(st, f"own_{e}") for e in ("act", "dve")}
        scale = HD ** -0.5

        def width(kind):
            return {"ctx": CTX, "all": T, "first": CTX + 2 * P, "last": CTX + 2 * P, "middle": CTX + 3 * P}[kind]

        def score_parts(x, g, parity, kind):
            rows = slice(HD * g, HD * (g + 1))
            query = qs[rows, x, :]
            if kind == "all":
                return [(lo, query, kT[rows, lo:lo + w]) for lo, w in SEGS]
            parts = [(256, query, kT[rows, SEQ:T])]
            if kind != "ctx":
                parts.append((512, query, near[rows, parity, 0:width(kind) - CTX]))
            if window:
                parts.append((256 + width(kind), k.consts[rows, C_ONES:C_ONES + P], sink[rows, 2 * g + x:2 * g + x + 1]))
            return parts

        def span(kind):
            lo = 0 if kind == "all" else 256
            return lo, lo + width(kind) + (1 if window else 0)

        def key_chunk(chunk, kind, j):
            if kind == "all":
                return j
            if j < CTX // P:
                return SEQ // P + j
            return chunk + j - CTX // P - (0 if kind == "first" else 1)

        def batches(kind):
            n = width(kind) // P
            size = 4 if n > 5 else (n + 1) // 2 if n > 2 else n
            return [(c, min(size, n - c), i % 2) for i, c in enumerate(range(0, n, size))]

        def columns(chunk):
            return bass.ds(chunk * P, P)

        def score_product(pe, part, g, last):
            col, stationary, moving = part
            mm = pe.matmul(ps[g][:, col:col + moving.shape[1]], stationary, moving, start=True, stop=True)
            if last:
                mm.then_inc(sem["score_dve"][g], 1)

        def tensor_first(pe, chunk, parity, kind):
            pe.wait_ge(q_pe, 1)
            pe.sem_inc(q_pe, -1)
            for g in range(2):
                parts = score_parts(0, g, parity, kind)
                for i, part in enumerate(parts):
                    score_product(pe, part, g, i == len(parts) - 1)

        def tensor_out(pe):
            pe.wait_ge(otok_pe, 1)
            pe.sem_inc(otok_pe, -1)
            for a in range(2):
                mm = pe.transpose(turned_ps[:, a * P:(a + 1) * P], otok[:, a * P:(a + 1) * P], k.const(C_IDENT))
            mm.then_inc(turn_out, 1)
            pe.wait_ge(out_taken, 1)
            pe.sem_inc(out_taken, -1)

        def tensor_step(pe, prev, cur, nxt):
            chunk, parity, kind = cur
            for h in range(4):
                x, g = h // 2, h % 2
                if h < 2:
                    parts = score_parts(1, g, parity, kind)
                else:
                    parts = score_parts(0, g, nxt[1], nxt[2]) if nxt else []
                if h % 2 == 0 and parts:
                    pe.wait_ge(q_pe, 1)
                    pe.sem_inc(q_pe, -1)
                pe.wait_ge(sem["prob_pe"][g], 1)
                pe.sem_inc(sem["prob_pe"][g], -1)
                turns = batches(kind)
                done = 0
                for i, (c, n, b) in enumerate(turns):
                    for j in range(c, c + n):
                        mm = pe.transpose(turned_ps[:, (j - c) * P:(j - c + 1) * P], prob[:, g, j * P:(j + 1) * P],
                                          k.const(C_IDENT))
                    mm.then_inc(sem["turn_full"][b], 1)
                    if done < len(parts):
                        score_product(pe, parts[done], g, done == len(parts) - 1)
                        done += 1
                    pe.wait_ge(sem["turn_free"][b], 1)
                    pe.sem_inc(sem["turn_free"][b], -1)
                if h == 0 and prev is not None:
                    tensor_out(pe)
                while done < len(parts):
                    score_product(pe, parts[done], g, done == len(parts) - 1)
                    done += 1
                pe.wait_ge(out_free, 1)
                pe.sem_inc(out_free, -1)
                for j in range(width(kind) // P):
                    mm = pe.matmul(out_ps[:, 0:HD], probT[:, g, j, :],
                                   vt[:, key_chunk(chunk, kind, j), HD * g:HD * (g + 1)],
                                   start=(j == 0), stop=(j == width(kind) // P - 1))
                mm.then_inc(out_dve, 1)

        def exponentials(act, g, kind):
            lo, hi = span(kind)
            act.wait_ge(sem["mx_act"][g], 1)
            act.sem_inc(sem["mx_act"][g], -1)
            act.activation(prob[:, g, 0:hi - lo], ps[g][:, lo:hi], ACT.Exp, bias=mx[:, g, 1:2],
                           scale=scale, accum_out=tot[:, g, 0:1]).then_inc(own["act"], 1)
            act.wait_ge(own["act"], 1)
            act.sem_inc(own["act"], -1)
            act.sem_inc(sem["prob_pe"][g], 1)
            act.sem_inc(sem["sum_dve"][g], 1)

        def copy_near(act, cur):
            chunk, parity, kind = cur
            if window and kind != "ctx":
                start = (chunk if kind == "first" else chunk - 1) * P
                w = width(kind) - CTX
                act.activation(near[:, parity, 0:w], kT[:, bass.ds(start, w)], ACT.Copy)

        def scalar_first(act, cur):
            copy_near(act, cur)
            act.activation(qs[:, 1, :], q[:, 1, columns(cur[0])], ACT.Copy)
            act.activation(qs[:, 0, :], q[:, 0, columns(cur[0])], ACT.Copy).then_inc(own["act"], 1)
            act.wait_ge(own["act"], 1)
            act.sem_inc(own["act"], -1)
            act.sem_inc(q_pe, 1)
            act.sem_inc(q_pe, 1)
            for g in range(2):
                exponentials(act, g, cur[2])

        def scalar_out(act, prev):
            act.wait_ge(turn_out, 1)
            act.sem_inc(turn_out, -1)
            act.activation(k.oT[:, oT_tile:oT_tile + 2, columns(prev[0])],
                           turned_ps[:, 0:2 * P].rearrange("p (a f) -> p a f", f=P), ACT.Copy)\
                .then_inc(own["act"], 1)
            act.wait_ge(own["act"], 1)
            act.sem_inc(own["act"], -1)
            act.sem_inc(out_taken, 1)

        def turn(eng, g, b, kind, copy, name):
            for c, n, bb in batches(kind):
                if bb == b:
                    eng.wait_ge(sem["turn_full"][b], 1)
                    eng.sem_inc(sem["turn_full"][b], -1)
                    copy(probT[:, g, c:c + n, :],
                         turned_ps[:, 0:n * P].rearrange("p (c f) -> p c f", f=P)).then_inc(own[name], 1)
                    eng.wait_ge(own[name], 1)
                    eng.sem_inc(own[name], -1)
                    eng.sem_inc(sem["turn_free"][b], 1)

        def scalar_step(act, prev, cur, nxt):
            for h in range(4):
                g = h % 2
                turn(act, g, 0, cur[2], lambda o, s: act.activation(o, s, ACT.Copy), "act")
                if h == 0 and prev is not None:
                    scalar_out(act, prev)
                if h == 0 and nxt:
                    copy_near(act, nxt)
                if h < 2:
                    exponentials(act, g, cur[2])
                elif nxt:
                    exponentials(act, g, nxt[2])
                if h % 2 and nxt:
                    act.activation(qs[:, h // 2, :], q[:, h // 2, columns(nxt[0])], ACT.Copy).then_inc(own["act"], 1)
                    act.wait_ge(own["act"], 1)
                    act.sem_inc(own["act"], -1)
                    act.sem_inc(q_pe, 1)

        def maximum(dve, g, kind):
            lo, hi = span(kind)
            dve.wait_ge(sem["score_dve"][g], 1)
            dve.sem_inc(sem["score_dve"][g], -1)
            for col, m in {"first": [(512 + P, 2)], "last": [(512, 0)],
                           "middle": [(512, 0), (512 + 2 * P, 2)]}.get(kind, []):
                part = ps[g][:, col:col + P]
                dve.tensor_tensor(part, part, band[:, m * P:(m + 1) * P], ALU.add).then_inc(own["dve"], 1)
                dve.wait_ge(own["dve"], 1)
                dve.sem_inc(own["dve"], -1)
            dve.reduce_max(mx[:, g, 0:1], ps[g][:, lo:hi], AX_X).then_inc(own["dve"], 1)
            dve.wait_ge(own["dve"], 1)
            dve.sem_inc(own["dve"], -1)
            dve.tensor_scalar(mx[:, g, 1:2], mx[:, g, 0:1], -scale, None, ALU.mult).then_inc(own["dve"], 1)
            dve.wait_ge(own["dve"], 1)
            dve.sem_inc(own["dve"], -1)
            dve.sem_inc(sem["mx_act"][g], 1)

        def vector_first(dve, cur):
            for g in range(2):
                maximum(dve, g, cur[2])

        def vector_step(dve, prev, cur, nxt):
            for h in range(4):
                x, g = h // 2, h % 2
                head = 2 * g + x
                dve.wait_ge(sem["sum_dve"][g], 1)
                dve.sem_inc(sem["sum_dve"][g], -1)
                dve.reciprocal(tot[:, g, 1:2], tot[:, g, 0:1]).then_inc(own["dve"], 1)
                dve.wait_ge(own["dve"], 1)
                dve.sem_inc(own["dve"], -1)
                turn(dve, g, 1, cur[2], dve.tensor_copy, "dve")
                if h < 2:
                    maximum(dve, g, cur[2])
                elif nxt:
                    maximum(dve, g, nxt[2])
                dve.wait_ge(out_dve, 1)
                dve.sem_inc(out_dve, -1)
                dve.tensor_scalar(otok[:, head * HD:(head + 1) * HD], out_ps[:, 0:HD], tot[:, g, 1:2],
                                  None, ALU.mult).then_inc(own["dve"], 1)
                dve.wait_ge(own["dve"], 1)
                dve.sem_inc(own["dve"], -1)
                dve.sem_inc(out_free, 1)
            dve.sem_inc(otok_pe, 1)

        last_latent = SEQ // P - 1
        tail = [(c, 0, "ctx") for c in range(SEQ // P, NT)] if with_ctx else []

        def chunks(eng, step):
            if window:
                step(eng, None, (0, 0, "first"), (1, 1, "middle"))
                with eng.Fori(0, 2) as i:
                    for u in range(2):
                        step(eng, (2 * i + u, u, ""), (2 * i + u + 1, 1 - u, "middle"), (2 * i + u + 2, u, "middle"))
                step(eng, (4, 0, ""), (5, 1, "middle"), (6, 0, "middle"))
                step(eng, (5, 1, ""), (6, 0, "middle"), (7, 1, "last"))
                step(eng, (6, 0, ""), (7, 1, "last"), tail[0] if tail else None)
            else:
                step(eng, None, (0, 0, "all"), (1, 0, "all"))
                with eng.Fori(1, last_latent) as i:
                    step(eng, (i - 1, 0, ""), (i, 0, "all"), (i + 1, 0, "all"))
                step(eng, (last_latent - 1, 0, ""), (last_latent, 0, "all"), tail[0] if tail else None)
            for n, cur in enumerate(tail):
                step(eng, (cur[0] - 1, 0, ""), cur, tail[n + 1] if n + 1 < len(tail) else None)

        first = (0, 0, "first" if window else "all")
        final = (tail[-1] if tail else (last_latent, 0, ""))
        with k.nc.Block() as block:
            @block.tensor
            def _(pe):
                tensor_first(pe, *first)
                chunks(pe, tensor_step)
                tensor_out(pe)

            @block.scalar
            def _(act):
                scalar_first(act, first)
                chunks(act, scalar_step)
                scalar_out(act, final)

            @block.vector
            def _(dve):
                dve.sem_inc(out_free, 1)
                vector_first(dve, first)
                chunks(dve, vector_step)
                dve.wait_ge(out_free, 1)
                dve.sem_inc(out_free, -1)


def trig_phase(k, a, trig):
    with k.phase() as st:
        came = k.sem(st, "came")
        with k.nc.Block() as block:
            @block.sync
            def _(sp):
                sp.dma_start(trig[:, :], a["consts"][:, N_MIX:NC]).then_inc(came, 16)
                sp.wait_ge(came, 16)
                sp.sem_inc(came, -16)


def attention_groups(k, a, with_ctx):
    with k.phase() as st:
        table = k.sb(st, "trig", [P, NC - N_MIX])
        band, trig = table[:, 0:3 * P], table[:, 3 * P:]
        trig_phase(k, a, table)
        for window, tq, tk, tv, out in ((False, T_BQ, T_BK, T_BV, 2), (True, T_CQ, T_CK, T_CV, 4)):
            with ExitStack() as inner:
                k.count += 1
                q = k.sb(inner, "q", [P, 2, T])
                kT = k.sb(inner, "kT", [P, T])
                vT = k.sb(inner, "vT", [P, T])
                vt = k.sb(inner, "vt", [P, NT, P])
                jobs = [Job(tq, q[:, 0, :], rope=True), Job(tq + 1, q[:, 1, :], rope=True), Job(tk, kT[:, :], rope=True)]
                if not window:
                    for job, col in zip(jobs, (V_QNORM, V_QNORM, V_KNORM)):
                        job.width, job.factor = HD, k.vec(col)
                jobs.append(Job(tv, vT[:, :], to_tokens=vt))
                rows_phase(k, jobs, trig)
                attention_phase(k, q, kT, vt, out, window, band, k.sink, with_ctx)


def ffn_phase(k, a, layer, n):
    with k.phase() as st:
        f = k.xT
        wu_hi = k.sb(st, "wu_hi", [P, 2, KD, P], F32R)
        wu_raw, wu_lo = k.twin(st, "wu_raw", [P, 2, KD, P])
        wd_hi = k.sb(st, "wd_hi", [P, FG, D_MODEL], F32R)
        wd_raw, wd_lo = k.twin(st, "wd_raw", [P, FG, D_MODEL])
        g_hi = k.sb(st, "g_hi", [P, 2, FG, T], F32R)
        g_whole, g_lo = k.twin(st, "g_whole", [P, 2, FG, T])
        y = k.sb(st, "y", [P, 2, T])
        ps = [k.banks(st, f"ps{s}", 3) for s in range(2)]
        wu_in, wu_free, wu_pool, wu_pe = (k.sems(st, s, 2) for s in ("wu_in", "wu_free", "wu_pool", "wu_pe"))
        wd_in, wd_free, wd_pool, wd_pe = (k.sems(st, s, 2) for s in ("wd_in", "wd_free", "wd_pool", "wd_pe"))
        up_act, down_dve, ps_free, centre_dve, y_free = (
            k.sems(st, s, 2) for s in ("up_act", "down_dve", "ps_free", "centre_dve", "y_free"))
        taps_act, gate_pool, value_pool, whole_act, hi_pool, g_pe = (
            k.sem(st, s) for s in ("taps_act", "gate_pool", "value_pool", "whole_act", "hi_pool", "g_pe"))
        own = {e: k.sem(st, f"own_{e}") for e in ("act", "dve", "pool")}
        parts = conv_parts(n)
        spilled_dve = k.sem(st, "spilled_dve")
        norm = Norm(k, st, n, 3, 4, y, g_whole[:, 1, 0, :], g_whole[:, 1, 1, :], ps[1], spill=k.x_dram)

        def load_up(sp, j, u, s):
            sp.wait_ge(wu_free[s], 1)
            sp.sem_inc(wu_free[s], -1)
            sp.dma_start(wu_raw[:, s], a["w_up"][layer, s * KF + j * FG + u]).then_inc(wu_in[s], 16)

        def load_down(sp, j):
            for u in range(FG):
                sp.wait_ge(wd_free[u], 1)
                sp.sem_inc(wd_free[u], -1)
                sp.dma_start(wd_raw[:, u], a["w_down"][layer, j * FG + u]).then_inc(wd_in[u], 16)

        def sync_group(sp, j, first=False, last=False):
            if not first:
                load_down(sp, j - 1)
            for s in range(2):
                load_up(sp, j, 1, s)
            if not last:
                for s in range(2):
                    load_up(sp, j + 1, 0, s)

        def tensor_up(pe, first=False):
            for u in range(FG):
                for s in range(2):
                    ready = (norm.even_pe, norm.odd_pe) if first and u + s == 0 else None
                    pe.wait_ge(wu_pe[s], 1)
                    pe.sem_inc(wu_pe[s], -1)
                    pe.wait_ge(ps_free[s], 1)
                    pe.sem_inc(ps_free[s], -1)
                    split_products(pe, ps[s], (wu_hi[:, s], wu_lo[:, s]), (k.hi, k.lo), KD, n, ready)\
                        .then_inc(up_act[s], 1)

        def tensor_down(pe, parity):
            for u in range(FG):
                pe.wait_ge(wd_pe[u], 1)
                pe.sem_inc(wd_pe[u], -1)
            pe.wait_ge(g_pe, FG)
            pe.sem_inc(g_pe, -FG)
            for o in range(KD):
                s, cols = o % 2, slice(o * P, (o + 1) * P)
                pe.wait_ge(ps_free[s], 1)
                pe.sem_inc(ps_free[s], -1)
                split_products(pe, ps[s], (wd_hi[:, :, cols], wd_lo[:, :, cols]), (g_hi[:, parity], g_lo[:, parity]),
                               FG, n).then_inc(down_dve[s], 1)

        def round_up(act, s):
            act.wait_ge(wu_in[s], 16)
            act.sem_inc(wu_in[s], -16)
            act.activation(wu_hi[:, s], wu_raw[:, s], ACT.Copy).then_inc(own["act"], 1)
            act.wait_ge(own["act"], 1)
            act.sem_inc(own["act"], -1)
            act.sem_inc(wu_pool[s], 1)

        def round_down(act):
            for u in range(FG):
                act.wait_ge(wd_in[u], 16)
                act.sem_inc(wd_in[u], -16)
                act.activation(wd_hi[:, u], wd_raw[:, u], ACT.Copy).then_inc(own["act"], 1)
                act.wait_ge(own["act"], 1)
                act.sem_inc(own["act"], -1)
                act.sem_inc(wd_pool[u], 1)

        def centre(act, j, u, s):
            act.wait_ge(up_act[s], 1)
            act.sem_inc(up_act[s], -1)
            act.sem_inc(wu_free[s], 1)
            act.wait_ge(y_free[s], 1)
            act.sem_inc(y_free[s], -1)
            act.activation(k.taps[:, s, 0:4], k.vecs[:, bass.ds(V_FCONV + s * KF + j * FG + u, 4, 2 * KF)],
                           ACT.Copy).then_inc(own["act"], 1)
            act.wait_ge(own["act"], 1)
            act.sem_inc(own["act"], -1)
            act.activation(y[:, s, 0:n], ps[s][:, 0:n], ACT.Identity, scale=k.taps[:, s, 1:2],
                           bias=k.taps[:, s, 3:4]).then_inc(own["act"], 1)
            act.wait_ge(own["act"], 1)
            act.sem_inc(own["act"], -1)
            act.sem_inc(centre_dve[s], 1)

        def scalar_group(act, j, parity, first=False, last=False):
            for u in range(FG):
                more = u == 0 or not last
                centre(act, j, u, 0)
                if more:
                    round_up(act, 0)
                act.wait_ge(taps_act, 1)
                act.sem_inc(taps_act, -1)
                act.activation(y[:, 0, 0:n], y[:, 0, 0:n], ACT.Silu).then_inc(own["act"], 1)
                act.wait_ge(own["act"], 1)
                act.sem_inc(own["act"], -1)
                act.sem_inc(gate_pool, 1)
                centre(act, j, u, 1)
                if more:
                    round_up(act, 1)
                if u == 0 and not first:
                    round_down(act)
                act.wait_ge(whole_act, 1)
                act.sem_inc(whole_act, -1)
                act.activation(g_hi[:, parity, u, 0:n], g_whole[:, parity, u, 0:n], ACT.Copy).then_inc(own["act"], 1)
                act.wait_ge(own["act"], 1)
                act.sem_inc(own["act"], -1)
                act.sem_inc(hi_pool, 1)

        def vector_up(dve):
            for u in range(FG):
                for s in range(2):
                    dve.wait_ge(centre_dve[s], 1)
                    dve.sem_inc(centre_dve[s], -1)
                    for lo, hi in parts:
                        dve.scalar_tensor_tensor(y[:, s, lo + 1:hi], ps[s][:, lo:hi - 1],
                                                 k.taps[:, s, 0:1], y[:, s, lo + 1:hi],
                                                 ALU.mult, ALU.add).then_inc(own["dve"], 1)
                        dve.wait_ge(own["dve"], 1)
                        dve.sem_inc(own["dve"], -1)
                        dve.scalar_tensor_tensor(y[:, s, lo:hi - 1], ps[s][:, lo + 1:hi],
                                                 k.taps[:, s, 2:3], y[:, s, lo:hi - 1],
                                                 ALU.mult, ALU.add).then_inc(own["dve"], 1)
                        dve.wait_ge(own["dve"], 1)
                        dve.sem_inc(own["dve"], -1)
                    dve.sem_inc(ps_free[s], 1)
                    dve.sem_inc(value_pool if s else taps_act, 1)

        def vector_down(dve):
            for o in range(KD):
                s = o % 2
                dve.wait_ge(down_dve[s], 1)
                dve.sem_inc(down_dve[s], -1)
                if o == KD - 1:
                    for u in range(FG):
                        dve.sem_inc(wd_free[u], 1)
                dve.tensor_tensor(f[:, o, 0:n], ps[s][:, 0:n], f[:, o, 0:n], ALU.add).then_inc(own["dve"], 1)
                dve.wait_ge(own["dve"], 1)
                dve.sem_inc(own["dve"], -1)
                dve.sem_inc(ps_free[s], 1)

        def rest_up(pool, s):
            pool.wait_ge(wu_pool[s], 1)
            pool.sem_inc(wu_pool[s], -1)
            pool.tensor_tensor(wu_lo[:, s], wu_raw[:, s], wu_hi[:, s].bitcast(F32), ALU.subtract)\
                .then_inc(own["pool"], 1)
            pool.wait_ge(own["pool"], 1)
            pool.sem_inc(own["pool"], -1)
            pool.sem_inc(wu_pe[s], 1)

        def rest_down(pool):
            for u in range(FG):
                pool.wait_ge(wd_pool[u], 1)
                pool.sem_inc(wd_pool[u], -1)
                pool.tensor_tensor(wd_lo[:, u], wd_raw[:, u], wd_hi[:, u].bitcast(F32), ALU.subtract)\
                    .then_inc(own["pool"], 1)
                pool.wait_ge(own["pool"], 1)
                pool.sem_inc(own["pool"], -1)
                pool.sem_inc(wd_pe[u], 1)

        def pool_group(pool, parity, first=False, last=False):
            for u in range(FG):
                if u == 0 or not last:
                    for s in range(2):
                        rest_up(pool, s)
                pool.wait_ge(gate_pool, 1)
                pool.sem_inc(gate_pool, -1)
                pool.wait_ge(value_pool, 1)
                pool.sem_inc(value_pool, -1)
                pool.tensor_tensor(g_whole[:, parity, u, 0:n], y[:, 0, 0:n], y[:, 1, 0:n], ALU.mult)\
                    .then_inc(own["pool"], 1)
                pool.wait_ge(own["pool"], 1)
                pool.sem_inc(own["pool"], -1)
                pool.sem_inc(y_free[0], 1)
                pool.sem_inc(y_free[1], 1)
                pool.sem_inc(whole_act, 1)
                if u == 0 and not first:
                    rest_down(pool)
                pool.wait_ge(hi_pool, 1)
                pool.sem_inc(hi_pool, -1)
                pool.tensor_tensor(g_lo[:, parity, u, 0:n], g_whole[:, parity, u, 0:n],
                                   g_hi[:, parity, u, 0:n].bitcast(F32), ALU.subtract).then_inc(own["pool"], 1)
                pool.wait_ge(own["pool"], 1)
                pool.sem_inc(own["pool"], -1)
                pool.sem_inc(g_pe, 1)

        with k.nc.Block() as block:
            @block.sync
            def _(sp):
                norm.sync(sp)
                for s in range(2):
                    load_up(sp, 0, 0, s)
                sp.wait_ge(norm.spilled, 16)
                sp.sem_inc(norm.spilled, -16)
                sp.sem_inc(spilled_dve, 1)
                sync_group(sp, 0, first=True)
                with sp.Fori(0, N_FG // 2 - 1) as i:
                    for b in range(2):
                        sync_group(sp, i * 2 + (1 + b))
                sync_group(sp, N_FG - 2)
                sync_group(sp, N_FG - 1, last=True)
                load_down(sp, N_FG - 1)

            @block.tensor
            def _(pe):
                norm.tensor(pe)
                tensor_up(pe, first=True)
                with pe.Fori(0, N_FG // 2) as i:
                    for b in range(2):
                        tensor_up(pe)
                        tensor_down(pe, b)
                tensor_down(pe, 0)

            @block.scalar
            def _(act):
                for s in range(2):
                    act.sem_inc(wu_free[s], 1)
                norm.scalar(act, lambda: [round_up(act, s) for s in range(2)])
                scalar_group(act, 0, 0, first=True)
                with act.Fori(0, N_FG // 2 - 1) as i:
                    for b in range(2):
                        scalar_group(act, i * 2 + (1 + b), 1 - b)
                scalar_group(act, N_FG - 2, 1)
                scalar_group(act, N_FG - 1, 0, last=True)
                round_down(act)
                for s in range(2):
                    act.wait_ge(wu_free[s], 1)
                    act.sem_inc(wu_free[s], -1)

            @block.vector
            def _(dve):
                for s in range(2):
                    dve.sem_inc(ps_free[s], 1)
                    dve.sem_inc(wd_free[s], 1)
                norm.vector(dve, lambda: None)
                dve.wait_ge(spilled_dve, 1)
                dve.sem_inc(spilled_dve, -1)
                dve.memset(f[:, :, :], 0.0).then_inc(own["dve"], 1)
                dve.wait_ge(own["dve"], 1)
                dve.sem_inc(own["dve"], -1)
                vector_up(dve)
                with dve.Fori(0, N_FG // 2) as i:
                    for b in range(2):
                        vector_up(dve)
                        vector_down(dve)
                vector_down(dve)
                for s in range(2):
                    dve.wait_ge(ps_free[s], 1)
                    dve.sem_inc(ps_free[s], -1)
                    dve.wait_ge(wd_free[s], 1)
                    dve.sem_inc(wd_free[s], -1)

            @block.gpsimd
            def _(pool):
                for s in range(2):
                    pool.sem_inc(y_free[s], 1)
                norm.gpsimd(pool, lambda: [rest_up(pool, s) for s in range(2)])
                pool_group(pool, 0, first=True)
                with pool.Fori(0, N_FG // 2 - 1) as i:
                    for b in range(2):
                        pool_group(pool, 1 - b)
                pool_group(pool, 1)
                pool_group(pool, 0, last=True)
                rest_down(pool)
                for s in range(2):
                    pool.wait_ge(y_free[s], 1)
                    pool.sem_inc(y_free[s], -1)


def store_phase(k, a):
    with k.phase() as st:
        done = k.sem(st, "done")
        with k.nc.Block() as block:
            @block.sync
            def _(sp):
                sp.dma_start(a["out"], k.xT[:, :, 0:SEQ]).then_inc(done, 16)
                sp.wait_ge(done, 16)
                sp.sem_inc(done, -16)


def build(nc, a):
    k = Chip(nc)
    with ExitStack() as st:
        k.rows = nc.dram_tensor("rows", (N_IN, P, T), F32).ap()
        k.x_dram = nc.dram_tensor("x_spilled", (P, KD, T), F32).ap()
        k.consts = k.sb(st, "consts", [P, N_BASE])
        k.all_vecs = k.sb(st, "vecs", [P, DEPTH, NV])
        k.ada_b = k.sb(st, "ada_b", [P, N_BLOCKS])
        k.all_mods = k.sb(st, "mods", [P, N_BLOCKS, 2])
        k.eps = k.sb(st, "eps", [P, 1])
        k.dots = k.sb(st, "dots", [P, 5, 2])
        k.all_lb = k.sb(st, "lb", [P, DEPTH, 8])
        k.all_expa = k.sb(st, "expa", [P, DEPTH, 1])
        k.all_sink = k.sb(st, "sink", [P, DEPTH, H])
        k.taps = k.sb(st, "taps", [P, 2, 4])
        k.xT = k.sb(st, "xT", [P, KD, T])
        load_phase(k, a)
        for layer in range(DEPTH):
            with_ctx = layer < DEPTH - 1
            n = T if with_ctx else SEQ
            k.vecs, k.lb, k.expa, k.sink = (t[:, layer, :] for t in (k.all_vecs, k.all_lb, k.all_expa, k.all_sink))
            k.mods = k.all_mods[:, layer * N_MOD * KD:(layer + 1) * N_MOD * KD, :]
            with ExitStack() as mixers:
                k.count += 1
                k.mix = k.sb(mixers, "mix", [P, N_MIX - N_BASE])
                with ExitStack() as inner:
                    k.hi = k.sb(inner, "h_hi", [P, KD, T], F32R)
                    k.h, k.lo = k.twin(inner, "h_whole", [P, KD, T])
                    input_projection_phase(k, a, layer)
                k.oT, k.o_lo = k.twin(mixers, "oT", [P, KD, T])
                gdn_group(k)
                attention_groups(k, a, with_ctx)
                hgrn_group(k)
                with ExitStack() as inner:
                    k.count += 1
                    y = k.sb(inner, "mixed", [P, KD, T])
                    output_projection_phase(k, a, layer, y, n)
                    residual_phase(k, y, k.xT, n, 2)
            with ExitStack() as inner:
                k.count += 1
                k.hi = k.sb(inner, "h_hi", [P, KD, T], F32R)
                k.h, k.lo = k.twin(inner, "h_whole", [P, KD, T])
                ffn_phase(k, a, layer, n)
            with ExitStack() as inner:
                k.count += 1
                x = k.sb(inner, "x_old", [P, KD, T])
                residual_phase(k, k.xT, x, n, 5, reload=k.x_dram)
        store_phase(k, a)


def layouts(x, c, ctx, c_ctx, ada_w, ada_b, norm_pre_mix, norm_post_mix, norm_pre_ffn, norm_post_ffn,
            w_in, w_out, gdn_conv_w, gdn_a_log, gdn_dt_bias, gdn_norm, attn_q_norm, attn_k_norm,
            swa_sink, hgrn_lb_raw, hgrn_norm, ffn_w_up, ffn_conv_w, ffn_conv_b, ffn_w_down):
    def cols(v):
        return np.asarray(v).reshape(-1, P).T

    def tiles(w, n_k):
        return np.asarray(w).reshape(n_k, P, -1, P).transpose(2, 1, 0, 3)

    out = {"xT": np.concatenate([np.asarray(x)[0], np.asarray(ctx)[0]]).T.reshape(KD, P, T).transpose(1, 0, 2)}
    out["cond"] = np.tile(np.stack([np.asarray(c)[0], np.asarray(c_ctx)]), (P, 1, 1))
    ada = np.asarray(ada_w).transpose(0, 2, 1).reshape(-1, P, D_MODEL)
    ada = np.concatenate([ada, np.zeros((N_BLOCKS - len(ada), P, D_MODEL), ada.dtype)])
    out["ada_first"] = ada[:N_FIRST].transpose(1, 0, 2)
    for l in range(DEPTH):
        part = ada[ITEM_START[l]:ITEM_START[l] + N_IN * ITEM[l]]
        out[f"ada_rest{l}"] = part.reshape(N_IN, ITEM[l], P, D_MODEL).transpose(0, 2, 1, 3)
    out["ada_b"] = np.zeros((P, N_BLOCKS), np.float32)
    out["ada_b"][:, :DEPTH * N_MOD * KD] = cols(ada_b)
    heads = [0, 2, 1, 3]
    w_in, vecs, ins = np.asarray(w_in), [], []
    for l in range(DEPTH):
        w = w_in[l]
        qkv_z, beta, a, rest = w[:, :1024], w[:, 1024:1032], w[:, 1032:1040], w[:, 1040:].copy()
        for at in (0, 512):
            q = rest[:, at:at + 256].reshape(-1, H, HD)[:, heads]
            rest[:, at:at + 256] = q.reshape(-1, 256)
        last = np.zeros((D_MODEL, P), w.dtype)
        last[:, BETA_ROW:BETA_ROW + 8] = beta
        last[:, G_ROW:G_ROW + 8] = a
        ins.append(tiles(np.concatenate([qkv_z, rest, last], 1), KD))
        v = np.zeros((P, NV), np.float32)
        for col, vec in ((V_PRE_MIX, norm_pre_mix), (V_POST_MIX, norm_post_mix), (V_PRE_FFN, norm_pre_ffn),
                         (V_POST_FFN, norm_post_ffn)):
            v[:, col:col + KD] = cols(vec[l])
        v[:, V_GCONV:V_GCONV + 18] = cols(gdn_conv_w[l])
        v[:, V_FCONV:V_FCONV + 6 * KF] = cols(ffn_conv_w[l])
        v[:, V_FBIAS:V_FBIAS + 2 * KF] = cols(ffn_conv_b[l])
        for col, vec in ((V_GNORM, gdn_norm), (V_QNORM, attn_q_norm), (V_KNORM, attn_k_norm), (V_HNORM, hgrn_norm)):
            v[:HD, col] = vec[l]
            v[HD:, col] = vec[l]
        v[G_ROW:G_ROW + 8, V_ALOG] = np.asarray(gdn_a_log[l]).reshape(-1)
        v[G_ROW:G_ROW + 8, V_DTB] = np.asarray(gdn_dt_bias[l]).reshape(-1)
        v[:, V_LB:V_LB + 8] = cols(hgrn_lb_raw)
        v[::HD, V_SINK:V_SINK + H] = np.asarray(swa_sink[l])[None, :]
        vecs.append(v)
    out["w_in"], out["vecs"] = np.stack(ins), np.stack(vecs, 1)
    out["w_out"] = np.stack([tiles(w, KD) for w in np.asarray(w_out)])
    out["w_up"] = np.stack([tiles(w, KD) for w in np.asarray(ffn_w_up)])
    out["w_down"] = np.asarray(ffn_w_down).reshape(DEPTH, KF, P, D_MODEL)
    out["consts"] = constants()
    return {n: np.ascontiguousarray(v) for n, v in out.items()}


def kernel(**inputs):
    import concourse.bacc as bacc
    from concourse.bass_utils import run_bass_kernel_spmd

    nc = bacc.Bacc("TRN2", target_bir_lowering=False, num_devices=1)
    arrays = {f"in_{n}_dram": v for n, v in layouts(**inputs).items()}
    aps = {n[3:-5]: nc.dram_tensor(n, v.shape, mybir.dt.from_np(v.dtype), kind="ExternalInput").ap()
           for n, v in arrays.items()}
    aps["out"] = nc.dram_tensor("out_0_dram", (P, KD, SEQ), F32, kind="ExternalOutput").ap()
    build(nc, aps)
    r = run_bass_kernel_spmd(nc, [arrays], core_ids=[0])
    got = r.results[0]["out_0_dram"]
    return got.transpose(1, 0, 2).reshape(D_MODEL, SEQ).T.reshape(1, SEQ, D_MODEL)
```
